# Optimizing a Trainium2 kernel written in Bass

```python
import jax, jax.numpy as jnp
from jax import lax
import numpy as np
import math
import jax
import jax.numpy as jnp

D_MODEL = 1024
BATCH = 1
SEQ = 256
DEPTH = 2

CHUNK = 64
N_MIXERS = 2
N_ATTN_LAYERS = (DEPTH + 1) // 2
N_REC_LAYERS = DEPTH // 2

N_HEADS = 16
HEAD_DIM = D_MODEL // N_HEADS
LEFT_CHUNKS = 8
BAND_CHUNKS = LEFT_CHUNKS + 1
BAND = BAND_CHUNKS * CHUNK
MAX_REL_DIST = 128
N_REL = 2 * MAX_REL_DIST + 1
NEG_INF = -1e30

D_RNN = D_MODEL
N_RG_BLOCKS = 8
RG_BLOCK = D_RNN // N_RG_BLOCKS
CONV_WIDTH = 4
RG_C = 8.0

D_FF = 4 * D_MODEL
RMS_EPS = 1e-6


def rmsnorm(x, g):
    xf = x.astype(jnp.float32)
    y = xf * lax.rsqrt(jnp.mean(xf * xf, axis=-1, keepdims=True) + RMS_EPS)
    return (y * g.astype(jnp.float32)).astype(x.dtype)

def chunked_band_attention(h, w_qkv, w_o, rel_table):
    B, S, _ = h.shape
    n_chunks = S // CHUNK
    qkv = jnp.einsum('bsd,de->bse', h, w_qkv).reshape(B, S, 3, N_HEADS, HEAD_DIM)
    q, k, v = qkv[:, :, 0], qkv[:, :, 1], qkv[:, :, 2]
    pad = LEFT_CHUNKS * CHUNK
    k_pad = jnp.pad(k, ((0, 0), (pad, 0), (0, 0), (0, 0)))
    v_pad = jnp.pad(v, ((0, 0), (pad, 0), (0, 0), (0, 0)))
    q_chunks = q.reshape(B, n_chunks, CHUNK, N_HEADS, HEAD_DIM).transpose(1, 0, 2, 3, 4)
    qi = jnp.arange(CHUNK)[:, None]
    kj = jnp.arange(BAND)[None, :]
    rel = qi + pad - kj
    idx = jnp.clip(rel, -MAX_REL_DIST, MAX_REL_DIST) + MAX_REL_DIST
    bias = rel_table[:, idx].astype(jnp.float32)
    scale = HEAD_DIM ** -0.5
    band_offsets = jnp.arange(BAND)

    def one_chunk(args):
        c, q_c = args
        start = c * CHUNK
        k_band = lax.dynamic_slice_in_dim(k_pad, start, BAND, axis=1)
        v_band = lax.dynamic_slice_in_dim(v_pad, start, BAND, axis=1)
        s = jnp.einsum('bqhd,bkhd->bhqk', q_c, k_band).astype(jnp.float32) * scale + bias
        key_pos = start - pad + band_offsets
        s = jnp.where(key_pos[None, None, None, :] >= 0, s, NEG_INF)
        p = jax.nn.softmax(s, axis=-1).astype(v_band.dtype)
        return jnp.einsum('bhqk,bkhd->bqhd', p, v_band)

    o = lax.map(one_chunk, (jnp.arange(n_chunks), q_chunks))
    o = o.transpose(1, 0, 2, 3, 4).reshape(B, S, D_MODEL)
    return jnp.einsum('bsd,de->bse', o, w_o)

def rglru_block(h, w_in, b_in, conv_w, conv_b, w_ga, b_ga, w_gx, b_gx, a_param, w_o, b_o):
    B, S, _ = h.shape
    u = jnp.einsum('bsd,de->bse', h, w_in) + b_in
    x_br = u[..., :D_RNN]
    y_br = jax.nn.gelu(u[..., D_RNN:], approximate=True)
    xp = jnp.pad(x_br, ((0, 0), (CONV_WIDTH - 1, 0), (0, 0)))
    xc = conv_b + xp[:, 0:S] * conv_w[0]
    for tap in range(1, CONV_WIDTH):
        xc = xc + xp[:, tap:tap + S] * conv_w[tap]
    xb = xc.reshape(B, S, N_RG_BLOCKS, RG_BLOCK)
    r = jax.nn.sigmoid(jnp.einsum('bsnc,nce->bsne', xb, w_ga) + b_ga).reshape(B, S, D_RNN)
    ig = jax.nn.sigmoid(jnp.einsum('bsnc,nce->bsne', xb, w_gx) + b_gx).reshape(B, S, D_RNN)
    log_a = -RG_C * r.astype(jnp.float32) * jax.nn.softplus(-a_param.astype(jnp.float32))
    a = jnp.exp(log_a)
    mult = jnp.sqrt(-jnp.expm1(2.0 * log_a))
    b_seq = mult * (ig * xc).astype(jnp.float32)

    def combine(left, right):
        a1, b1 = left
        a2, b2 = right
        return a1 * a2, a2 * b1 + b2

    _, hs = lax.associative_scan(combine, (a, b_seq), axis=1)
    out = hs.astype(h.dtype) * y_br
    return jnp.einsum('bse,ed->bsd', out, w_o) + b_o

def sq_relu_mlp(h, w1, w2):
    z = jax.nn.relu(jnp.einsum('bsd,df->bsf', h, w1))
    return jnp.einsum('bsf,fd->bsd', z * z, w2)

def first_inputs(seed: int = 0) -> dict:
    key = jax.random.key(seed)
    ks = jax.random.split(key, 20)
    nrm = lambda k, shape, s: jax.random.normal(k, shape, jnp.float32) * s
    x = jax.random.normal(ks[0], (BATCH, SEQ, D_MODEL), jnp.float32)
    norm_mix = 1.0 + nrm(ks[1], (DEPTH, D_MODEL), 0.05)
    norm_mlp = 1.0 + nrm(ks[2], (DEPTH, D_MODEL), 0.05)
    attn_w_qkv = nrm(ks[3], (N_ATTN_LAYERS, D_MODEL, 3 * D_MODEL), D_MODEL ** -0.5)
    attn_w_o = nrm(ks[4], (N_ATTN_LAYERS, D_MODEL, D_MODEL), D_MODEL ** -0.5)
    attn_rel_bias = nrm(ks[5], (N_ATTN_LAYERS, N_HEADS, N_REL), 0.2)
    rec_w_in = nrm(ks[6], (N_REC_LAYERS, D_MODEL, 2 * D_RNN), D_MODEL ** -0.5)
    rec_b_in = nrm(ks[7], (N_REC_LAYERS, 2 * D_RNN), 0.02)
    rec_conv_w = nrm(ks[8], (N_REC_LAYERS, CONV_WIDTH, D_RNN), CONV_WIDTH ** -0.5)
    rec_conv_b = nrm(ks[9], (N_REC_LAYERS, D_RNN), 0.02)
    rec_w_ga = nrm(ks[10], (N_REC_LAYERS, N_RG_BLOCKS, RG_BLOCK, RG_BLOCK), RG_BLOCK ** -0.5)
    rec_b_ga = nrm(ks[11], (N_REC_LAYERS, N_RG_BLOCKS, RG_BLOCK), 0.02)
    rec_w_gx = nrm(ks[12], (N_REC_LAYERS, N_RG_BLOCKS, RG_BLOCK, RG_BLOCK), RG_BLOCK ** -0.5)
    rec_b_gx = nrm(ks[13], (N_REC_LAYERS, N_RG_BLOCKS, RG_BLOCK), 0.02)
    a0 = jax.random.uniform(ks[14], (N_REC_LAYERS, D_RNN), jnp.float32, 0.81, 0.998)
    s0 = a0 ** (1.0 / RG_C)
    rec_a_param = jnp.log(s0) - jnp.log1p(-s0)
    rec_w_o = nrm(ks[15], (N_REC_LAYERS, D_RNN, D_MODEL), D_RNN ** -0.5)
    rec_b_o = nrm(ks[16], (N_REC_LAYERS, D_MODEL), 0.02)
    mlp_w1 = nrm(ks[17], (DEPTH, D_MODEL, D_FF), D_MODEL ** -0.5)
    mlp_w2 = nrm(ks[18], (DEPTH, D_FF, D_MODEL), D_FF ** -0.5)
    norm_final = 1.0 + nrm(ks[19], (D_MODEL,), 0.05)
    return {"x": x, "norm_mix": norm_mix, "norm_mlp": norm_mlp,
            "attn_w_qkv": attn_w_qkv, "attn_w_o": attn_w_o, "attn_rel_bias": attn_rel_bias,
            "rec_w_in": rec_w_in, "rec_b_in": rec_b_in, "rec_conv_w": rec_conv_w,
            "rec_conv_b": rec_conv_b, "rec_w_ga": rec_w_ga, "rec_b_ga": rec_b_ga,
            "rec_w_gx": rec_w_gx, "rec_b_gx": rec_b_gx, "rec_a_param": rec_a_param,
            "rec_w_o": rec_w_o, "rec_b_o": rec_b_o,
            "mlp_w1": mlp_w1, "mlp_w2": mlp_w2, "norm_final": norm_final}

def first_block(x, norm_mix, norm_mlp, attn_w_qkv, attn_w_o, attn_rel_bias,
              rec_w_in, rec_b_in, rec_conv_w, rec_conv_b, rec_w_ga, rec_b_ga,
              rec_w_gx, rec_b_gx, rec_a_param, rec_w_o, rec_b_o,
              mlp_w1, mlp_w2, norm_final):
    h = x
    for layer in range(DEPTH):
        hn = rmsnorm(h, norm_mix[layer])
        j = layer // N_MIXERS
        if layer % N_MIXERS == 0:
            mix = chunked_band_attention(hn, attn_w_qkv[j], attn_w_o[j], attn_rel_bias[j])
        else:
            mix = rglru_block(hn, rec_w_in[j], rec_b_in[j], rec_conv_w[j], rec_conv_b[j],
                              rec_w_ga[j], rec_b_ga[j], rec_w_gx[j], rec_b_gx[j],
                              rec_a_param[j], rec_w_o[j], rec_b_o[j])
        h = h + mix
        h = h + sq_relu_mlp(rmsnorm(h, norm_mlp[layer]), mlp_w1[layer], mlp_w2[layer])
    return rmsnorm(h, norm_final)


N_A = DEPTH // 2
N_B = DEPTH - N_A
PLE_DIM = 256
RWKV_HEAD = 64
RWKV_HEADS = D_MODEL // RWKV_HEAD
DECAY_LORA = 64
ICLR_LORA = 64
GN_EPS = 64e-5
DIFF_HEAD = 64
DIFF_HEADS = D_MODEL // (2 * DIFF_HEAD)
ROPE_DIMS = DIFF_HEAD // 4
ROPE_THETA = 500000.0
Q_BLOCK = 128
NORM_EPS = 1e-6
SUBLN_EPS = 1e-5


def rms_norm(x, g, eps=NORM_EPS):
    xf = x.astype(jnp.float32)
    y = xf * lax.rsqrt(jnp.mean(xf * xf, axis=-1, keepdims=True) + eps)
    return (y * g.astype(jnp.float32)).astype(x.dtype)

def rwkv7_time_mix(xn, mu, w_in, w0, w1, w2, a0, a1, a2, k_k, k_a, r_k, lnx_g, lnx_b, w_out):
    B, S, D = xn.shape
    H, N = RWKV_HEADS, RWKV_HEAD
    f32 = jnp.float32
    x_prev = jnp.pad(xn, ((0, 0), (1, 0), (0, 0)))[:, :-1]
    xmix = xn[None] + (x_prev - xn)[None] * mu[:, None, None, :]
    rkvg = jnp.einsum('cbsd,cde->cbse', xmix[:4], w_in)
    r, k, v, g = rkvg[0], rkvg[1], rkvg[2], rkvg[3]
    xw, xa = xmix[4], xmix[5]
    w_pre = (w0 + jnp.tanh(xw @ w1) @ w2).astype(f32)
    decay = jnp.exp(-jnp.exp(-jax.nn.softplus(-w_pre) - 0.5))
    a = jax.nn.sigmoid((a0 + (xa @ a1) @ a2).astype(f32))
    heads = lambda t: t.astype(f32).reshape(B, S, H, N)
    r, k, v, decay, a = heads(r), heads(k), heads(v), heads(decay), heads(a)
    kk = k * k_k.astype(f32).reshape(H, N)
    kk = kk / jnp.maximum(jnp.linalg.norm(kk, axis=-1, keepdims=True), 1e-12)
    k = k * (1.0 + (a - 1.0) * k_a.astype(f32).reshape(H, N))

    def step(state, inp):
        r_t, w_t, k_t, v_t, kk_t, a_t = inp
        s_kk = jnp.einsum('bhij,bhj->bhi', state, kk_t)
        state = (state * w_t[:, :, None, :]
                 - s_kk[..., None] * (kk_t * a_t)[:, :, None, :]
                 + v_t[..., None] * k_t[:, :, None, :])
        return state, jnp.einsum('bhij,bhj->bhi', state, r_t)

    seq_first = lambda t: jnp.swapaxes(t, 0, 1)
    state0 = jnp.zeros((B, H, N, N), f32)
    _, y = lax.scan(step, state0, (seq_first(r), seq_first(decay), seq_first(k),
                                   seq_first(v), seq_first(kk), seq_first(a)))
    y = jnp.swapaxes(y, 0, 1)
    mean = jnp.mean(y, axis=-1, keepdims=True)
    var = jnp.mean(jnp.square(y - mean), axis=-1, keepdims=True)
    y = ((y - mean) * lax.rsqrt(var + GN_EPS) * lnx_g.astype(f32).reshape(H, N)
         + lnx_b.astype(f32).reshape(H, N))
    y = y + jnp.sum(r * k * r_k.astype(f32), axis=-1, keepdims=True) * v
    y = y.reshape(B, S, D).astype(xn.dtype) * jax.nn.silu(g)
    return y @ w_out

def rope_tables(S):
    inv = ROPE_THETA ** (-jnp.arange(0, ROPE_DIMS, 2, dtype=jnp.float32) / ROPE_DIMS)
    ang = jnp.arange(S, dtype=jnp.float32)[:, None] * inv[None, :]
    return jnp.cos(ang), jnp.sin(ang)

def partial_rope(x, cos, sin):
    half = ROPE_DIMS // 2
    c = cos[None, :, None, None, :].astype(x.dtype)
    s = sin[None, :, None, None, :].astype(x.dtype)
    x1, x2 = x[..., :half], x[..., half:ROPE_DIMS]
    return jnp.concatenate([x1 * c - x2 * s, x2 * c + x1 * s, x[..., ROPE_DIMS:]], axis=-1)

def shared_kv(h, kv_norm, kv_w, cos, sin):
    B, S, D = h.shape
    kv = rms_norm(h, kv_norm) @ kv_w
    k = partial_rope(kv[..., :D].reshape(B, S, DIFF_HEADS, 2, DIFF_HEAD), cos, sin)
    v = kv[..., D:].reshape(B, S, DIFF_HEADS, 2 * DIFF_HEAD)
    return k.transpose(0, 2, 3, 1, 4), v.transpose(0, 2, 1, 3)

def diff_attention_mix(xn, k_sh, v_sh, w_in, lam_qk, subln_g, w_out, lam_init, cos, sin):
    B, S, D = xn.shape
    H, Dh = DIFF_HEADS, DIFF_HEAD
    f32 = jnp.float32
    proj = xn @ w_in
    q = partial_rope(proj[..., :D].reshape(B, S, H, 2, Dh), cos, sin) * (Dh ** -0.5)
    gate = proj[..., D:]
    lq = lam_qk.astype(f32)
    lam = jnp.exp(jnp.sum(lq[0] * lq[1])) - jnp.exp(jnp.sum(lq[2] * lq[3])) + lam_init
    nblk = S // Q_BLOCK
    qb = q.reshape(B, nblk, Q_BLOCK, H, 2, Dh).transpose(1, 0, 3, 4, 2, 5)
    kf = k_sh.astype(f32)
    vf = v_sh.astype(f32)
    k_pos = jnp.arange(S)

    def block(args):
        q_blk, blk = args
        s = jnp.einsum('bhcqd,bhckd->bhcqk', q_blk.astype(f32), kf)
        q_pos = blk * Q_BLOCK + jnp.arange(Q_BLOCK)
        s = jnp.where(k_pos[None, :] <= q_pos[:, None], s, -1e30)
        prob = jax.nn.softmax(s, axis=-1)
        attn = prob[:, :, 0] - lam * prob[:, :, 1]
        return jnp.einsum('bhqk,bhkv->bhqv', attn, vf)

    o = lax.map(block, (qb, jnp.arange(nblk)))
    o = o.transpose(1, 0, 3, 2, 4).reshape(B, S, H, 2 * Dh)
    o = rms_norm(o, subln_g, SUBLN_EPS) * (1.0 - lam_init)
    o = o.reshape(B, S, D).astype(xn.dtype) * jax.nn.silu(gate)
    return o @ w_out

def second_inputs(seed: int = 0) -> dict:
    key = jax.random.key(seed)
    ks = iter(jax.random.split(key, 32))
    D, f32 = D_MODEL, jnp.float32
    nrm = lambda shape, scale: jax.random.normal(next(ks), shape, f32) * scale
    gain = lambda shape: 1.0 + nrm(shape, 0.02)
    return {
        'x': nrm((BATCH, SEQ, D), 1.0),
        'p': nrm((DEPTH, BATCH, SEQ, PLE_DIM), 1.0),
        'norm_pre': gain((DEPTH, D)),
        'norm_post': gain((DEPTH, D)),
        'a_mu': jax.random.uniform(next(ks), (N_A, 6, D), f32),
        'a_w_in': nrm((N_A, 4, D, D), D ** -0.5),
        'a_w0': jax.random.uniform(next(ks), (N_A, D), f32, -6.0, 1.0),
        'a_w1': nrm((N_A, D, DECAY_LORA), D ** -0.5),
        'a_w2': nrm((N_A, DECAY_LORA, D), 0.1),
        'a_a0': nrm((N_A, D), 0.5),
        'a_a1': nrm((N_A, D, ICLR_LORA), D ** -0.5),
        'a_a2': nrm((N_A, ICLR_LORA, D), 0.5 * ICLR_LORA ** -0.5),
        'a_k_k': 1.0 + nrm((N_A, D), 0.1),
        'a_k_a': 1.0 + nrm((N_A, D), 0.1),
        'a_r_k': nrm((N_A, RWKV_HEADS, RWKV_HEAD), 0.1),
        'a_lnx_g': gain((N_A, D)),
        'a_lnx_b': nrm((N_A, D), 0.02),
        'a_w_out': nrm((N_A, D, D), D ** -0.5),
        'kv_norm': gain((D,)),
        'kv_w': nrm((D, 2 * D), D ** -0.5),
        'b_w_in': nrm((N_B, D, 2 * D), D ** -0.5),
        'b_lambda': nrm((N_B, 4, DIFF_HEAD), 0.1),
        'b_subln': gain((N_B, 2 * DIFF_HEAD)),
        'b_w_out': nrm((N_B, D, D), D ** -0.5),
        'ple_w': nrm((DEPTH, PLE_DIM, D), PLE_DIM ** -0.5),
        'ple_gate': nrm((DEPTH, D, D), D ** -0.5),
        'ple_norm': gain((DEPTH, D)),
    }

def second_block(x, p, norm_pre, norm_post, a_mu, a_w_in, a_w0, a_w1, a_w2, a_a0, a_a1, a_a2,
              a_k_k, a_k_a, a_r_k, a_lnx_g, a_lnx_b, a_w_out, kv_norm, kv_w, b_w_in, b_lambda,
              b_subln, b_w_out, ple_w, ple_gate, ple_norm):
    S = x.shape[1]
    cos, sin = rope_tables(S)
    h = x
    k_sh = None
    v_sh = None
    for i in range(DEPTH):
        xn = rms_norm(h, norm_pre[i])
        if i < N_A:
            y = rwkv7_time_mix(xn, a_mu[i], a_w_in[i], a_w0[i], a_w1[i], a_w2[i], a_a0[i],
                               a_a1[i], a_a2[i], a_k_k[i], a_k_a[i], a_r_k[i], a_lnx_g[i],
                               a_lnx_b[i], a_w_out[i])
        else:
            if i == N_A:
                k_sh, v_sh = shared_kv(h, kv_norm, kv_w, cos, sin)
            j = i - N_A
            lam_init = 0.8 - 0.6 * math.exp(-0.3 * i)
            y = diff_attention_mix(xn, k_sh, v_sh, b_w_in[j], b_lambda[j], b_subln[j],
                                   b_w_out[j], lam_init, cos, sin)
        h = h + rms_norm(y, norm_post[i])
        e = p[i] @ ple_w[i]
        g = jax.nn.sigmoid(h @ ple_gate[i])
        h = h + rms_norm(g * e, ple_norm[i])
    return h


def setup_inputs(seed=0):
    out = dict(first_inputs(seed))
    for name, value in second_inputs(seed + 1).items():
        if name != "x":
            out[name + "_2"] = value
    return out


def reference(
    x, norm_mix, norm_mlp, attn_w_qkv, attn_w_o, attn_rel_bias, rec_w_in, rec_b_in, rec_conv_w,
    rec_conv_b, rec_w_ga, rec_b_ga, rec_w_gx, rec_b_gx, rec_a_param, rec_w_o, rec_b_o, mlp_w1,
    mlp_w2, norm_final, p_2, norm_pre_2, norm_post_2, a_mu_2, a_w_in_2, a_w0_2, a_w1_2, a_w2_2,
    a_a0_2, a_a1_2, a_a2_2, a_k_k_2, a_k_a_2, a_r_k_2, a_lnx_g_2, a_lnx_b_2, a_w_out_2,
    kv_norm_2, kv_w_2, b_w_in_2, b_lambda_2, b_subln_2, b_w_out_2, ple_w_2, ple_gate_2,
    ple_norm_2,
):
    x = first_block(
        x, norm_mix, norm_mlp, attn_w_qkv, attn_w_o, attn_rel_bias, rec_w_in, rec_b_in,
        rec_conv_w, rec_conv_b, rec_w_ga, rec_b_ga, rec_w_gx, rec_b_gx, rec_a_param, rec_w_o,
        rec_b_o, mlp_w1, mlp_w2, norm_final,
    )
    return second_block(
        x, p_2, norm_pre_2, norm_post_2, a_mu_2, a_w_in_2, a_w0_2, a_w1_2, a_w2_2, a_a0_2,
        a_a1_2, a_a2_2, a_k_k_2, a_k_a_2, a_r_k_2, a_lnx_g_2, a_lnx_b_2, a_w_out_2, kv_norm_2,
        kv_w_2, b_w_in_2, b_lambda_2, b_subln_2, b_w_out_2, ple_w_2, ple_gate_2, ple_norm_2,
    )


_drawn_inputs = setup_inputs


def setup_inputs(seed=0):
    import zlib

    import numpy as np

    out = dict(_drawn_inputs(seed))
    spreads = {}
    factors = {'rec_b_ga': 8.0,
     'rec_b_gx': 8.0,
     'norm_post_2': 3.445,
     'a_lnx_g_2': 4.387,
     'a_lnx_b_2': 3.594,
     'kv_norm_2': 4.99,
     'b_subln_2': 6.981,
     'ple_norm_2': 3.707}
    for name, (base, spread) in spreads.items():
        noise = np.random.default_rng([zlib.crc32(name.encode()), seed]).standard_normal(out[name].shape)
        drawn = base * np.exp(spread * noise) if base else spread * noise
        out[name] = jnp.asarray(drawn.astype(out[name].dtype))
    for name, factor in factors.items():
        out[name] = (out[name] * factor).astype(out[name].dtype)
    return out
```

```python
from contextlib import ExitStack

import numpy as np

import concourse.bass as bass
from concourse import mybir

ALU = mybir.AluOpType
ACT = mybir.ActivationFunctionType
F32 = mybir.dt.float32
AX = mybir.AxisListType

P = 128
SEQ, D, DFF = 256, 1024, 4096
NT, KT = SEQ // P, D // P
HALF = 512
HEADS, HD = 16, 64
EPS = 1e-6
RING = 2

W_QKV, W_O, W_MLP0, W_IN, W_GATES, W_RO, W_MLP1 = 0, 6, 8, 24, 28, 29, 31
W_RKVG, W_OUT_A, W_PLE0, W_KV, W_QG, W_OUT_B, W_PLE1, W_TILES = 47, 55, 57, 60, 64, 68, 70, 73

COLS = ["norm_mix0", "norm_mix1", "norm_mlp0", "norm_mlp1", "b_in_x", "b_in_y", "conv_w0", "conv_w1", "conv_w2",
        "conv_w3", "conv_b", "b_ga", "b_gx", "a_param", "norm_pre0", "norm_pre1", "kv_norm",
        "mu0", "mu1", "mu2", "mu3", "mu4", "mu5"]
ROWS = ["b_o", "norm_final", "w0", "a0", "k_k", "k_a", "r_k", "lnx_g", "lnx_b", "norm_post0", "ple_norm0",
        "subln", "norm_post1", "ple_norm1"]
CONSTS = {}
_at = 0
for _name, _n in (("ident", 128), ("tri_incl", 128), ("mask_x", 512), ("mask_a", 384), ("causal", 384),
                  ("cos", 16), ("sin", 16), ("eye2", 64), ("last", 2)):
    CONSTS[_name] = (_at, _n)
    _at += _n
N_CONSTS = _at


def shape_constants():
    i = np.arange(P)
    c = np.zeros((P, N_CONSTS), np.float32)

    def put(name, value):
        a, n = CONSTS[name]
        c[:, a:a + n] = np.asarray(value, np.float32).reshape(P, n)

    r, s = i[:, None], i[None, :]
    same = lambda n: (r // n) == (s // n)
    put("ident", r == s)
    put("tri_incl", (r <= s) & same(64))
    put("mask_x", np.stack([-1.0 * ((r < s) & same(16)), 1.0 * ((r <= s) & same(64)),
                            1.0 * ((r < s) & same(64)), 1.0 * ((r <= s) & same(64))], 1))
    put("mask_a", np.stack([-1.0 * ((s < r) & same(16)), 1.0 * ((s < r) & same(32) & ~same(16)),
                            1.0 * ((s < r) & same(64) & ~same(32))], 1))
    k = np.arange(SEQ)[None, :]
    put("causal", np.concatenate([np.where(k <= P + r, 0, -1e30), np.where(s <= r, 0, -1e30)], 1))
    inv = np.float32(500000.0) ** (-np.arange(0, 16, 2, dtype=np.float32) / np.float32(16))
    ang = (np.arange(SEQ, dtype=np.float32)[:, None] * inv.astype(np.float32)[None, :]).astype(np.float32)
    tok = ang.reshape(NT, P, 8).transpose(1, 0, 2)
    put("cos", np.cos(tok.astype(np.float64)))
    put("sin", np.sin(tok.astype(np.float64)))
    put("eye2", (i[:, None] % 64) == np.arange(64)[None, :])
    put("last", np.stack([i == 63, i == 127], 1))
    return c


def build(nc, x, w, cols, rows, consts, relt, lora1, lora2, pT, lam, out):
    with ExitStack() as ctx:
        def sb(name, shape):
            return ctx.enter_context(nc.sbuf_tensor(name, shape, F32))

        def sem(name):
            return ctx.enter_context(nc.semaphore(name))

        ring = sb("ring", [P, RING, 4096])
        h = sb("h", [P, NT, D])
        ARENA = 32800
        arena = sb("arena", [P, ARENA])
        col = sb("col", [P, len(COLS), KT])
        row = sb("row", [P, 5, D])
        con = sb("con", [P, N_CONSTS])
        small = sb("small", [P, 1024])
        psum = ctx.enter_context(nc.psum_tensor("psum", [P, 8, HALF], F32))

        def C(name):
            a, n = CONSTS[name]
            return con[:, a:a + n]

        ident = C("ident")

        def c8(name):
            return col[:, COLS.index(name), :]

        def view(off, *dims):
            n = int(np.prod(dims))
            assert off + n <= ARENA, (off, dims)
            v = arena[:, off:off + n]
            if len(dims) == 1:
                return v
            names = "abcd"[:len(dims)]
            return v.rearrange("p (" + " ".join(names) + ") -> p " + " ".join(names),
                               **{k: d for k, d in zip(names[1:], dims[1:])})

        def wt(n, *dims):
            v = ring[:, n % RING, :]
            names = "abcd"[:len(dims)]
            return v.rearrange("p (" + " ".join(names) + ") -> p " + " ".join(names),
                               **{k: d for k, d in zip(names[1:], dims[1:])})

        small_at = [0]

        def little(n):
            small_at[0] += n
            assert small_at[0] <= 1024
            return small[:, small_at[0] - n:small_at[0]]

        S = 2048
        tile_landed = [sem(f"tile_landed{i}") for i in range(RING)]
        tile_used = sem("tile_used")
        x_landed, spread_stored = sem("x_landed"), sem("spread_stored")
        spread = nc.dram_tensor("bias_spread", (P, HEADS * 384), F32, kind="Internal").ap()
        par_landed = sem("par_landed")
        row_landed = [sem(f"row_landed{i}") for i in range(5)]
        act_step, dve_step, pool_step = sem("act_step"), sem("dve_step"), sem("pool_step")
        stat_sum, stat_var, stat_root, rstd_ready = sem("stat_sum"), sem("stat_var"), sem("stat_root"), sem("rstd_ready")
        h_ready = sem("h_ready")
        tp_filled = sem("tp_filled")
        tp_act, tp_dve = sem("tp_act"), sem("tp_dve")
        out_stored = sem("out_stored")

        N_STATS = 12
        ss, var, root, rstd = little(2 * N_STATS), little(2 * N_STATS), little(2 * N_STATS), little(2 * N_STATS)

        (T_H0, T_Q, T_K, T_O, T_H1, T_N2, T_H3, T_N5, T_KAP, T_RH, T_BET, T_KH, T_YA, T_H6, T_H7, T_KB, T_QB, T_OB,
         T_H8) = range(19)

        def pe_transposes(pe, inst, src, n=4):
            for b in range(n):
                g = sum(T_COUNT[:inst]) + b
                if g >= 2:
                    pe.wait_ge(tp_act if g % 2 == 0 else tp_dve, g // 2)
                for j in range(2):
                    for t in range(NT):
                        ins = nc.tensor.transpose(psum[:, 6 + g % 2, (2 * j + t) * P:(2 * j + t + 1) * P],
                                                  src[:, t, (2 * b + j) * P:(2 * b + j + 1) * P], ident)
                ins.then_inc(tp_filled, 1)

        T_COUNT = [4] * 40

        def evacuate(eng, inst, b, dst, gain=None, gain2=None, dst2=None):
            g = sum(T_COUNT[:inst]) + b
            eng.wait_ge(tp_filled, g + 1)
            bank = psum[:, 6 + g % 2, :].rearrange("p (j t) -> p j t", j=2)
            on_act = g % 2 == 0
            assert on_act == (eng is engines["act"])
            ins = None
            pairs = [(dst, gain)] + ([(dst2, gain2)] if dst2 is not None else [])
            for d, gn in pairs:
                if gn is None:
                    dd = d[:, 2 * b:2 * b + 2, :]
                    ins = nc.scalar.copy(dd, bank) if on_act else nc.vector.tensor_copy(dd, bank)
                else:
                    for j in range(2):
                        k = 2 * b + j
                        if on_act:
                            ins = nc.scalar.activation(d[:, k, :], bank[:, j, :], ACT.Copy, scale=gn[:, k:k + 1])
                        else:
                            ins = nc.vector.tensor_scalar(d[:, k, :], bank[:, j, :], gn[:, k:k + 1], None, ALU.mult)
            ins.then_inc(tp_act if on_act else tp_dve, 1)

        def evacuated(eng, inst, n=None):
            g = sum(T_COUNT[:inst]) + (T_COUNT[inst] if n is None else n)
            eng.wait_ge(tp_act, (g + 1) // 2)
            eng.wait_ge(tp_dve, g // 2)

        engines = {}

        qkv_act, qkv_dve = sem("qkv_act"), sem("qkv_dve")
        sc_done, sc_read, mx_ready, exp_done, pt_filled, pt_copied, pv_done, o_ready = (
            sem(n) for n in ("sc_done", "sc_read", "mx_ready", "exp_done", "pt_filled", "pt_copied", "pv_done", "o_ready"))
        bias_ready = sem("bias_ready")
        z_filled, z_relu, zz_ready, mlp_done = sem("z_filled"), sem("z_relu"), sem("zz_ready"), sem("mlp_done")
        mask_set = sem("mask_set")

        in_filled, x_read, y_read, xc_ready, gates_filled, gates_read = (
            sem(n) for n in ("in_filled", "x_read", "y_read", "xc_ready", "gates_filled", "gates_read"))
        xn_ready, pad_zero, decay_ready, decay_part, m2_ready, m_ready, g_ready = (
            sem(n) for n in ("xn_ready", "pad_zero", "decay_ready", "decay_part", "m2_ready", "m_ready", "g_ready"))
        lor_landed, lam_landed = sem("lor_landed"), sem("lam_landed")
        mix_ready, lora_filled, lora_out, lora2_filled, lora2_read, sig_ready, cum_filled, cum_prev, decays, last_filled, last_read = (
            sem(n) for n in ("mix_ready", "lora_filled", "lora_out", "lora2_filled", "lora2_read", "sig_ready",
                             "cum_filled", "cum_prev", "decays", "last_filled", "last_read"))
        proj_act, proj_dve, kk_raw, kk_sq, kk_var, kk_root, kk_unit, k_ready, beta_kap, khat, bonus = (
            sem(n) for n in ("proj_act", "proj_dve", "kk_raw", "kk_sq", "kk_var", "kk_root", "kk_unit", "k_ready",
                             "beta_kap", "khat", "bonus"))
        core_filled, core_dve, core_act, core_pool = ([sem(f"{n}{b}") for b in range(2)] for n in
                                                      ("core_filled", "core_dve", "core_act", "core_pool"))
        state_filled, state_ready, ys_filled, y_sq, y_var, y_root, y_ready, bv_ready, y_cent = (
            sem(n) for n in ("state_filled", "state_ready", "ys_filled", "y_sq", "y_var", "y_root", "y_ready",
                             "bv_ready", "y_cent"))
        yo_act, e_act, gate_act, ge_ready = sem("yo_act"), sem("e_act"), sem("gate_act"), sem("ge_ready")
        kv_act, kv_dve, roped, lam_sum, lam_exp, comb_ready, o_act, o_sq, o_var, o_root, od_ready = (
            sem(n) for n in ("kv_act", "kv_dve", "roped", "lam_sum", "lam_exp", "comb_ready", "o_act", "o_sq", "o_var",
                             "o_root", "od_ready"))
        row_ready = row_landed

        qn, kn, vn = (view(i * S, NT, D) for i in (0, 1, 2))
        qT, kT = view(3 * S, KT, SEQ), view(4 * S, KT, SEQ)
        on = view(5 * S, NT, D)
        bias = view(6 * S, HEADS, 384)
        sbuf_s = view(9 * S, 3, 384)
        sbuf_pt = view(9 * S + 1152, 2, 384)
        XT = 30720
        xT = view(XT, KT, SEQ)
        junk = view(14 * S, NT, D)
        def junk_at(i):
            return view((14 if i < 6 else 8) * S, NT, D)
        nmx = little(2 * 2 * HEADS).rearrange("p (h t) -> p h t", t=2)
        sums = little(2 * 2 * HEADS).rearrange("p (h t) -> p h t", t=2)
        rsum = little(2 * 2 * HEADS).rearrange("p (h t) -> p h t", t=2)
        QKV = [(qn, 0), (kn, 0), (vn, 0), (qn, 1), (kn, 1), (vn, 1)]
        zz = view(0, 2, 4, SEQ)
        zr = view(S, 2, 4, SEQ)

        def tile_ready(eng, n):
            eng.wait_ge(tile_landed[n % RING], 16 * (n // RING + 1))

        def used(eng, n):
            for m, first in enumerate((W_MLP0, W_MLP1)):
                if first <= n < first + 16:
                    kind, c = list(mlp_order())[n - first]
                    if kind == 1:
                        eng.wait_ge(z_filled, 16 * m + 2 * c + 2)
                    else:
                        eng.wait_ge(mlp_done, 8 * m + c + 1)
                    return
            if W_IN <= n < W_GATES:
                eng.wait_ge(in_filled, 2 * (n - W_IN) + 2)
            elif n == W_GATES:
                eng.wait_ge(gates_filled, 4)
            else:
                eng.wait_ge(tile_used, n + 1 - sum(k for first, k in ((W_MLP0, 16), (W_IN, 5), (W_MLP1, 16)) if first < n))

        def pe_chunk(pe, n, c, lhs, banks_free):
            tile_ready(pe, n)
            if banks_free is not None:
                banks_free(pe, c)
            for t in range(NT):
                for k in range(KT):
                    ins = nc.tensor.matmul(psum[:, 2 * (c % 2) + t, :], lhs[:, k, t * P:(t + 1) * P],
                                           wt(n, KT, HALF)[:, k, :], start=(k == 0), stop=(k == KT - 1))
            ins.then_inc(tile_used, 1)

        def pe_linear(pe, first, chunks, lhs, banks_free=None):
            for c in range(chunks):
                pe_chunk(pe, first + c, c, lhs, banks_free)

        xn = view(S, NT, D)
        xb = view(2 * S, KT, SEQ + 3)
        yg, xc, rg, ig, aa, th, bb_, hs, og = (view(i * S, KT, SEQ) for i in (4, 5, 6, 7, 8, 9, 10, 11, 12))
        sp8, nsp8 = little(KT), little(KT)
        spt = [little(KT) for _ in range(5)]

        vN, kap, bet, kN = (view(i * S, NT, D) for i in (0, 1, 2, 3))
        Pd, Pi, Pp, aN, rN = (view(i * S, NT, D) for i in (4, 5, 6, 7, 8))
        gN, tmp1, tmp2, sg = view(9 * S, NT, D), view(9 * S, NT, D), view(10 * S, NT, D), view(11 * S, NT, D)
        yN = rN
        KR = view(4 * S, KT, 2, SEQ)
        bT, khT = view(6 * S, KT, SEQ), view(7 * S, KT, SEQ)
        xTs = view(XT, KT, SEQ + 1)
        dT = view(14 * S, KT, SEQ)
        xm = [view(13 * S, KT, SEQ), view(12 * S, KT, SEQ)]
        xn5 = view(13 * S, NT, D)
        lora2_sb = view(8 * S, 2, D)
        lora1_sb = view(9 * S, 2, KT, 64)
        lt = view(10 * S, 2, SEQ)
        WORK = 23040
        MN = view(10 * S, KT, 5, 64)
        M_OF, N_OF = {1: 3, 2: 0}, {0: 1, 1: 4, 2: 2}
        U = [view(WORK + 4864 * b, 4, 5, P) for b in range(2)]
        OFF = [view(WORK + 4864 * b + 2560, 2, 4, P) for b in range(2)]
        XX = [view(WORK + 4864 * b + 3584, 4, P) for b in range(2)]
        BV = [view(WORK + 4864 * b + 4096, 4, 64) for b in range(2)]
        WU = [view(WORK + 4864 * b + 4352, 4, P) for b in range(2)]
        Sg = [None] + [view(WORK + 512 * g, KT, 64) for g in range(3)]
        stmp = view(WORK + 2048, KT, 64)
        bon = little(32).rearrange("p (t h) -> p t h", t=NT)
        pc = little(32).rearrange("p (f g) -> p f g", f=KT)
        nrm = [[little(16).rearrange("p (t h) -> p t h", t=NT) for _ in range(2)] for _ in range(2)]
        mu_y, vr_y, rt_y, rs_y = (little(32).rearrange("p (t h) -> p t h", t=NT) for _ in range(4))
        yo, eN, ge = view(3 * S, NT, D), view(4 * S, NT, D), view(5 * S, NT, D)
        posted = view(6 * S, NT, D)
        pT_sb = view(7 * S, 2, SEQ)
        MIX = [4, 5, 1, 0, 2, 3]

        DVE_AT = {s_: i for i, s_ in enumerate(["x0", "x1", "x2", "x3", 1, 2, 3, 4, 5, 6, 7, 8, 9, 11])}
        ACT_AT = {s_: i for i, s_ in enumerate([2, 3, 4, 6, 8, 10, 11])}
        PE_AT = {s_: i for i, s_ in enumerate(["x0", "x1", "x2", "x3"] + list(range(1, 12)))}

        def core_wait(eng, sems, table, pp, b, step):
            eng.wait_ge(sems[b], pp * len(table) + table[step] + 1)

        kD, vD, qD, gD = (view(i * S, NT, D) for i in (0, 1, 2, 3))
        kDT, qDT, oD, oD2 = view(4 * S, KT, SEQ), view(5 * S, KT, SEQ), view(6 * S, NT, D), view(7 * S, NT, D)
        xTb = view(13 * S, KT, SEQ)
        rt = [view(8 * S + 256 * i, NT, 16, 8) for i in range(4)]
        sd = view(9 * S, 4, 384)
        pt2 = view(10 * S, 2, 384)
        lamb = view(11 * S, 4, 64)
        lamp = view(11 * S + 256, 2, 64)
        lams, lame, nlam = little(2), little(2), little(1)
        LAM0 = 0.8 - 0.6 * float(np.exp(-0.3))
        rd = [little(4).rearrange("p (c t) -> p c t", c=2) for _ in range(2)]
        eye_b = C("eye2")

        def mlp_order():
            yield 1, 0
            for c in range(1, 8):
                yield 1, c
                yield 2, c - 1
            yield 2, 7

        def attention_act(act):
            for hh in range(HEADS + 1):
                if hh < HEADS:
                    act.wait_ge(mx_ready, hh + 1)
                    buf = sbuf_s[:, hh % 3, :]
                    nc.scalar.activation(buf[:, 0:256], buf[:, 0:256], ACT.Exp, bias=nmx[:, hh, 1:2],
                                         accum_out=sums[:, hh, 1:2])
                    nc.scalar.activation(buf[:, 256:384], buf[:, 256:384], ACT.Exp, bias=nmx[:, hh, 0:1],
                                         accum_out=sums[:, hh, 0:1]).then_inc(exp_done, 1)
                if hh >= 1:
                    g = hh - 1
                    act.wait_ge(pt_filled, g + 1)
                    if g >= 2:
                        act.wait_ge(pv_done, g - 1)
                    nc.scalar.copy(sbuf_pt[:, g % 2, :], psum[:, 6 + g % 2, 0:384]).then_inc(pt_copied, 1)

        def mlp_act(act, m):
            for c in range(8):
                for b in range(2):
                    act.wait_ge(z_filled, 16 * m + 2 * c + b + 1)
                    if c >= 2:
                        act.wait_ge(zz_ready, 16 * m + 2 * (c - 2) + b + 1)
                    nc.scalar.activation(zr[:, c % 2, 2 * b:2 * b + 2, :], psum[:, 4 + b, :], ACT.Relu).then_inc(z_relu, 1)

        def head_outputs(dve, settle, g):
            dve.wait_ge(exp_done, 4 * g + 4)
            settle(nc.vector.reciprocal(rsum[:, 4 * g:4 * g + 4, :], sums[:, 4 * g:4 * g + 4, :]))
            dve.wait_ge(pv_done, 4 * g + 4)
            dst = on[:, :, 4 * g * HD:(4 * g + 4) * HD].rearrange("p t (h d) -> p h t d", d=HD)
            src = psum[:, g, :].rearrange("p (h t d) -> p h t d", t=NT, d=HD)
            nc.vector.tensor_tensor(dst, src, rsum[:, 4 * g:4 * g + 4, :].unsqueeze(3).broadcast_to([P, 4, NT, HD]),
                                    ALU.mult).then_inc(o_ready, 1)

        def mlp_dve(dve, settle, m, i):
            for c in range(8):
                for b in range(2):
                    dve.wait_ge(z_relu, 16 * m + 2 * c + b + 1)
                    if c >= 2:
                        dve.wait_ge(mlp_done, 8 * m + c - 1)
                    r = zr[:, c % 2, 2 * b:2 * b + 2, :]
                    nc.vector.tensor_tensor(zz[:, c % 2, 2 * b:2 * b + 2, :], r, r, ALU.mult).then_inc(zz_ready, 1)
            r2 = rstd[:, 2 * i:2 * i + 2]
            settle(nc.vector.tensor_tensor(root[:, 2 * i:2 * i + 2], r2, r2, ALU.mult))
            dve.wait_ge(mlp_done, 8 * m + 8)
            for t in range(NT):
                for c in range(2):
                    part = h[:, t, c * HALF:(c + 1) * HALF]
                    ins = nc.vector.scalar_tensor_tensor(out=part, in0=psum[:, 2 * t + c, :],
                                                         scalar=root[:, 2 * i + t:2 * i + t + 1], in1=part,
                                                         op0=ALU.mult, op1=ALU.add)
            ins.then_inc(h_ready, 1)

        def mlp_pe(pe, m, first):
            for i, (kind, c) in enumerate(mlp_order()):
                n = first + i
                tile_ready(pe, n)
                if kind == 1:
                    for b in range(2):
                        if c >= 1:
                            pe.wait_ge(z_relu, 16 * m + 2 * (c - 1) + b + 1)
                        for j in range(2):
                            f = 2 * b + j
                            for k in range(KT):
                                ins = nc.tensor.matmul(psum[:, 4 + b, j * SEQ:(j + 1) * SEQ],
                                                       wt(n, KT, HALF)[:, k, f * P:(f + 1) * P], xT[:, k, :],
                                                       start=(k == 0), stop=(k == KT - 1))
                        ins.then_inc(z_filled, 1)
                else:
                    for f in range(4):
                        pe.wait_ge(zz_ready, 16 * m + 2 * c + f // 2 + 1)
                        for t in range(NT):
                            for half in range(2):
                                ins = nc.tensor.matmul(psum[:, 2 * t + half, :], zz[:, c % 2, f, t * P:(t + 1) * P],
                                                       wt(n, 4, D)[:, f, half * HALF:(half + 1) * HALF],
                                                       start=(c == 0 and f == 0), stop=(c == 7 and f == 3))
                    ins.then_inc(mlp_done, 1)

        def ODD_EVEN(inst):
            g = sum(T_COUNT[:inst])
            own = [b for b in range(T_COUNT[inst]) if (g + b) % 2 == 0]
            return own, [b for b in range(T_COUNT[inst]) if b not in own]

        TF = [(T_KAP, KR[:, :, 0, :]), (T_RH, KR[:, :, 1, :]), (T_BET, bT), (T_KH, khT)]

        block = ctx.enter_context(nc.Block())

        @block.sync
        def _(sp):
            sp.dma_start(h[:, :, :], x.rearrange("(t p) d -> p t d", p=P)).then_inc(x_landed, 16)
            sp.dma_start(con[:, :], consts).then_inc(par_landed, 16)
            sp.dma_start(col[:, :, :], cols).then_inc(par_landed, 16)
            for n in range(W_TILES):
                if n >= RING:
                    used(sp, n - RING)
                sp.dma_start(ring[:, n % RING, :], w[n]).then_inc(tile_landed[n % RING], 16)
                if n == 1:
                    sp.dma_start(spread, bass.AP(relt.tensor, 0, [[0, P], [1, HEADS * 384]])).then_inc(spread_stored, 16)
                if n == 3:
                    sp.wait_ge(spread_stored, 16)
                    sp.dma_start(bias[:, :, 0:256], bass.AP(spread.tensor, 127, [[HEADS * 384 - 1, P], [384, HEADS], [1, 256]])).then_inc(bias_ready, 16)
            sp.wait_ge(h_ready, 9)
            sp.dma_start(out.rearrange("(t p) d -> p t d", p=P), h[:, :, :]).then_inc(out_stored, 16)
            sp.wait_ge(out_stored, 16)

        @block.gpsimd
        def _(pool):
            pool.wait_ge(bias_ready, 16)
            nc.gpsimd.memset(bias[0:64, :, 192:256], -1e30).then_inc(pool_step, 1)
            pool.wait_ge(pool_step, 1)
            nc.gpsimd.tensor_copy(bias[:, :, 256:384], bias[:, :, 128:256]).then_inc(mask_set, 1)

            def load_row(r):
                pool.dma_start(row[:, r % 5, :], bass.AP(rows.tensor, r * D, [[0, P], [1, D]])).then_inc(row_landed[r % 5], 16)

            for r in range(5):
                load_row(r)
            pool.wait_ge(h_ready, 5)
            load_row(5)
            load_row(6)
            pool.dma_start(lora1_sb, lora1).then_inc(lor_landed, 16)
            pool.dma_start(lora2_sb[0:64], lora2).then_inc(lor_landed, 16)
            pool.wait_ge(lora2_read, 2)
            load_row(7)
            load_row(8)
            pool.wait_ge(decays, 3)
            for j in range(2):
                hl = slice(j * HALF, (j + 1) * HALF)
                pool.wait_ge(kk_unit, j + 1)
                nc.gpsimd.tensor_tensor(bet[:, :, hl], kap[:, :, hl], aN[:, :, hl], ALU.mult).then_inc(pool_step, 1)
                pool.wait_ge(pool_step, 2 + 2 * j)
                nc.gpsimd.tensor_tensor(bet[:, :, hl], bet[:, :, hl], Pi[:, :, hl], ALU.mult).then_inc(pool_step, 1)
                pool.wait_ge(pool_step, 3 + 2 * j)
                nc.gpsimd.tensor_tensor(kap[:, :, hl], kap[:, :, hl], Pp[:, :, hl], ALU.mult).then_inc(beta_kap, 1)
                pool.wait_ge(proj_dve, j + 1)
                nc.gpsimd.tensor_tensor(kN[:, :, hl], kN[:, :, hl], Pi[:, :, hl], ALU.mult).then_inc(khat, 1)
            pool.wait_ge(kk_unit, 2)
            load_row(9)
            for pp in range(4):
                for b in range(2):
                    core_wait(pool, core_dve, DVE_AT, pp, b, "x3")
                    nc.gpsimd.tensor_tensor(U[b][:, :, 0, :], U[b][:, :, 1, :], ident.unsqueeze(1).broadcast_to([P, 4, P]),
                                            ALU.add).then_inc(core_pool[b], 1)
            core_wait(pool, core_filled, PE_AT, 3, 1, 11)
            pool.wait_ge(bonus, 2)
            nc.gpsimd.tensor_tensor(kap.rearrange("p t (h d) -> p t h d", d=HD), vN.rearrange("p t (h d) -> p t h d", d=HD),
                                    bon.unsqueeze(3).broadcast_to([P, NT, HEADS, HD]), ALU.mult).then_inc(bv_ready, 1)
            pool.wait_ge(core_filled[0], 4 * len(PE_AT))
            load_row(10)
            pool.wait_ge(y_ready, 1)
            pool.dma_start(pT_sb, pT[:, 0]).then_inc(lor_landed, 16)
            load_row(11)
            pool.wait_ge(h_ready, 6)
            load_row(12)
            load_row(13)
            pool.wait_ge(h_ready, 7)
            pool.dma_start(lamb, bass.AP(lam.tensor, 0, [[0, P], [64, 4], [1, 64]])).then_inc(lam_landed, 16)
            cosb = C("cos").rearrange("p (t f) -> p t f", t=NT).unsqueeze(2).broadcast_to([P, NT, 16, 8])
            sinb = C("sin").rearrange("p (t f) -> p t f", t=NT).unsqueeze(2).broadcast_to([P, NT, 16, 8])
            n = 5
            for i, (a, count) in enumerate(((kD, 2), (qD, 6))):
                pool.wait_ge(kv_act, count)
                pool.wait_ge(kv_dve, count)
                v = a.rearrange("p t (s d) -> p t s d", d=64)
                x1, x2 = v[:, :, :, 0:8], v[:, :, :, 8:16]
                for d, s0, s1 in ((0, x1, cosb), (1, x2, sinb), (2, x2, cosb), (3, x1, sinb)):
                    ins = nc.gpsimd.tensor_tensor(rt[d], s0, s1, ALU.mult)
                ins.then_inc(pool_step, 1)
                n += 1
                pool.wait_ge(pool_step, n)
                nc.gpsimd.tensor_tensor(x1, rt[0], rt[1], ALU.subtract)
                nc.gpsimd.tensor_tensor(x2, rt[2], rt[3], ALU.add).then_inc(roped, 1)
                pool.wait_ge(roped, i + 1)
            pool.wait_ge(od_ready, 1)
            pool.dma_start(pT_sb, pT[:, 1]).then_inc(lor_landed, 16)

        @block.scalar
        def _(act):
            engines["act"] = act
            steps = [0]

            def settle(ins):
                steps[0] += 1
                ins.then_inc(act_step, 1)
                act.wait_ge(act_step, steps[0])

            def moments(i, src=h):
                for t in range(NT):
                    ins = nc.scalar.activation(junk_at(i)[:, t, :], src[:, t, :], ACT.Square, accum_out=ss[:, 2 * i + t:2 * i + t + 1])
                ins.then_inc(stat_sum, 1)
                act.wait_ge(stat_var, i + 1)
                nc.scalar.activation(root[:, 2 * i:2 * i + 2], var[:, 2 * i:2 * i + 2], ACT.Sqrt).then_inc(stat_root, 1)

            act.wait_ge(x_landed, 16)
            act.wait_ge(par_landed, 32)
            for b in (0, 2):
                evacuate(act, T_H0, b, xT, c8("norm_mix0"))
            moments(0)
            for c, (dst, half) in enumerate(QKV):
                used(act, W_QKV + c)
                act.wait_ge(rstd_ready, 1)
                nc.scalar.activation(dst[:, 0, half * HALF:(half + 1) * HALF], psum[:, 2 * (c % 2), :], ACT.Copy,
                                     scale=rstd[:, 0:1]).then_inc(qkv_act, 1)
            for inst, dst in ((T_Q, qT), (T_K, kT)):
                for b in (0, 2):
                    evacuate(act, inst, b, dst)
            attention_act(act)
            for b in (0, 2):
                evacuate(act, T_O, b, xT)
            act.wait_ge(h_ready, 1)
            for b in (0, 2):
                evacuate(act, T_H1, b, xT, c8("norm_mlp0"))
            moments(1)
            act.wait_ge(decay_part, 1)
            nc.scalar.activation(spt[1], spt[0], ACT.Exp, scale=-1.0).then_inc(decay_part, 1)
            act.wait_ge(decay_part, 3)
            nc.scalar.activation(spt[3], spt[2], ACT.Ln).then_inc(decay_part, 1)
            mlp_act(act, 0)

            act.wait_ge(h_ready, 2)
            moments(2)
            for b in ODD_EVEN(T_N2)[0]:
                evacuate(act, T_N2, b, xT, c8("norm_mix1"))
            for i in range(4):
                act.wait_ge(in_filled, 4 + i + 1)
                for j in range(2):
                    f = 2 * i + j
                    ins = nc.scalar.activation(yg[:, f, :], psum[:, i, j * SEQ:(j + 1) * SEQ], ACT.Gelu_apprx_tanh,
                                               bias=c8("b_in_y")[:, f:f + 1])
                ins.then_inc(y_read, 1)
            for i in range(4):
                act.wait_ge(gates_filled, i + 1)
                for j in range(2):
                    f = 2 * i + j
                    nc.scalar.activation(rg[:, f, :], psum[:, 4 + i % 2, j * SEQ:(j + 1) * SEQ], ACT.Sigmoid,
                                         bias=c8("b_ga")[:, f:f + 1])
                    ins = nc.scalar.activation(ig[:, f, :], psum[:, 6 + i % 2, j * SEQ:(j + 1) * SEQ], ACT.Sigmoid,
                                               bias=c8("b_gx")[:, f:f + 1])
                ins.then_inc(gates_read, 1)
            act.wait_ge(gates_read, 4)
            act.wait_ge(decay_ready, 1)
            for f in range(KT):
                nc.scalar.activation(aa[:, f, :], rg[:, f, :], ACT.Exp, scale=nsp8[:, f:f + 1])
                settle(nc.scalar.activation(th[:, f, :], rg[:, f, :], ACT.Tanh, scale=sp8[:, f:f + 1]))
                ins = nc.scalar.activation(bb_[:, f, :], aa[:, f, :], ACT.Square)
                if f % 4 == 3:
                    ins.then_inc(g_ready, 1)
            for q in range(2):
                act.wait_ge(m2_ready, q + 1)
                nc.scalar.activation(th[:, 4 * q:4 * q + 4, :], th[:, 4 * q:4 * q + 4, :], ACT.Sqrt).then_inc(m_ready, 1)
            act.wait_ge(h_ready, 3)
            for b in ODD_EVEN(T_H3)[0]:
                evacuate(act, T_H3, b, xT, c8("norm_mlp1"))
            moments(3)
            mlp_act(act, 1)
            act.wait_ge(h_ready, 4)
            moments(4)

            act.wait_ge(h_ready, 5)
            moments(5)
            for b in ODD_EVEN(T_N5)[0]:
                evacuate(act, T_N5, b, xTs[:, :, 1:SEQ + 1], c8("norm_pre0"))
            act.wait_ge(lora_filled, 1)
            nc.scalar.activation(lt[0:64, 0, :], psum[0:64, 4, 0:SEQ], ACT.Tanh).then_inc(lora_out, 1)
            act.wait_ge(lora_filled, 2)
            nc.scalar.copy(lt[0:64, 1, :], psum[0:64, 5, 0:SEQ]).then_inc(lora_out, 1)
            act.wait_ge(lora2_read, 1)
            nc.scalar.activation(sg, sg, ACT.Sigmoid).then_inc(sig_ready, 1)
            act.wait_ge(lora2_read, 2)
            nc.scalar.activation(aN, aN, ACT.Sigmoid).then_inc(sig_ready, 1)
            act.wait_ge(cum_prev, 1)
            cum = psum[:, 0:4, :].rearrange("p (t q) n -> p t (q n)", t=NT)
            CD = float(np.exp(-0.5))
            nc.scalar.activation(Pd, cum, ACT.Exp, scale=-CD).then_inc(decays, 1)
            nc.scalar.activation(Pi, cum, ACT.Exp, scale=CD).then_inc(decays, 1)
            nc.scalar.activation(Pp, Pp, ACT.Exp, scale=-CD).then_inc(decays, 1)

            def pair_out(c):
                return psum[:, 2 * (c % 2):2 * (c % 2) + 2, :]

            for j in range(2):
                used(act, W_RKVG + j)
                nc.scalar.copy(kN[:, :, j * HALF:(j + 1) * HALF], pair_out(j)).then_inc(proj_act, 1)
            act.wait_ge(last_filled, 1)
            nc.scalar.copy(pc.rearrange("p f g -> p (f g)"), psum[:, 4, 0:32]).then_inc(last_read, 1)
            for j in range(2):
                hl = slice(j * HALF, (j + 1) * HALF)
                act.wait_ge(kk_raw, j + 1)
                nc.scalar.activation(tmp1[:, :, hl], kap[:, :, hl], ACT.Square).then_inc(kk_sq, 1)
                act.wait_ge(kk_var, j + 1)
                nc.scalar.activation(nrm[j][1], nrm[j][0], ACT.Sqrt).then_inc(kk_root, 1)
            for j in range(2):
                used(act, W_RKVG + 4 + j)
                nc.scalar.copy(vN[:, :, j * HALF:(j + 1) * HALF], pair_out(j)).then_inc(proj_act, 1)
            for inst, dst in TF:
                for b in ODD_EVEN(inst)[0]:
                    evacuate(act, inst, b, dst)
            act.wait_ge(bonus, 2)
            for j in range(2):
                used(act, W_RKVG + 6 + j)
                nc.scalar.activation(gN[:, :, j * HALF:(j + 1) * HALF], pair_out(j), ACT.Silu).then_inc(proj_act, 1)
            for pp in range(4):
                for s_ in (2, 3, 4, 6, 8, 10, 11):
                    for b in range(2):
                        f, B = 2 * pp + b, 4 * b
                        core_wait(act, core_filled, PE_AT, pp, b, s_)
                        four = lambda k: psum[:, B + k, :].rearrange("p (q n) -> p q n", q=4)
                        if s_ == 2:
                            act.wait_ge(core_pool[b], pp + 1)
                            nc.scalar.copy(U[b][:, :, 1, :], four(1))
                            ins = nc.scalar.copy(BV[b], psum[:, B + 3, 0:256].rearrange("p (q n) -> p q n", q=4))
                        elif s_ == 3:
                            nc.scalar.copy(U[b][:, :, 1, :], four(1))
                            ins = nc.scalar.copy(XX[b], four(2))
                        elif s_ == 4:
                            ins = nc.scalar.copy(XX[b], four(2))
                        elif s_ in (6, 8):
                            ins = nc.scalar.copy(XX[b], four(1))
                        elif s_ == 10:
                            ins = nc.scalar.activation(WU[b], four(1), ACT.Copy, scale=-1.0)
                        else:
                            nc.scalar.copy(MN[:, f, 0:3, :].rearrange("p g i -> p (g i)"), psum[:, B + 2, 0:192])
                            nc.scalar.copy(MN[:, f, 3:5, :].rearrange("p g i -> p (g i)"), psum[:, B + 3, 0:128])
                            dst = yN[:, :, 2 * f * HD:(2 * f + 2) * HD].rearrange("p t (h d) -> p h t d", d=HD)
                            ins = nc.scalar.copy(dst, psum[:, B, 0:256].rearrange("p (h t d) -> p h t d", h=2, t=NT))
                        ins.then_inc(core_act[b], 1)
            act.wait_ge(y_cent, 1)
            nc.scalar.activation(bet, yN, ACT.Square).then_inc(y_sq, 1)
            act.wait_ge(y_var, 1)
            nc.scalar.activation(rt_y, vr_y, ACT.Sqrt).then_inc(y_root, 1)

            def out_norm(i, first, e_n, T, ready):
                for c in range(2):
                    used(act, first + c)
                    nc.scalar.copy(yo[:, :, c * HALF:(c + 1) * HALF], pair_out(c)).then_inc(yo_act, 1)
                act.wait_ge(yo_act, 2 * e_n + 2)
                moments(i, yo)

            def embed(i, tile, e_n, T):
                used(act, tile)
                for c in range(2):
                    ins = nc.scalar.copy(eN[:, :, c * HALF:(c + 1) * HALF], pair_out(c))
                ins.then_inc(e_act, 1)
                for b in ODD_EVEN(T)[0]:
                    evacuate(act, T, b, xT)
                for c in range(2):
                    used(act, tile + 1 + c)
                    nc.scalar.activation(ge[:, :, c * HALF:(c + 1) * HALF], pair_out(c), ACT.Sigmoid).then_inc(gate_act, 1)
                act.wait_ge(ge_ready, 2 * e_n + 2)
                moments(i, ge)

            for b in ODD_EVEN(T_YA)[0]:
                evacuate(act, T_YA, b, xT)
            out_norm(6, W_OUT_A, 0, None, None)
            embed(7, W_PLE0, 0, T_H6)

            act.wait_ge(h_ready, 7)
            for b in ODD_EVEN(T_H7)[0]:
                evacuate(act, T_H7, b, xT, c8("norm_pre1"), c8("kv_norm"), xTb)
            moments(8)
            act.wait_ge(lam_sum, 1)
            nc.scalar.activation(lame, lams, ACT.Exp).then_inc(lam_exp, 1)
            act.wait_ge(rstd_ready, 9)
            for c, dst in enumerate((kD, vD, qD, gD)):
                for j in range(2):
                    used(act, W_KV + 2 * c + j)
                    hl = slice(j * HALF, (j + 1) * HALF)
                    if c < 3:
                        ins = nc.scalar.activation(dst[:, 0, hl], pair_out(j)[:, 0], ACT.Copy, scale=rstd[:, 16:17])
                    else:
                        for t in range(NT):
                            ins = nc.scalar.activation(dst[:, t, hl], pair_out(j)[:, t], ACT.Silu,
                                                       scale=rstd[:, 16 + t:17 + t])
                    ins.then_inc(kv_act, 1)
            for inst, dst in ((T_KB, kDT), (T_QB, qDT)):
                for b in ODD_EVEN(inst)[0]:
                    evacuate(act, inst, b, dst)
            for hh in range(HEADS + 2):
                if hh < HEADS:
                    act.wait_ge(mx_ready, HEADS + hh + 1)
                    buf = sd[:, hh % 4, :]
                    nc.scalar.activation(buf[:, 0:256], buf[:, 0:256], ACT.Exp, bias=nmx[:, hh, 1:2],
                                         accum_out=sums[:, hh, 1:2])
                    nc.scalar.activation(buf[:, 256:384], buf[:, 256:384], ACT.Exp, bias=nmx[:, hh, 0:1],
                                         accum_out=sums[:, hh, 0:1]).then_inc(exp_done, 1)
                if hh >= 3 and hh % 2 == 1:
                    g = (hh - 3) // 2
                    act.wait_ge(pt_filled, HEADS + g + 1)
                    if g >= 2:
                        act.wait_ge(pv_done, HEADS + g - 1)
                    nc.scalar.copy(pt2[:, g % 2, :], psum[:, 6 + g % 2, 0:384]).then_inc(pt_copied, 1)
            for g in range(2):
                act.wait_ge(pv_done, HEADS + 4 * g + 4)
                dst = oD[:, :, g * HALF:(g + 1) * HALF].rearrange("p t (h d) -> p h t d", d=P)
                src = psum[:, 2 * g:2 * g + 2, :].rearrange("p b (h t d) -> p (b h) t d", h=2, t=NT)
                ins = nc.scalar.copy(dst, src)
            settle(ins)
            nc.scalar.activation(oD2, oD, ACT.Square).then_inc(o_sq, 1)
            act.wait_ge(o_var, 1)
            nc.scalar.activation(rt_y[:, :, 0:8], vr_y[:, :, 0:8], ACT.Sqrt).then_inc(o_root, 1)
            for b in ODD_EVEN(T_OB)[0]:
                evacuate(act, T_OB, b, xT)
            out_norm(9, W_OUT_B, 1, None, None)
            embed(10, W_PLE1, 1, T_H8)

        @block.vector
        def _(dve):
            engines["dve"] = dve
            steps = [0]

            def settle(ins):
                steps[0] += 1
                ins.then_inc(dve_step, 1)
                dve.wait_ge(dve_step, steps[0])

            def rms(i, n=D, eps=EPS):
                dve.wait_ge(stat_sum, i + 1)
                nc.vector.tensor_scalar(var[:, 2 * i:2 * i + 2], ss[:, 2 * i:2 * i + 2], 1.0 / n, eps, ALU.mult,
                                        ALU.add).then_inc(stat_var, 1)
                dve.wait_ge(stat_root, i + 1)
                nc.vector.reciprocal(rstd[:, 2 * i:2 * i + 2], root[:, 2 * i:2 * i + 2]).then_inc(rstd_ready, 1)
                dve.wait_ge(rstd_ready, i + 1)

            def residual(first, chunks=2):
                for c in range(chunks):
                    used(dve, first + c)
                    for t in range(NT):
                        part = h[:, t, c * HALF:(c + 1) * HALF]
                        ins = nc.vector.tensor_tensor(part, psum[:, 2 * (c % 2) + t, :], part, ALU.add)
                ins.then_inc(h_ready, 1)

            dve.wait_ge(par_landed, 32)
            for b in (1, 3):
                evacuate(dve, T_H0, b, xT, c8("norm_mix0"))
            rms(0)
            for c, (dst, half) in enumerate(QKV):
                used(dve, W_QKV + c)
                nc.vector.tensor_scalar(dst[:, 1, half * HALF:(half + 1) * HALF], psum[:, 2 * (c % 2) + 1, :],
                                        rstd[:, 1:2], None, ALU.mult).then_inc(qkv_dve, 1)
            for inst, dst in ((T_Q, qT), (T_K, kT)):
                for b in (1, 3):
                    evacuate(dve, inst, b, dst)
            dve.wait_ge(mask_set, 1)
            for hh in range(HEADS + 1):
                if hh < HEADS:
                    dve.wait_ge(sc_done, hh + 1)
                    if hh >= 3:
                        dve.wait_ge(pt_filled, hh - 2)
                    buf = sbuf_s[:, hh % 3, :]
                    nc.vector.scalar_tensor_tensor(out=buf, in0=psum[:, 4 + hh % 2, 0:384], scalar=HD ** -0.5,
                                                   in1=bias[:, hh, :], op0=ALU.mult, op1=ALU.add).then_inc(sc_read, 1)
                    dve.wait_ge(sc_read, hh + 1)
                    nc.vector.tensor_reduce(nmx[:, hh, 1:2], buf[:, 0:256], AX.X, ALU.max, negate=True)
                    nc.vector.tensor_reduce(nmx[:, hh, 0:1], buf[:, 256:384], AX.X, ALU.max, negate=True).then_inc(mx_ready, 1)
                if hh >= 4 and hh % 4 == 0:
                    head_outputs(dve, settle, hh // 4 - 1)
            for b in (1, 3):
                evacuate(dve, T_O, b, xT)
            residual(W_O)
            for b in (1, 3):
                evacuate(dve, T_H1, b, xT, c8("norm_mlp0"))
            rms(1)
            p_ = c8("a_param")
            settle(nc.vector.tensor_scalar(spt[1], p_, -1.0, None, ALU.mult))
            nc.vector.tensor_tensor(spt[0], p_, spt[1], ALU.max).then_inc(decay_part, 1)
            dve.wait_ge(decay_part, 2)
            nc.vector.tensor_scalar(spt[2], spt[1], 1.0, None, ALU.add).then_inc(decay_part, 1)
            dve.wait_ge(decay_part, 4)
            settle(nc.vector.tensor_scalar(spt[2], spt[2], -1.0, None, ALU.add))
            settle(nc.vector.tensor_scalar(spt[4], spt[2], 0.0, None, ALU.is_equal))
            settle(nc.vector.tensor_tensor(spt[2], spt[2], spt[4], ALU.add))
            settle(nc.vector.reciprocal(spt[2], spt[2]))
            settle(nc.vector.tensor_tensor(spt[3], spt[3], spt[2], ALU.mult))
            settle(nc.vector.tensor_tensor(spt[3], spt[3], spt[4], ALU.add))
            settle(nc.vector.tensor_tensor(spt[3], spt[3], spt[1], ALU.mult))
            settle(nc.vector.tensor_scalar(spt[4], p_, -1.0, 0.0, ALU.mult, ALU.max))
            settle(nc.vector.tensor_tensor(spt[3], spt[3], spt[4], ALU.add))
            nc.vector.tensor_scalar(sp8, spt[3], 8.0, None, ALU.mult)
            nc.vector.tensor_scalar(nsp8, spt[3], -8.0, None, ALU.mult).then_inc(decay_ready, 1)
            mlp_dve(dve, settle, 0, 1)

            def normed(dst, i):
                for t in range(NT):
                    ins = nc.vector.tensor_scalar(dst[:, t, :], h[:, t, :], rstd[:, 2 * i + t:2 * i + t + 1], None, ALU.mult)
                ins.then_inc(xn_ready, 1)

            def row_of(name):
                r = ROWS.index(name)
                dve.wait_ge(row_landed[r % 5], 16 * (r // 5 + 1))
                return row[:, r % 5, :]

            rms(2)
            normed(xn, 2)
            nc.vector.memset(xb[:, :, 0:3], 0.0).then_inc(pad_zero, 1)
            bo = row_of("b_o")
            dve.wait_ge(xn_ready, 1)
            for t in range(NT):
                settle(nc.vector.tensor_tensor(h[:, t, :], h[:, t, :], bo, ALU.add))
            for b in ODD_EVEN(T_N2)[1]:
                evacuate(dve, T_N2, b, xT, c8("norm_mix1"))
            dve.wait_ge(pad_zero, 1)
            for i in range(4):
                dve.wait_ge(in_filled, i + 1)
                for j in range(2):
                    f = 2 * i + j
                    ins = nc.vector.tensor_scalar(xb[:, f, 3:], psum[:, i, j * SEQ:(j + 1) * SEQ],
                                                  c8("b_in_x")[:, f:f + 1], None, ALU.add)
                ins.then_inc(x_read, 1)
                dve.wait_ge(x_read, i + 1)
                for tap in range(4):
                    wc = c8(f"conv_w{tap}")
                    for j in range(2):
                        f = 2 * i + j
                        src, o = xb[:, f, tap:tap + SEQ], xc[:, f, :]
                        if tap == 0:
                            ins = nc.vector.tensor_scalar(o, src, wc[:, f:f + 1], c8("conv_b")[:, f:f + 1], ALU.mult, ALU.add)
                        else:
                            ins = nc.vector.scalar_tensor_tensor(out=o, in0=src, scalar=wc[:, f:f + 1], in1=o,
                                                                 op0=ALU.mult, op1=ALU.add)
                    if tap < 3:
                        settle(ins)
                ins.then_inc(xc_ready, 1)
            dve.wait_ge(xc_ready, 4)
            dve.wait_ge(gates_read, 4)
            for q in range(2):
                u = slice(4 * q, 4 * q + 4)
                nc.vector.tensor_tensor(ig[:, u, :], ig[:, u, :], xc[:, u, :], ALU.mult)
                dve.wait_ge(g_ready, q + 1)
                nc.vector.scalar_tensor_tensor(out=th[:, u, :], in0=bb_[:, u, :], scalar=1.0, in1=th[:, u, :],
                                               op0=ALU.add, op1=ALU.mult).then_inc(m2_ready, 1)
            for q in range(2):
                u = slice(4 * q, 4 * q + 4)
                dve.wait_ge(m_ready, q + 1)
                settle(nc.vector.tensor_tensor(bb_[:, u, :], th[:, u, :], ig[:, u, :], ALU.mult))
                for f in range(4 * q, 4 * q + 4):
                    ins = nc.vector.tensor_tensor_scan(hs[:, f, :], aa[:, f, :], bb_[:, f, :], 0.0, ALU.mult, ALU.add)
                settle(ins)
                dve.wait_ge(y_read, 4)
                nc.vector.tensor_tensor(og[:, u, :], hs[:, u, :], yg[:, u, :], ALU.mult).then_inc(o_ready, 1)
            residual(W_RO)
            for b in ODD_EVEN(T_H3)[1]:
                evacuate(dve, T_H3, b, xT, c8("norm_mlp1"))
            rms(3)
            mlp_dve(dve, settle, 1, 3)
            rms(4)
            nf = row_of("norm_final")
            for t in range(NT):
                ins = nc.vector.scalar_tensor_tensor(out=h[:, t, :], in0=h[:, t, :], scalar=rstd[:, 8 + t:9 + t], in1=nf,
                                                     op0=ALU.mult, op1=ALU.mult)
            ins.then_inc(h_ready, 1)
            dve.wait_ge(h_ready, 5)

            rms(5)
            normed(xn5, 5)
            nc.vector.memset(xTs[:, :, 0:1], 0.0)
            for b in ODD_EVEN(T_N5)[1]:
                evacuate(dve, T_N5, b, xTs[:, :, 1:SEQ + 1], c8("norm_pre0"))
            evacuated(dve, T_N5)
            settle(nc.vector.tensor_tensor(dT, xTs[:, :, 0:SEQ], xTs[:, :, 1:SEQ + 1], ALU.subtract))

            def mix(i):
                if i in (2, 3):
                    dve.wait_ge(lora_filled, i - 1)
                if i >= 4:
                    used(dve, W_RKVG + 2 * (i - 4) + 1)
                for k in range(KT):
                    ins = nc.vector.scalar_tensor_tensor(out=xm[i % 2][:, k, :], in0=dT[:, k, :],
                                                         scalar=c8(f"mu{MIX[i]}")[:, k:k + 1],
                                                         in1=xTs[:, k, 1:SEQ + 1], op0=ALU.mult, op1=ALU.add)
                ins.then_inc(mix_ready, 1)

            mix(0)
            mix(1)
            four_banks = psum[:, 0:4, :].rearrange("p (t q) n -> p t (q n)", t=NT)
            for i, (dst, name) in enumerate(((sg, "w0"), (aN, "a0"))):
                r_ = row_of(name)
                dve.wait_ge(lora2_filled, i + 1)
                nc.vector.tensor_tensor(dst, four_banks, r_.unsqueeze(1).broadcast_to([P, NT, D]), ALU.add).then_inc(lora2_read, 1)
                mix(2 + i)
            dve.wait_ge(cum_filled, 1)
            nc.vector.tensor_tensor(Pp, four_banks, sg, ALU.subtract).then_inc(cum_prev, 1)
            for j in range(2):
                hl = slice(j * HALF, (j + 1) * HALF)
                over = lambda r_: r_[:, hl].unsqueeze(1).broadcast_to([P, NT, HALF])
                heads = lambda a: a[:, :, hl].rearrange("p t (h d) -> p t h d", d=HD)
                per_head = lambda a: a.unsqueeze(3).broadcast_to([P, NT, 8, HD])
                dve.wait_ge(proj_act, j + 1)
                nc.vector.tensor_tensor(kap[:, :, hl], kN[:, :, hl], over(row_of("k_k")), ALU.mult).then_inc(kk_raw, 1)
                dve.wait_ge(sig_ready, 2)
                for t in range(NT):
                    ins = nc.vector.scalar_tensor_tensor(out=tmp2[:, t, hl], in0=aN[:, t, hl], scalar=1.0,
                                                         in1=row_of("k_a")[:, hl], op0=ALU.subtract, op1=ALU.mult)
                settle(ins)
                nc.vector.scalar_tensor_tensor(out=kN[:, :, hl], in0=tmp2[:, :, hl], scalar=1.0, in1=kN[:, :, hl],
                                               op0=ALU.add, op1=ALU.mult).then_inc(k_ready, 1)
                dve.wait_ge(kk_sq, j + 1)
                settle(nc.vector.tensor_reduce(nrm[j][0], heads(tmp1), AX.X, ALU.add))
                nc.vector.tensor_scalar(nrm[j][0], nrm[j][0], 1e-24, None, ALU.max).then_inc(kk_var, 1)
                dve.wait_ge(kk_root, j + 1)
                settle(nc.vector.reciprocal(nrm[j][1], nrm[j][1]))
                dve.wait_ge(kk_raw, j + 1)
                nc.vector.tensor_tensor(heads(kap), heads(kap), per_head(nrm[j][1]), ALU.mult).then_inc(kk_unit, 1)
                if j == 0:
                    mix(4)
            for j in range(2):
                hl = slice(j * HALF, (j + 1) * HALF)
                heads = lambda a: a[:, :, hl].rearrange("p t (h d) -> p t h d", d=HD)
                used(dve, W_RKVG + 2 + j)
                pr = psum[:, 2 * j:2 * j + 2, :]
                dve.wait_ge(decays, 3)
                dve.wait_ge(k_ready, j + 1)
                nc.vector.tensor_tensor(rN[:, :, hl], pr, Pd[:, :, hl], ALU.mult)
                nc.vector.tensor_tensor(tmp1[:, :, hl], pr, kN[:, :, hl], ALU.mult).then_inc(proj_dve, 1)
                dve.wait_ge(proj_dve, j + 1)
                settle(nc.vector.tensor_tensor(tmp1[:, :, hl], tmp1[:, :, hl],
                                               row_of("r_k")[:, hl].unsqueeze(1).broadcast_to([P, NT, HALF]), ALU.mult))
                nc.vector.tensor_reduce(bon[:, :, 8 * j:8 * j + 8], heads(tmp1), AX.X, ALU.add).then_inc(bonus, 1)
            mix(5)
            for inst, dst in TF:
                for b in ODD_EVEN(inst)[1]:
                    evacuate(dve, inst, b, dst)

            for pp in range(4):
                for s_ in ("x0", "x1", "x2", "x3", 1, 2, 3, 4, 5, 6, 7, 8, 9, 11):
                    for b in range(2):
                        f, B = 2 * pp + b, 4 * b
                        core_wait(dve, core_filled, PE_AT, pp, b, s_)
                        four = lambda k: psum[:, B + k, :].rearrange("p (q n) -> p q n", q=4)
                        Z = U[b][:, :, 0, :]
                        if isinstance(s_, str):
                            q = int(s_[1])
                            ins = nc.vector.tensor_tensor(U[b][:, q, 1:5, :].rearrange("p a n -> p (a n)"), psum[:, B + q, :],
                                                          C("mask_x"), ALU.mult)
                        elif s_ == 1:
                            src = psum[:, B:B + 2, 0:256].rearrange("p h (t n) -> p h t n", t=2)
                            for m, dst in enumerate((XX[b], OFF[b][:, 0], OFF[b][:, 1])):
                                mk = C("mask_a")[:, m * P:(m + 1) * P].unsqueeze(1).unsqueeze(1).broadcast_to([P, 2, 2, P])
                                ins = nc.vector.tensor_tensor(dst.rearrange("p (h t) n -> p h t n", h=2), src, mk, ALU.mult)
                        elif s_ == 2:
                            ins = nc.vector.tensor_copy(XX[b], four(2))
                        elif s_ == 3:
                            dve.wait_ge(core_pool[b], pp + 1)
                            ins = nc.vector.tensor_tensor(Z, four(0), Z, ALU.add)
                        elif s_ == 4:
                            ins = nc.vector.tensor_tensor(Z, four(3), Z, ALU.add)
                        elif s_ == 5:
                            ins = nc.vector.tensor_tensor(Z, four(0), Z, ALU.add)
                        elif s_ in (6, 8):
                            ins = nc.vector.tensor_copy(U[b][:, :, 1, :], four(2))
                        elif s_ in (7, 9):
                            ins = nc.vector.tensor_tensor(Z, Z, four(0), ALU.subtract)
                        else:
                            ins = nc.vector.tensor_tensor(KR[:, f, 1, :], psum[:, B + 1, 0:256], KR[:, f, 1, :], ALU.add)
                        ins.then_inc(core_dve[b], 1)
            for b in range(2):
                core_wait(dve, core_act, ACT_AT, 3, b, 11)
                core_wait(dve, core_dve, DVE_AT, 3, b, 11)
            dve.wait_ge(last_read, 1)
            pcg = lambda g: pc[:, :, g:g + 1].broadcast_to([P, KT, 64])
            nc.vector.tensor_tensor(Sg[1], MN[:, :, N_OF[0], :], pcg(0), ALU.mult).then_inc(state_ready, 1)
            for g in (1, 2):
                dve.wait_ge(state_filled, g)
                for p0 in (0, HD):
                    hp = slice(p0, p0 + HD)
                    src = psum[hp, 2 * (g - 1) + p0 // HD, :].rearrange("p (f n) -> p f n", f=KT)
                    ins = nc.vector.tensor_tensor(stmp[hp], src, MN[hp, :, N_OF[g], :], ALU.add)
                settle(ins)
                nc.vector.tensor_tensor(Sg[g + 1], stmp, pcg(g), ALU.mult).then_inc(state_ready, 1)
            dve.wait_ge(ys_filled, 1)
            for par in range(2):
                for t, r_ in ((0, slice(64, P)), (1, slice(0, P))):
                    part = yN[r_, t, :].rearrange("p (f c d) -> p f c d", c=2, d=HD)[:, :, par]
                    ins = nc.vector.tensor_tensor(part, part, psum[r_, 4 + 2 * t + par, :].rearrange("p (f d) -> p f d", f=KT), ALU.add)
            settle(ins)
            yh = yN.rearrange("p t (h d) -> p t h d", d=HD)
            ph = lambda a: a.unsqueeze(3).broadcast_to([P, NT, HEADS, HD])
            settle(nc.vector.tensor_reduce(mu_y, yh, AX.X, ALU.add))
            settle(nc.vector.tensor_scalar(mu_y, mu_y, 1.0 / HD, None, ALU.mult))
            nc.vector.tensor_tensor(yh, yh, ph(mu_y), ALU.subtract).then_inc(y_cent, 1)
            dve.wait_ge(y_sq, 1)
            settle(nc.vector.tensor_reduce(vr_y, bet.rearrange("p t (h d) -> p t h d", d=HD), AX.X, ALU.add))
            nc.vector.tensor_scalar(vr_y, vr_y, 1.0 / HD, 64e-5, ALU.mult, ALU.add).then_inc(y_var, 1)
            dve.wait_ge(y_root, 1)
            settle(nc.vector.reciprocal(rs_y, rt_y))
            settle(nc.vector.tensor_tensor(yh, yh, ph(rs_y), ALU.mult))
            both = lambda r_: r_.unsqueeze(1).broadcast_to([P, NT, D])
            settle(nc.vector.tensor_tensor(yN, yN, both(row_of("lnx_g")), ALU.mult))
            settle(nc.vector.tensor_tensor(yN, yN, both(row_of("lnx_b")), ALU.add))
            dve.wait_ge(bv_ready, 1)
            settle(nc.vector.tensor_tensor(yN, yN, kap, ALU.add))
            dve.wait_ge(proj_act, 6)
            nc.vector.tensor_tensor(yN, yN, gN, ALU.mult).then_inc(y_ready, 1)

            def add_normed(i, src, name):
                rms(i)
                g_ = row_of(name)
                for t in range(NT):
                    ins = nc.vector.scalar_tensor_tensor(out=posted[:, t, :], in0=src[:, t, :],
                                                         scalar=rstd[:, 2 * i + t:2 * i + t + 1], in1=g_,
                                                         op0=ALU.mult, op1=ALU.mult)
                settle(ins)
                nc.vector.tensor_tensor(h[:, :, :], h[:, :, :], posted, ALU.add).then_inc(h_ready, 1)

            def embed_dve(i, e_n, T, name):
                for b in ODD_EVEN(T)[1]:
                    evacuate(dve, T, b, xT)
                dve.wait_ge(e_act, e_n + 1)
                for c in range(2):
                    dve.wait_ge(gate_act, 2 * e_n + c + 1)
                    hl = slice(c * HALF, (c + 1) * HALF)
                    nc.vector.tensor_tensor(ge[:, :, hl], ge[:, :, hl], eN[:, :, hl], ALU.mult).then_inc(ge_ready, 1)
                add_normed(i, ge, name)

            for b in ODD_EVEN(T_YA)[1]:
                evacuate(dve, T_YA, b, xT)
            add_normed(6, yo, "norm_post0")
            dve.wait_ge(h_ready, 6)
            embed_dve(7, 0, T_H6, "ple_norm0")
            dve.wait_ge(h_ready, 7)

            for b in ODD_EVEN(T_H7)[1]:
                evacuate(dve, T_H7, b, xT, c8("norm_pre1"), c8("kv_norm"), xTb)
            dve.wait_ge(lam_landed, 16)
            lv = lamb.rearrange("p (a b) d -> p a b d", b=2)
            settle(nc.vector.tensor_tensor(lamp, lv[:, :, 0, :], lv[:, :, 1, :], ALU.mult))
            nc.vector.tensor_reduce(lams, lamp, AX.X, ALU.add).then_inc(lam_sum, 1)
            rms(8)
            dve.wait_ge(lam_exp, 1)
            settle(nc.vector.tensor_tensor(nlam, lame[:, 1:2], lame[:, 0:1], ALU.subtract))
            settle(nc.vector.tensor_scalar(nlam, nlam, -LAM0, None, ALU.add))
            for c, dst in enumerate((kD, vD, qD)):
                for j in range(2):
                    used(dve, W_KV + 2 * c + j)
                    nc.vector.tensor_scalar(dst[:, 1, j * HALF:(j + 1) * HALF], psum[:, 2 * j + 1, :], rstd[:, 17:18], None,
                                            ALU.mult).then_inc(kv_dve, 1)
            for inst, dst in ((T_KB, kDT), (T_QB, qDT)):
                for b in ODD_EVEN(inst)[1]:
                    evacuate(dve, inst, b, dst)
            for hh in range(HEADS + 1):
                if hh < HEADS:
                    dve.wait_ge(sc_done, HEADS + hh + 1)
                    if hh >= 4:
                        dve.wait_ge(pt_filled, HEADS + hh // 2 - 1)
                    buf = sd[:, hh % 4, :]
                    nc.vector.scalar_tensor_tensor(out=buf, in0=psum[:, 4 + hh % 2, 0:384], scalar=HD ** -0.5,
                                                   in1=C("causal"), op0=ALU.mult, op1=ALU.add).then_inc(sc_read, 1)
                    dve.wait_ge(sc_read, HEADS + hh + 1)
                    nc.vector.tensor_reduce(nmx[:, hh, 1:2], buf[:, 0:256], AX.X, ALU.max, negate=True)
                    nc.vector.tensor_reduce(nmx[:, hh, 0:1], buf[:, 256:384], AX.X, ALU.max, negate=True).then_inc(mx_ready, 1)
                if hh >= 2 and hh % 2 == 0:
                    g = hh // 2 - 1
                    dve.wait_ge(exp_done, HEADS + 2 * g + 2)
                    settle(nc.vector.reciprocal(rd[g % 2], sums[:, 2 * g:2 * g + 2, :]))
                    settle(nc.vector.tensor_scalar(rd[g % 2][:, 1, :], rd[g % 2][:, 1, :], nlam, None, ALU.mult))
                    b0, b1 = sd[:, (2 * g) % 4, :], sd[:, (2 * g + 1) % 4, :]
                    for t, cut in ((1, slice(0, 256)), (0, slice(256, 384))):
                        ins = nc.vector.tensor_scalar(b0[:, cut], b0[:, cut], rd[g % 2][:, 0, t:t + 1], None, ALU.mult)
                    settle(ins)
                    for t, cut in ((1, slice(0, 256)), (0, slice(256, 384))):
                        ins = nc.vector.scalar_tensor_tensor(out=b0[:, cut], in0=b1[:, cut], scalar=rd[g % 2][:, 1, t:t + 1],
                                                             in1=b0[:, cut], op0=ALU.mult, op1=ALU.add)
                    ins.then_inc(comb_ready, 1)
            dve.wait_ge(o_sq, 1)
            settle(nc.vector.tensor_reduce(vr_y[:, :, 0:8], oD2.rearrange("p t (h d) -> p t h d", d=P), AX.X, ALU.add))
            nc.vector.tensor_scalar(vr_y[:, :, 0:8], vr_y[:, :, 0:8], 1.0 / P, 1e-5, ALU.mult, ALU.add).then_inc(o_var, 1)
            dve.wait_ge(o_root, 1)
            settle(nc.vector.reciprocal(rs_y[:, :, 0:8], rt_y[:, :, 0:8]))
            oh = oD.rearrange("p t (h d) -> p t h d", d=P)
            settle(nc.vector.tensor_tensor(oh, oh, rs_y[:, :, 0:8].unsqueeze(3).broadcast_to([P, NT, 8, P]), ALU.mult))
            sl = row_of("subln")
            for t in range(NT):
                ins = nc.vector.scalar_tensor_tensor(out=oD[:, t, :], in0=oD[:, t, :], scalar=1.0 - LAM0, in1=sl,
                                                     op0=ALU.mult, op1=ALU.mult)
            settle(ins)
            dve.wait_ge(kv_act, 8)
            nc.vector.tensor_tensor(oD, oD, gD, ALU.mult).then_inc(od_ready, 1)
            for b in ODD_EVEN(T_OB)[1]:
                evacuate(dve, T_OB, b, xT)
            add_normed(9, yo, "norm_post1")
            dve.wait_ge(h_ready, 8)
            embed_dve(10, 1, T_H8, "ple_norm1")

        @block.tensor
        def _(pe):
            pe.wait_ge(par_landed, 32)
            pe.wait_ge(x_landed, 16)
            pe_transposes(pe, T_H0, h)
            evacuated(pe, T_H0)

            def qkv_free(pe, c):
                if c >= 2:
                    pe.wait_ge(qkv_act, c - 1)
                    pe.wait_ge(qkv_dve, c - 1)
            pe_linear(pe, W_QKV, 6, xT, qkv_free)
            pe.wait_ge(qkv_act, 6)
            pe.wait_ge(qkv_dve, 6)
            pe_transposes(pe, T_Q, qn)
            pe_transposes(pe, T_K, kn)
            evacuated(pe, T_K)
            for hh in range(HEADS + 2):
                if hh < HEADS:
                    if hh >= 2:
                        pe.wait_ge(sc_read, hh - 1)
                    p0, f = HD * (hh % 2), hh // 2
                    q, k = qT[p0:p0 + HD, f, :], kT[p0:p0 + HD, f, :]
                    nc.tensor.matmul(psum[:, 4 + hh % 2, 0:256], q[:, P:2 * P], k, start=True, stop=True)
                    nc.tensor.matmul(psum[:, 4 + hh % 2, 256:384], q[:, 0:P], k[:, 0:P], start=True, stop=True).then_inc(sc_done, 1)
                if hh >= 2:
                    g = hh - 2
                    pe.wait_ge(exp_done, g + 1)
                    if g >= 2:
                        pe.wait_ge(pt_copied, g - 1)
                    for j in range(3):
                        ins = nc.tensor.transpose(psum[:, 6 + g % 2, j * P:(j + 1) * P], sbuf_s[:, g % 3, j * P:(j + 1) * P], ident)
                    ins.then_inc(pt_filled, 1)
                    pe.wait_ge(pt_copied, g + 1)
                    pt = sbuf_pt[:, g % 2, :]
                    o = psum[:, g // 4, :].rearrange("p (h t d) -> p h t d", t=NT, d=HD)[:, g % 4]
                    v = vn[:, :, g * HD:(g + 1) * HD]
                    nc.tensor.matmul(o[:, 0], pt[:, 256:384], v[:, 0], start=True, stop=True)
                    nc.tensor.matmul(o[:, 1], pt[:, 0:128], v[:, 0], start=True, stop=False)
                    nc.tensor.matmul(o[:, 1], pt[:, 128:256], v[:, 1], start=False, stop=True).then_inc(pv_done, 1)
            pe.wait_ge(o_ready, 4)
            pe_transposes(pe, T_O, on)
            evacuated(pe, T_O)
            pe_linear(pe, W_O, 2, xT)
            pe.wait_ge(h_ready, 1)
            pe_transposes(pe, T_H1, h)
            evacuated(pe, T_H1)
            mlp_pe(pe, 0, W_MLP0)

            pe.wait_ge(xn_ready, 1)
            pe_transposes(pe, T_N2, xn)
            evacuated(pe, T_N2)
            pe.wait_ge(h_ready, 2)
            for i in range(8):
                n = W_IN + i // 2
                tile_ready(pe, n)
                if i >= 4:
                    pe.wait_ge(x_read, i - 3)
                for j in range(2):
                    f = 2 * (i % 2) + j
                    for k in range(KT):
                        ins = nc.tensor.matmul(psum[:, i % 4, j * SEQ:(j + 1) * SEQ],
                                               wt(n, KT, HALF)[:, k, f * P:(f + 1) * P], xT[:, k, :],
                                               start=(k == 0), stop=(k == KT - 1))
                ins.then_inc(in_filled, 1)
            tile_ready(pe, W_GATES)
            gw = wt(W_GATES, 4, KT, P)
            for i in range(4):
                pe.wait_ge(xc_ready, i + 1)
                if i >= 2:
                    pe.wait_ge(gates_read, i - 1)
                for j in range(2):
                    f = 2 * i + j
                    nc.tensor.matmul(psum[:, 4 + i % 2, j * SEQ:(j + 1) * SEQ], gw[:, 0, f, :], xc[:, f, :], start=True, stop=True)
                    ins = nc.tensor.matmul(psum[:, 6 + i % 2, j * SEQ:(j + 1) * SEQ], gw[:, 1, f, :], xc[:, f, :], start=True, stop=True)
                ins.then_inc(gates_filled, 1)
            pe.wait_ge(o_ready, 6)
            pe.wait_ge(y_read, 4)
            pe_linear(pe, W_RO, 2, og)
            pe.wait_ge(h_ready, 3)
            pe_transposes(pe, T_H3, h)
            evacuated(pe, T_H3)
            mlp_pe(pe, 1, W_MLP1)

            pe.wait_ge(xn_ready, 2)
            pe_transposes(pe, T_N5, xn5)
            pe.wait_ge(lor_landed, 32)
            for i in range(2):
                pe.wait_ge(mix_ready, i + 1)
                for k in range(KT):
                    ins = nc.tensor.matmul(psum[0:64, 4 + i, 0:SEQ], lora1_sb[:, i, k, :], xm[i][:, k, :],
                                           start=(k == 0), stop=(k == KT - 1))
                ins.then_inc(lora_filled, 1)
            for i in range(2):
                pe.wait_ge(lora_out, i + 1)
                if i == 1:
                    pe.wait_ge(lora2_read, 1)
                for t in range(NT):
                    for half in range(2):
                        ins = nc.tensor.matmul(psum[:, 2 * t + half, :], lt[0:64, i, t * P:(t + 1) * P],
                                               lora2_sb[0:64, i, half * HALF:(half + 1) * HALF], start=True, stop=True)
                ins.then_inc(lora2_filled, 1)
            pe.wait_ge(sig_ready, 1)
            pe.wait_ge(lora2_read, 2)
            for t in range(NT):
                for half in range(2):
                    ins = nc.tensor.matmul(psum[:, 2 * t + half, :], C("tri_incl"), sg[:, t, half * HALF:(half + 1) * HALF],
                                           start=True, stop=True)
            ins.then_inc(cum_filled, 1)

            def rkvg_free(pe, c):
                if c == 0:
                    pe.wait_ge(decays, 2)
                    pe.wait_ge(cum_prev, 1)
                elif c in (2, 3):
                    pe.wait_ge(proj_act, c - 1)
                elif c in (4, 5):
                    pe.wait_ge(proj_dve, c - 3)
                elif c in (6, 7):
                    pe.wait_ge(proj_act, c - 3)
                if c % 2 == 0:
                    pe.wait_ge(mix_ready, 3 + c // 2)

            def project(i):
                for c in (2 * i, 2 * i + 1):
                    pe_chunk(pe, W_RKVG + c, c, xm[i % 2], rkvg_free)

            project(0)
            pe.wait_ge(decays, 1)
            for f in range(KT):
                for t in range(NT):
                    ins = nc.tensor.matmul(psum[:, 4, 4 * f + 2 * t:4 * f + 2 * t + 2], Pd[:, t, f * P:(f + 1) * P], C("last"),
                                           start=True, stop=True)
            ins.then_inc(last_filled, 1)
            project(1)
            project(2)
            pe.wait_ge(beta_kap, 2)
            pe.wait_ge(khat, 2)
            pe.wait_ge(bonus, 2)
            for inst, src in ((T_KAP, kap), (T_RH, rN), (T_BET, bet), (T_KH, kN)):
                pe_transposes(pe, inst, src)
            project(3)
            evacuated(pe, T_KH)

            for b in range(2):
                pe.wait_ge(proj_act, 6)
                pe.wait_ge(last_read, 1)
            STEPS = ["x0", "x1", "x2", "x3"] + list(range(1, 12))
            for pp in range(4):
                for s_ in STEPS:
                    for b in range(2):
                        f, B = 2 * pp + b, 4 * b
                        dve_did = lambda st, p_=pp: core_wait(pe, core_dve, DVE_AT, p_, b, st)
                        act_did = lambda st, p_=pp: core_wait(pe, core_act, ACT_AT, p_, b, st)
                        u, x_, o_, z_ = U[b], XX[b], OFF[b], U[b][:, :, 0, :]
                        bank = lambda k, q: psum[:, B + k, q * P:(q + 1) * P]
                        for q in range(4):
                            hh, t = q // 2, q % 2
                            p0 = HD * hh
                            head = slice((2 * f + hh) * HD, (2 * f + hh + 1) * HD)
                            tt = slice(t * P, (t + 1) * P)
                            if isinstance(s_, str):
                                if q != int(s_[1]):
                                    continue
                                if q == 0 and pp > 0:
                                    dve_did(11, pp - 1)
                                    act_did(11, pp - 1)
                                kr = KR[p0:p0 + HD, f, :, tt]
                                nc.tensor.matmul(psum[:, B + q, 0:256], bT[p0:p0 + HD, f, tt], kr, start=True, stop=True)
                                ins = nc.tensor.matmul(psum[:, B + q, 256:512], khT[p0:p0 + HD, f, tt], kr, start=True, stop=True)
                            elif s_ == 1:
                                if q == 0:
                                    dve_did("x1")
                                ins = nc.tensor.matmul(psum[:, B + hh, tt], KR[p0:p0 + HD, f, 0, tt], bT[p0:p0 + HD, f, tt], start=True, stop=True)
                            elif s_ == 2:
                                if q == 0:
                                    dve_did(1)
                                nc.tensor.matmul(bank(1, q), x_[:, q, :], u[:, q, 1, :], start=True, stop=True)
                                nc.tensor.matmul(bank(2, q), u[:, q, 1, :], x_[:, q, :], start=True, stop=True)
                                ins = nc.tensor.matmul(psum[:, B + 3, q * 64:(q + 1) * 64], u[:, q, 3, :], vN[:, t, head], start=True, stop=True)
                            elif s_ == 3:
                                if q == 0:
                                    dve_did(2)
                                    act_did(2)
                                    pe.wait_ge(core_pool[b], pp + 1)
                                nc.tensor.matmul(bank(0, q), x_[:, q, :], z_[:, q, :], start=True, stop=True)
                                nc.tensor.matmul(bank(1, q), x_[:, q, :], u[:, q, 1, :], start=True, stop=True)
                                ins = nc.tensor.matmul(bank(2, q), u[:, q, 1, :], x_[:, q, :], start=True, stop=True)
                            elif s_ == 4:
                                if q == 0:
                                    dve_did(3)
                                    act_did(3)
                                nc.tensor.matmul(bank(3, q), x_[:, q, :], z_[:, q, :], start=True, stop=True)
                                ins = nc.tensor.matmul(bank(2, q), u[:, q, 1, :], x_[:, q, :], start=True, stop=True)
                            elif s_ == 5:
                                if q == 0:
                                    dve_did(4)
                                    act_did(4)
                                ins = nc.tensor.matmul(bank(0, q), x_[:, q, :], z_[:, q, :], start=True, stop=True)
                            elif s_ in (6, 8):
                                if q == 0:
                                    dve_did(s_ - 1)
                                nc.tensor.transpose(bank(1, q), z_[:, q, :], ident)
                                ins = nc.tensor.matmul(bank(2, q), o_[:, (s_ - 6) // 2, q, :], z_[:, q, :], start=True, stop=True)
                            elif s_ in (7, 9):
                                if q == 0:
                                    dve_did(s_ - 1)
                                    act_did(s_ - 1)
                                ins = nc.tensor.matmul(bank(0, q), x_[:, q, :], u[:, q, 1, :], start=True, stop=True)
                            elif s_ == 10:
                                if q == 0:
                                    dve_did(9)
                                nc.tensor.matmul(bank(1, q)[:, 0:64], z_[:, q, :], kap[:, t, head], start=True, stop=True)
                                ins = nc.tensor.matmul(bank(1, q)[:, 64:128], z_[:, q, :], BV[b][:, q, :], start=True, stop=True)
                            else:
                                if q == 0:
                                    act_did(10)
                                wu = WU[b][:, q, :]
                                for c in range(2):
                                    g = 2 * t + c
                                    cc = slice(64 * c, 64 * c + 64)
                                    at = lambda n: psum[p0:p0 + HD, B + 2 + c, 64 * (n - 3 * c):64 * (n - 3 * c) + 64]
                                    if g in (1, 2):
                                        o = at(M_OF[g])
                                        nc.tensor.matmul(o, C("eye2")[cc, :], C("eye2")[cc, :], start=True, stop=False)
                                        nc.tensor.matmul(o, wu[cc, 0:64], bet[cc, t, head], start=False, stop=True)
                                    if g < 3:
                                        o = at(N_OF[g])
                                        nc.tensor.matmul(o, kN[cc, t, head], vN[cc, t, head], start=True, stop=False)
                                        nc.tensor.matmul(o, bet[cc, t, head], wu[cc, 64:128], start=False, stop=True)
                                nc.tensor.matmul(psum[p0:p0 + HD, B + 1, tt], wu[:, 0:64], u[:, q, 2, :],
                                                 start=True, stop=True)
                                o = psum[:, B, q * 64:(q + 1) * 64]
                                nc.tensor.matmul(o, u[:, q, 4, :], vN[:, t, head], start=True, stop=False)
                                ins = nc.tensor.matmul(o, u[:, q, 2, :], wu[:, 64:128], start=False, stop=True)
                        ins.then_inc(core_filled[b], 1)
            for b in range(2):
                core_wait(pe, core_dve, DVE_AT, 3, b, 11)
                core_wait(pe, core_act, ACT_AT, 3, b, 11)
            for g in (1, 2):
                pe.wait_ge(state_ready, g)
                for f in range(KT):
                    for p0 in (0, HD):
                        ins = nc.tensor.matmul(psum[p0:p0 + HD, 2 * (g - 1) + p0 // HD, f * 64:(f + 1) * 64], MN[p0:p0 + HD, f, M_OF[g], :],
                                               Sg[g][p0:p0 + HD, f, :], start=True, stop=True)
                ins.then_inc(state_filled, 1)
            pe.wait_ge(state_ready, 3)
            for g in (1, 2, 3):
                t, c = g // 2, g % 2
                for hh in range(HEADS):
                    f, p0 = hh // 2, HD * (hh % 2)
                    ins = nc.tensor.matmul(psum[64 * c:64 * c + 64, 4 + 2 * t + hh % 2, f * 64:(f + 1) * 64],
                                           KR[p0:p0 + HD, f, 1, t * P + 64 * c:t * P + 64 * c + 64], Sg[g][p0:p0 + HD, f, :],
                                           start=True, stop=True)
            ins.then_inc(ys_filled, 1)
            pe.wait_ge(y_ready, 1)

            def embed_pe(tile, e_n, T):
                tile_ready(pe, tile)
                pe.wait_ge(lor_landed, 48 + 16 * e_n)
                pe.wait_ge(yo_act, 2 * e_n + 2)
                for c in range(2):
                    for t in range(NT):
                        for k in range(2):
                            ins = nc.tensor.matmul(psum[:, 2 * c + t, :], pT_sb[:, k, t * P:(t + 1) * P],
                                                   wt(tile, 4, D)[:, k, c * HALF:(c + 1) * HALF], start=(k == 0), stop=(k == 1))
                ins.then_inc(tile_used, 1)
                pe.wait_ge(h_ready, 6 + 2 * e_n)
                pe_transposes(pe, T, h)
                evacuated(pe, T)
                pe.wait_ge(e_act, e_n + 1)
                pe_linear(pe, tile + 1, 2, xT)

            pe_transposes(pe, T_YA, yN)
            evacuated(pe, T_YA)
            pe_linear(pe, W_OUT_A, 2, xT)
            embed_pe(W_PLE0, 0, T_H6)

            pe.wait_ge(h_ready, 7)
            pe_transposes(pe, T_H7, h)
            evacuated(pe, T_H7)

            def kvqg_free(pe, c):
                if c >= 2:
                    pe.wait_ge(kv_act, c - 1)
                    pe.wait_ge(kv_dve, min(c - 1, 6))
            for c in range(8):
                pe_chunk(pe, W_KV + c, c, xTb if c < 4 else xT, kvqg_free)
            pe.wait_ge(roped, 1)
            pe_transposes(pe, T_KB, kD)
            pe.wait_ge(roped, 2)
            pe_transposes(pe, T_QB, qD)
            evacuated(pe, T_QB)
            pe.wait_ge(kv_act, 8)
            for hh in range(HEADS + 3):
                if hh < HEADS:
                    if hh >= 2:
                        pe.wait_ge(sc_read, HEADS + hh - 1)
                    p0, f = HD * (hh % 2), hh // 2
                    q, k = qDT[p0:p0 + HD, f, :], kDT[p0:p0 + HD, f, :]
                    nc.tensor.matmul(psum[:, 4 + hh % 2, 0:256], q[:, P:2 * P], k, start=True, stop=True)
                    nc.tensor.matmul(psum[:, 4 + hh % 2, 256:384], q[:, 0:P], k[:, 0:P], start=True, stop=True).then_inc(sc_done, 1)
                if hh >= 3 and hh % 2 == 1:
                    g = (hh - 3) // 2
                    pe.wait_ge(comb_ready, g + 1)
                    if g >= 2:
                        pe.wait_ge(pt_copied, HEADS + g - 1)
                    for j in range(3):
                        ins = nc.tensor.transpose(psum[:, 6 + g % 2, j * P:(j + 1) * P], sd[:, (2 * g) % 4, j * P:(j + 1) * P], ident)
                    ins.then_inc(pt_filled, 1)
                    pe.wait_ge(pt_copied, HEADS + g + 1)
                    pt = pt2[:, g % 2, :]
                    o = psum[:, g // 2, :].rearrange("p (h t d) -> p h t d", t=NT, d=P)[:, g % 2]
                    v = vD[:, :, g * P:(g + 1) * P]
                    nc.tensor.matmul(o[:, 0], pt[:, 256:384], v[:, 0], start=True, stop=True)
                    nc.tensor.matmul(o[:, 1], pt[:, 0:128], v[:, 0], start=True, stop=False)
                    nc.tensor.matmul(o[:, 1], pt[:, 128:256], v[:, 1], start=False, stop=True).then_inc(pv_done, 1)
            pe.wait_ge(od_ready, 1)
            pe_transposes(pe, T_OB, oD)
            evacuated(pe, T_OB)
            pe_linear(pe, W_OUT_B, 2, xT)
            embed_pe(W_PLE1, 1, T_H8)

def layout(inp):
    f = lambda n: np.ascontiguousarray(np.asarray(inp[n]))
    tiles = []

    def cols_tile(wm, c):
        tiles.append(wm[:, c * HALF:(c + 1) * HALF].reshape(KT, P, HALF).transpose(1, 0, 2).reshape(P, 4096))

    def rows_tile(wm, c):
        tiles.append(wm[c * HALF:(c + 1) * HALF].reshape(4, P, D).transpose(1, 0, 2).reshape(P, 4096))

    def mlp(m):
        w1, w2 = f("mlp_w1")[m], f("mlp_w2")[m]
        cols_tile(w1, 0)
        for c in range(1, 8):
            cols_tile(w1, c)
            rows_tile(w2, c - 1)
        rows_tile(w2, 7)

    def ple(i):
        half = f("ple_w_2")[i].reshape(2, P, D).transpose(1, 0, 2).reshape(P, 2048)
        tiles.append(np.concatenate([half, half], 1))
        for c in range(2):
            cols_tile(f("ple_gate_2")[i], c)

    qkv = f("attn_w_qkv")[0]
    for c in (0, 2, 4, 1, 3, 5):
        cols_tile(qkv, c)
    for c in range(2):
        cols_tile(f("attn_w_o")[0], c)
    mlp(0)
    for c in range(4):
        cols_tile(f("rec_w_in")[0], c)
    tiles.append(np.concatenate([f(n)[0].transpose(1, 0, 2).reshape(P, D) for n in ("rec_w_ga", "rec_w_gx")] * 2, 1))
    for c in range(2):
        cols_tile(f("rec_w_o")[0], c)
    mlp(1)
    for j in (1, 0, 2, 3):
        for c in range(2):
            cols_tile(f("a_w_in_2")[0, j], c)
    for c in range(2):
        cols_tile(f("a_w_out_2")[0], c)
    ple(0)
    for c in range(4):
        cols_tile(f("kv_w_2"), c)
    for c in range(4):
        cols_tile(f("b_w_in_2")[0], c)
    for c in range(2):
        cols_tile(f("b_w_out_2")[0], c)
    ple(1)
    w = np.stack(tiles)
    assert w.shape[0] == W_TILES

    col = lambda v: v.reshape(KT, P).T
    b_in, cw, mu = f("rec_b_in")[0], f("rec_conv_w")[0], f("a_mu_2")[0]
    vals = {"norm_mix0": f("norm_mix")[0], "norm_mix1": f("norm_mix")[1], "norm_mlp0": f("norm_mlp")[0],
            "norm_mlp1": f("norm_mlp")[1], "b_in_x": b_in[:D], "b_in_y": b_in[D:], "conv_b": f("rec_conv_b")[0],
            "b_ga": f("rec_b_ga")[0].reshape(-1), "b_gx": f("rec_b_gx")[0].reshape(-1), "a_param": f("rec_a_param")[0],
            "norm_pre0": f("norm_pre_2")[0], "norm_pre1": f("norm_pre_2")[1], "kv_norm": f("kv_norm_2")}
    vals |= {f"conv_w{i}": cw[i] for i in range(4)} | {f"mu{i}": mu[i] for i in range(6)}
    cols = np.stack([col(vals[n]) for n in COLS], 1)
    rv = {"b_o": f("rec_b_o")[0], "norm_final": f("norm_final"), "w0": f("a_w0_2")[0], "a0": f("a_a0_2")[0],
          "k_k": f("a_k_k_2")[0], "k_a": f("a_k_a_2")[0], "r_k": f("a_r_k_2")[0].reshape(-1),
          "lnx_g": f("a_lnx_g_2")[0], "lnx_b": f("a_lnx_b_2")[0], "norm_post0": f("norm_post_2")[0],
          "norm_post1": f("norm_post_2")[1], "ple_norm0": f("ple_norm_2")[0], "ple_norm1": f("ple_norm_2")[1],
          "subln": np.concatenate([f("b_subln_2")[0]] * 8)}
    rows = np.stack([rv[n] for n in ROWS])
    rel = f("attn_rel_bias")[0][:, ::-1]
    relt = np.concatenate([rel[:, :1]] * 127 + [rel], 1)
    lora1 = np.stack([f(n)[0].reshape(KT, P, 64).transpose(1, 0, 2) for n in ("a_w1_2", "a_a1_2")], 1)
    lora2 = np.stack([f(n)[0] for n in ("a_w2_2", "a_a2_2")], 1)
    pT = f("p_2")[:, 0].transpose(0, 2, 1).reshape(2, 2, P, SEQ).transpose(2, 0, 1, 3)
    lam = f("b_lambda_2")[0].reshape(1, 256)
    x = f("x")[0]
    return {"x": x, "w": w, "cols": cols, "rows": rows, "consts": shape_constants(), "relt": relt, "lora1": lora1,
            "lora2": lora2, "pT": pT, "lam": lam}


def kernel(**inputs):
    import concourse.bacc as bacc
    from concourse.bass_utils import run_bass_kernel_spmd

    nc = bacc.Bacc("TRN2", target_bir_lowering=False, num_devices=1)
    arrays = {k: np.ascontiguousarray(v) for k, v in layout(inputs).items()}
    aps = {k: nc.dram_tensor(k, v.shape, F32, kind="ExternalInput").ap() for k, v in arrays.items()}
    out = nc.dram_tensor("out", (SEQ, D), F32, kind="ExternalOutput").ap()
    build(nc, **aps, out=out)
    r = run_bass_kernel_spmd(nc, [arrays], core_ids=[0])
    return r.results[0]["out"].reshape(1, SEQ, D)
```

```python
from contextlib import ExitStack

import numpy as np

import concourse.bass as bass
from concourse import mybir

ALU = mybir.AluOpType
ACT = mybir.ActivationFunctionType
F32 = mybir.dt.float32
F32R = mybir.dt.float32r
AX = mybir.AxisListType

P = 128
SEQ, D, DFF = 256, 1024, 4096
NT, KT = SEQ // P, D // P
HALF = 512
HEADS, HD = 16, 64
EPS = 1e-6
PIECE = 1024
RING = 8

W_QKV, W_O, W_MLP0, W_INX, W_GATES, W_INY, W_RO, W_MLP1 = 0, 6, 8, 24, 26, 27, 29, 31
W_RKVG, W_OUT_A, W_PLE0, W_KV, W_QG, W_OUT_B, W_PLE1, W_TILES = 47, 55, 57, 60, 64, 68, 70, 73

PLAIN = {W_GATES, W_PLE0, W_PLE1} | set(range(W_RKVG, W_RKVG + 6))
SPLITS = [0]
for _m in range(4 * W_TILES):
    SPLITS.append(SPLITS[-1] + (_m // 4 not in PLAIN))

COLS = ["norm_mix0", "norm_mix1", "norm_mlp0", "norm_mlp1", "b_in_x", "b_in_y", "conv_w0", "conv_w1", "conv_w2",
        "conv_w3", "conv_b", "b_ga", "b_gx", "a_param", "norm_pre0", "norm_pre1", "kv_norm",
        "mu0", "mu1", "mu2", "mu3", "mu4", "mu5"]
ROWS = ["b_o", "norm_final", "w0", "a0", "k_k", "k_a", "r_k", "lnx_g", "lnx_b", "norm_post0", "ple_norm0",
        "subln", "norm_post1", "ple_norm1"]
CONSTS = {}
_at = 0
for _name, _n in (("ident", 128), ("tri_incl", 128), ("mask_x", 512), ("mask_a", 384), ("causal", 384),
                  ("cos", 16), ("sin", 16), ("eye2", 64), ("last", 2)):
    CONSTS[_name] = (_at, _n)
    _at += _n
N_CONSTS = _at


def shape_constants():
    i = np.arange(P)
    c = np.zeros((P, N_CONSTS), np.float32)

    def put(name, value):
        a, n = CONSTS[name]
        c[:, a:a + n] = np.asarray(value, np.float32).reshape(P, n)

    r, s = i[:, None], i[None, :]
    same = lambda n: (r // n) == (s // n)
    put("ident", r == s)
    put("tri_incl", (r <= s) & same(64))
    put("mask_x", np.stack([-1.0 * ((r < s) & same(16)), 1.0 * ((r <= s) & same(64)),
                            1.0 * ((r < s) & same(64)), 1.0 * ((r <= s) & same(64))], 1))
    put("mask_a", np.stack([-1.0 * ((s < r) & same(16)), 1.0 * ((s < r) & same(32) & ~same(16)),
                            1.0 * ((s < r) & same(64) & ~same(32))], 1))
    k = np.arange(SEQ)[None, :]
    put("causal", np.concatenate([np.where(k <= P + r, 0, -1e30), np.where(s <= r, 0, -1e30)], 1))
    inv = np.float32(500000.0) ** (-np.arange(0, 16, 2, dtype=np.float32) / np.float32(16))
    ang = (np.arange(SEQ, dtype=np.float32)[:, None] * inv.astype(np.float32)[None, :]).astype(np.float32)
    tok = ang.reshape(NT, P, 8).transpose(1, 0, 2)
    put("cos", np.cos(tok.astype(np.float64)))
    put("sin", np.sin(tok.astype(np.float64)))
    put("eye2", (i[:, None] % 64) == np.arange(64)[None, :])
    put("last", np.stack([i == 63, i == 127], 1))
    return c


def build(nc, x, w, cols, rows, consts, relt, lora1, lora2, pT, lam, out):
    with ExitStack() as ctx:
        def sb(name, shape):
            return ctx.enter_context(nc.sbuf_tensor(name, shape, F32))

        def sem(name):
            return ctx.enter_context(nc.semaphore(name))

        ring = sb("ring", [P, RING, PIECE])
        ring_r = nc.alloc_sbuf_tensor_at("ring_r", [P, RING, PIECE], F32R, offset=nc.sbuf_base - 4 * RING * PIECE,
                                         align_bytes=32)
        h = sb("h", [P, NT, D])
        ARENA = 32800
        arena = sb("arena", [P, ARENA])
        arena_base = nc.sbuf_base - 4 * ARENA
        col = sb("col", [P, len(COLS), KT])
        row = sb("row", [P, 5, D])
        con = sb("con", [P, N_CONSTS])
        small = sb("small", [P, 1024])
        psum = ctx.enter_context(nc.psum_tensor("psum", [P, 8, HALF], F32))

        def C(name):
            a, n = CONSTS[name]
            return con[:, a:a + n]

        ident = C("ident")

        def c8(name):
            return col[:, COLS.index(name), :]

        def shaped(v, dims):
            if len(dims) < 2:
                return v
            names = "abcd"[:len(dims)]
            return v.rearrange("p (" + " ".join(names) + ") -> p " + " ".join(names),
                               **{k: d for k, d in zip(names[1:], dims[1:])})

        def view(off, *dims):
            n = int(np.prod(dims))
            assert off + n <= ARENA, (off, dims)
            return shaped(arena[:, off:off + n], dims)

        def place_r(name, off, n):
            assert off + n <= ARENA
            return nc.alloc_sbuf_tensor_at(name, [P, n], F32R, offset=arena_base + 4 * off, align_bytes=32)[:, :]

        def raw(m, *dims):
            return shaped(ring[:, m % RING, :], dims)

        def high(m, *dims):
            return shaped(high_r[:, PIECE * (m % RING):PIECE * (m % RING + 1)], dims)

        def read(v):
            return v.bitcast(F32)

        def low(m, *dims):
            return shaped(ring_r[:, m % RING, :], dims)

        small_at = [0]

        def little(n):
            small_at[0] += n
            assert small_at[0] <= 1024
            return small[:, small_at[0] - n:small_at[0]]

        S = 2048
        high_r = place_r("high_r", 12 * S, RING * PIECE)
        piece_landed = [sem(f"piece_landed{i}") for i in range(RING)]
        high_made, low_made, piece_used = sem("high_made"), sem("low_made"), sem("piece_used")
        x_landed, spread_stored = sem("x_landed"), sem("spread_stored")
        spread = nc.dram_tensor("bias_spread", (P, HEADS * 384), F32, kind="Internal").ap()
        par_landed = sem("par_landed")
        row_landed = [sem(f"row_landed{i}") for i in range(5)]
        act_step, dve_step, pool_step = sem("act_step"), sem("dve_step"), sem("pool_step")
        stat_sum, stat_var, stat_root, rstd_ready = sem("stat_sum"), sem("stat_var"), sem("stat_root"), sem("rstd_ready")
        h_ready = sem("h_ready")
        tp_filled = sem("tp_filled")
        tp_act, tp_dve = sem("tp_act"), sem("tp_dve")
        out_stored = sem("out_stored")

        N_STATS = 12
        ss, var, root, rstd = little(2 * N_STATS), little(2 * N_STATS), little(2 * N_STATS), little(2 * N_STATS)

        (T_H0, T_Q, T_K, T_O, T_H1, T_N2, T_H3, T_N5, T_KAP, T_RH, T_BET, T_KH, T_YA, T_H6, T_H7, T_KB, T_QB, T_OB,
         T_H8) = range(19)

        SPLIT_T = {T_H0, T_O, T_H1, T_N2, T_H3, T_YA, T_H6, T_H7, T_OB, T_H8}
        BANK_OF, ACT_BANKS, DVE_BANKS, PREVIOUS, _last = [], [0], [0], [], {}
        for _i in range(T_H8 + 1):
            for _b in range(4):
                bank_ = 4 + _b if _i in SPLIT_T else 6 + _b % 2
                BANK_OF.append(bank_)
                PREVIOUS.append(_last.get(bank_))
                _last[bank_] = len(BANK_OF) - 1
                ACT_BANKS.append(ACT_BANKS[-1] + (_i in SPLIT_T or _b % 2 == 0))
                DVE_BANKS.append(DVE_BANKS[-1] + (_i in SPLIT_T or _b % 2 == 1))

        def bank_out(eng, g):
            if ACT_BANKS[g + 1]:
                eng.wait_ge(tp_act, ACT_BANKS[g + 1])
            if DVE_BANKS[g + 1]:
                eng.wait_ge(tp_dve, DVE_BANKS[g + 1])

        def pe_transposes(pe, inst, src):
            for b in range(4):
                g = 4 * inst + b
                if PREVIOUS[g] is not None:
                    bank_out(pe, PREVIOUS[g])
                for j in range(2):
                    for t in range(NT):
                        ins = nc.tensor.transpose(psum[:, BANK_OF[g], (2 * j + t) * P:(2 * j + t + 1) * P],
                                                  src[:, t, (2 * b + j) * P:(2 * b + j + 1) * P], ident)
                ins.then_inc(tp_filled, 1)

        def filling(g):
            return psum[:, BANK_OF[g], :].rearrange("p (j t) -> p j t", j=2)

        def evacuate(eng, inst, b, dst, gain=None):
            g = 4 * inst + b
            eng.wait_ge(tp_filled, g + 1)
            on_act = b % 2 == 0
            assert on_act == (eng is engines["act"])
            if gain is None:
                dd = dst[:, 2 * b:2 * b + 2, :]
                ins = nc.scalar.copy(dd, filling(g)) if on_act else nc.vector.tensor_copy(dd, filling(g))
            else:
                for j in range(2):
                    k = 2 * b + j
                    if on_act:
                        ins = nc.scalar.activation(dst[:, k, :], filling(g)[:, j, :], ACT.Copy, scale=gain[:, k:k + 1])
                    else:
                        ins = nc.vector.tensor_scalar(dst[:, k, :], filling(g)[:, j, :], gain[:, k:k + 1], None, ALU.mult)
            ins.then_inc(tp_act if on_act else tp_dve, 1)

        def evacuate_high(act, inst, *pairs):
            for b in range(4):
                g = 4 * inst + b
                act.wait_ge(tp_filled, g + 1)
                for dst, gain in pairs:
                    if gain is None:
                        ins = nc.scalar.copy(dst[:, 2 * b:2 * b + 2, :], filling(g))
                    else:
                        for j in range(2):
                            k = 2 * b + j
                            ins = nc.scalar.activation(dst[:, k, :], filling(g)[:, j, :], ACT.Copy, scale=gain[:, k:k + 1])
                ins.then_inc(tp_act, 1)

        def evacuate_low(dve, inst, *triples):
            for b in range(4):
                g = 4 * inst + b
                dve.wait_ge(tp_act, ACT_BANKS[g + 1])
                for hi, dst, gain in triples:
                    if gain is None:
                        u = slice(2 * b, 2 * b + 2)
                        ins = nc.vector.tensor_tensor(dst[:, u, :], filling(g), read(hi[:, u, :]), ALU.subtract)
                    else:
                        for j in range(2):
                            k = 2 * b + j
                            ins = nc.vector.scalar_tensor_tensor(out=dst[:, k, :], in0=filling(g)[:, j, :],
                                                                 scalar=gain[:, k:k + 1], in1=read(hi[:, k, :]),
                                                                 op0=ALU.mult, op1=ALU.subtract)
                ins.then_inc(tp_dve, 1)

        def evacuated(eng, inst):
            bank_out(eng, 4 * inst + 3)

        engines = {}

        qkv_act, qkv_dve = sem("qkv_act"), sem("qkv_dve")
        sc_done, sc_read, mx_ready, exp_done, pt_filled, pt_copied, pv_done, o_ready = (
            sem(n) for n in ("sc_done", "sc_read", "mx_ready", "exp_done", "pt_filled", "pt_copied", "pv_done", "o_ready"))
        bias_ready = sem("bias_ready")
        z_relu, zz_ready, z_high, z_low = sem("z_relu"), sem("zz_ready"), sem("z_high"), sem("z_low")
        mask_set = sem("mask_set")

        x_read, y_read, xc_ready, gates_read, og_high, og_low = (
            sem(n) for n in ("x_read", "y_read", "xc_ready", "gates_read", "og_high", "og_low"))
        xn_ready, pad_zero, decay_ready, decay_part, m2_ready, m_ready, g_ready = (
            sem(n) for n in ("xn_ready", "pad_zero", "decay_ready", "decay_part", "m2_ready", "m_ready", "g_ready"))
        lor_landed, lam_landed = sem("lor_landed"), sem("lam_landed")
        mix_ready, lora_filled, lora_out, lora2_filled, lora2_read, sig_ready, cum_filled, cum_prev, decays, last_filled, last_read = (
            sem(n) for n in ("mix_ready", "lora_filled", "lora_out", "lora2_filled", "lora2_read", "sig_ready",
                             "cum_filled", "cum_prev", "decays", "last_filled", "last_read"))
        proj_act, proj_dve, kk_raw, kk_sq, kk_var, kk_root, kk_unit, k_ready, beta_kap, khat, bonus = (
            sem(n) for n in ("proj_act", "proj_dve", "kk_raw", "kk_sq", "kk_var", "kk_root", "kk_unit", "k_ready",
                             "beta_kap", "khat", "bonus"))
        xg_high, xg_low = sem("xg_high"), sem("xg_low")
        core_filled, core_dve, core_act, core_pool = ([sem(f"{n}{b}") for b in range(2)] for n in
                                                      ("core_filled", "core_dve", "core_act", "core_pool"))
        state_filled, state_ready, ys_filled, y_sq, y_var, y_root, y_ready, bv_ready, y_cent = (
            sem(n) for n in ("state_filled", "state_ready", "ys_filled", "y_sq", "y_var", "y_root", "y_ready",
                             "bv_ready", "y_cent"))
        yo_act, e_act, gate_act, ge_ready = sem("yo_act"), sem("e_act"), sem("gate_act"), sem("ge_ready")
        kv_act, kv_dve, roped, lam_sum, lam_exp, comb_ready, o_act, o_sq, o_var, o_root, od_ready = (
            sem(n) for n in ("kv_act", "kv_dve", "roped", "lam_sum", "lam_exp", "comb_ready", "o_act", "o_sq", "o_var",
                             "o_root", "od_ready"))
        row_ready = row_landed

        qn, kn, vn = (view(i * S, NT, D) for i in (0, 1, 2))
        qT, kT = view(3 * S, KT, SEQ), view(4 * S, KT, SEQ)
        on = view(5 * S, NT, D)
        bias = view(6 * S, HEADS, 384)
        sbuf_s = view(9 * S, 3, 384)
        sbuf_pt = view(9 * S + 1152, 2, 384)
        XT = 30720
        XH, XL, XBH, XBL = (shaped(place_r(name, at * S, S), (KT, SEQ)) for name, at in
                            (("x_high", 10), ("x_low", 11), ("xb_high", 6), ("xb_low", 7)))
        xT2, xTb2 = (XH, XL), (XBH, XBL)

        def junk_at(i):
            return view((5 if i < 6 else 8) * S, NT, D)
        nmx = little(2 * 2 * HEADS).rearrange("p (h t) -> p h t", t=2)
        sums = little(2 * 2 * HEADS).rearrange("p (h t) -> p h t", t=2)
        rsum = little(2 * 2 * HEADS).rearrange("p (h t) -> p h t", t=2)
        QKV = [(qn, 0), (kn, 0), (vn, 0), (qn, 1), (kn, 1), (vn, 1)]
        zr, zz = view(0, 4, SEQ), view(1024, 4, SEQ)
        zh, zl = (shaped(place_r(name, at * S, S), (2, 4, SEQ)) for name, at in (("zz_high", 1), ("zz_low", 2)))

        def used_piece(eng, m):
            eng.wait_ge(piece_used, m + 1)

        def used(eng, n):
            used_piece(eng, 4 * n + 3)

        def piece_ready(pe, m):
            if m // 4 in PLAIN:
                pe.wait_ge(piece_landed[m % RING], 16 * (m // RING + 1))
            else:
                pe.wait_ge(low_made, SPLITS[m] + 1)

        def parts(lhs, rhs):
            return ((lhs[0], rhs[0]), (lhs[0], rhs[1]), (lhs[1], rhs[0]))

        def transposed(pe, inst):
            return lambda i: bank_out(pe, 4 * inst + i)

        def pe_chunk(pe, n, c, lhs, banks_free, ready=None):
            for i in range(4):
                m = 4 * n + i
                piece_ready(pe, m)
                if ready is not None:
                    ready(i)
                if i == 0 and banks_free is not None:
                    banks_free(pe, c)
                for t in range(NT):
                    tt = slice(t * P, (t + 1) * P)
                    for j in range(2):
                        k = 2 * i + j
                        if n in PLAIN:
                            pairs = ((lhs[:, k, tt], raw(m, 2, HALF)[:, j, :]),)
                        else:
                            pairs = parts([x_[:, k, tt] for x_ in lhs], (high(m, 2, HALF)[:, j, :], low(m, 2, HALF)[:, j, :]))
                        for q, (a, b) in enumerate(pairs):
                            ins = nc.tensor.matmul(psum[:, 2 * (c % 2) + t, :], a, b, start=(k == 0 and q == 0),
                                                   stop=(k == KT - 1 and q == len(pairs) - 1))
                ins.then_inc(piece_used, 1)

        def pe_linear(pe, first, chunks, lhs, banks_free=None, ready=None):
            for c in range(chunks):
                pe_chunk(pe, first + c, c, lhs, banks_free, ready if c == 0 else None)

        def pe_feature_tile(pe, m, out, ready=None):
            piece_ready(pe, m)
            for k in range(KT):
                if ready is not None and k % 2 == 0:
                    ready(k // 2)
                for q, (a, b) in enumerate(parts((high(m, KT, P)[:, k, :], low(m, KT, P)[:, k, :]), [x_[:, k, :] for x_ in xT2])):
                    ins = nc.tensor.matmul(out, a, b, start=(k == 0 and q == 0), stop=(k == KT - 1 and q == 2))
            ins.then_inc(piece_used, 1)

        xn = view(0, NT, D)
        xb = view(2 * S, KT, SEQ + 3)
        yg, xc, rg, ig, aa, th, bb_, hs = (view(i * S, KT, SEQ) for i in (4, 5, 6, 7, 8, 9, 0, 1))
        og = xc
        sp8, nsp8 = little(KT), little(KT)
        spt = [little(KT) for _ in range(5)]

        vN, kap, bet, kN = (view(i * S, NT, D) for i in (0, 1, 2, 3))
        Pd, Pi, Pp, aN, rN = (view(i * S, NT, D) for i in (4, 5, 6, 7, 8))
        gN, tmp1, tmp2, sg = view(9 * S, NT, D), view(9 * S, NT, D), view(10 * S, NT, D), view(11 * S, NT, D)
        yN = rN
        KR = view(4 * S, KT, 2, SEQ)
        bT, khT = view(6 * S, KT, SEQ), view(7 * S, KT, SEQ)
        xTs = view(XT, KT, SEQ + 1)
        dT = view(14 * S, KT, SEQ)
        xm = [view(13 * S, KT, SEQ), view(12 * S, KT, SEQ)]
        xn5 = view(13 * S, NT, D)
        lora2_sb = view(8 * S, 2, D)
        lora1_sb = view(9 * S, 2, KT, 64)
        lt = view(10 * S, 2, SEQ)
        WORK = 23040
        MN = view(10 * S, KT, 5, 64)
        M_OF, N_OF = {1: 3, 2: 0}, {0: 1, 1: 4, 2: 2}
        U = [view(WORK + 4864 * b, 4, 5, P) for b in range(2)]
        OFF = [view(WORK + 4864 * b + 2560, 2, 4, P) for b in range(2)]
        XX = [view(WORK + 4864 * b + 3584, 4, P) for b in range(2)]
        BV = [view(WORK + 4864 * b + 4096, 4, 64) for b in range(2)]
        WU = [view(WORK + 4864 * b + 4352, 4, P) for b in range(2)]
        Sg = [None] + [view(WORK + 512 * g, KT, 64) for g in range(3)]
        stmp = view(2 * S, KT, 64)
        xg = view(9 * S, KT, SEQ)
        bonus_v = row[:, 0:2, :]
        bon = little(32).rearrange("p (t h) -> p t h", t=NT)
        pc = little(32).rearrange("p (f g) -> p f g", f=KT)
        nrm = [[little(16).rearrange("p (t h) -> p t h", t=NT) for _ in range(2)] for _ in range(2)]
        mu_y, vr_y, rt_y, rs_y = (little(32).rearrange("p (t h) -> p t h", t=NT) for _ in range(4))
        yo, eN, ge = view(3 * S, NT, D), view(4 * S, NT, D), view(5 * S, NT, D)
        posted = view(6 * S, NT, D)
        pT_sb = view(7 * S, 2, SEQ)
        MIX = [4, 5, 1, 0, 2, 3]

        DVE_AT = {s_: i for i, s_ in enumerate(["x0", "x1", "x2", "x3", 1, 2, 3, 4, 5, 6, 7, 8, 9, 11])}
        ACT_AT = {s_: i for i, s_ in enumerate([2, 3, 4, 6, 8, 10, 11])}
        PE_AT = {s_: i for i, s_ in enumerate(["x0", "x1", "x2", "x3"] + list(range(1, 12)))}

        def core_wait(eng, sems, table, pp, b, step):
            eng.wait_ge(sems[b], pp * len(table) + table[step] + 1)

        kD, vD, qD, gD = (view(i * S, NT, D) for i in (0, 1, 2, 3))
        kDT, qDT, oD, oD2 = view(4 * S, KT, SEQ), view(5 * S, KT, SEQ), view(6 * S, NT, D), view(7 * S, NT, D)
        rt = [view(8 * S + 256 * i, NT, 16, 8) for i in range(4)]
        sd = view(9 * S, 4, 384)
        pt2 = view(8 * S + 1024, 2, 384)
        lamb = view(9 * S + 1536, 4, 64)
        lamp = view(9 * S + 1792, 2, 64)
        lams, lame, nlam = little(2), little(2), little(1)
        LAM0 = 0.8 - 0.6 * float(np.exp(-0.3))
        rd = [little(4).rearrange("p (c t) -> p c t", c=2) for _ in range(2)]
        eye_b = C("eye2")

        def mlp_order():
            yield 1, 0
            for c in range(1, 8):
                yield 1, c
                yield 2, c - 1
            yield 2, 7

        def w1_piece(m, c, f):
            return 4 * ((W_MLP0, W_MLP1)[m] + list(mlp_order()).index((1, c))) + f

        def w2_piece(m, c, f):
            return 4 * ((W_MLP0, W_MLP1)[m] + list(mlp_order()).index((2, c))) + f

        def attention_act(act, split_until):
            for hh in range(HEADS + 1):
                split_until(min(4 * W_O + 1 + hh, 4 * W_O + 8))
                if hh < HEADS:
                    act.wait_ge(mx_ready, hh + 1)
                    buf = sbuf_s[:, hh % 3, :]
                    nc.scalar.activation(buf[:, 0:256], buf[:, 0:256], ACT.Exp, bias=nmx[:, hh, 1:2],
                                         accum_out=sums[:, hh, 1:2])
                    nc.scalar.activation(buf[:, 256:384], buf[:, 256:384], ACT.Exp, bias=nmx[:, hh, 0:1],
                                         accum_out=sums[:, hh, 0:1]).then_inc(exp_done, 1)
                if hh >= 1:
                    g = hh - 1
                    act.wait_ge(pt_filled, g + 1)
                    if g >= 2:
                        act.wait_ge(pv_done, g - 1)
                    nc.scalar.copy(sbuf_pt[:, g % 2, :], psum[:, 6 + g % 2, 0:384]).then_inc(pt_copied, 1)

        def mlp_act(act, m, split_until):
            for c in range(8):
                for b in range(2):
                    split_until(w1_piece(m, c, 2 * b + 1) + 1 + AHEAD)
                    used_piece(act, w1_piece(m, c, 2 * b + 1))
                    if c >= 1:
                        act.wait_ge(z_low, 16 * m + 2 * (c - 1) + b + 1)
                    u = slice(2 * b, 2 * b + 2)
                    nc.scalar.activation(zr[:, u, :], psum[:, 4 + 2 * (c % 2) + b, :], ACT.Relu).then_inc(z_relu, 1)
                    act.wait_ge(z_relu, 16 * m + 2 * c + b + 1)
                    if c >= 2:
                        used_piece(act, w2_piece(m, c - 2, 3))
                    nc.scalar.activation(zh[:, c % 2, u, :], zr[:, u, :], ACT.Square).then_inc(z_high, 1)
            split_until(min(w2_piece(m, 7, 3) + 1 + AHEAD, 4 * W_RKVG))

        def head_outputs(dve, settle, g):
            dve.wait_ge(exp_done, 4 * g + 4)
            settle(nc.vector.reciprocal(rsum[:, 4 * g:4 * g + 4, :], sums[:, 4 * g:4 * g + 4, :]))
            dve.wait_ge(pv_done, 4 * g + 4)
            dst = on[:, :, 4 * g * HD:(4 * g + 4) * HD].rearrange("p t (h d) -> p h t d", d=HD)
            src = psum[:, g, :].rearrange("p (h t d) -> p h t d", t=NT, d=HD)
            nc.vector.tensor_tensor(dst, src, rsum[:, 4 * g:4 * g + 4, :].unsqueeze(3).broadcast_to([P, 4, NT, HD]),
                                    ALU.mult).then_inc(o_ready, 1)

        def mlp_dve(dve, settle, m, i):
            for c in range(8):
                for b in range(2):
                    i_ = 16 * m + 2 * c + b + 1
                    u = slice(2 * b, 2 * b + 2)
                    dve.wait_ge(z_relu, i_)
                    nc.vector.tensor_tensor(zz[:, u, :], zr[:, u, :], zr[:, u, :], ALU.mult).then_inc(zz_ready, 1)
                    dve.wait_ge(zz_ready, i_)
                    dve.wait_ge(z_high, i_)
                    if c >= 2:
                        used_piece(dve, w2_piece(m, c - 2, 3))
                    nc.vector.tensor_tensor(zl[:, c % 2, u, :], zz[:, u, :], read(zh[:, c % 2, u, :]),
                                            ALU.subtract).then_inc(z_low, 1)
            r2 = rstd[:, 2 * i:2 * i + 2]
            settle(nc.vector.tensor_tensor(root[:, 2 * i:2 * i + 2], r2, r2, ALU.mult))
            used_piece(dve, w2_piece(m, 7, 3))
            for t in range(NT):
                for c in range(2):
                    part = h[:, t, c * HALF:(c + 1) * HALF]
                    ins = nc.vector.scalar_tensor_tensor(out=part, in0=psum[:, 2 * t + c, :],
                                                         scalar=root[:, 2 * i + t:2 * i + t + 1], in1=part,
                                                         op0=ALU.mult, op1=ALU.add)
            ins.then_inc(h_ready, 1)

        def mlp_pe(pe, m, inst):
            for kind, c in mlp_order():
                for f in range(4):
                    if kind == 1:
                        if c >= 2 and f % 2 == 0:
                            pe.wait_ge(z_relu, 16 * m + 2 * (c - 2) + f // 2 + 1)
                        pe_feature_tile(pe, w1_piece(m, c, f), psum[:, 4 + 2 * (c % 2) + f // 2, (f % 2) * SEQ:(f % 2 + 1) * SEQ],
                                        transposed(pe, inst) if c == 0 and f == 0 else None)
                    else:
                        n = w2_piece(m, c, f)
                        piece_ready(pe, n)
                        pe.wait_ge(z_low, 16 * m + 2 * c + f // 2 + 1)
                        for t in range(NT):
                            for half in range(2):
                                hf = slice(half * HALF, (half + 1) * HALF)
                                pairs = parts([z[:, c % 2, f, t * P:(t + 1) * P] for z in (zh, zl)], (high(n)[:, hf], low(n)[:, hf]))
                                for q, (a, b) in enumerate(pairs):
                                    ins = nc.tensor.matmul(psum[:, 2 * t + half, :], a, b, start=(c == 0 and f == 0 and q == 0),
                                                           stop=(c == 7 and f == 3 and q == 2))
                        ins.then_inc(piece_used, 1)

        def ODD_EVEN(inst):
            return [0, 2], [1, 3]

        AHEAD = 6

        TF = [(T_KAP, KR[:, :, 0, :]), (T_RH, KR[:, :, 1, :]), (T_BET, bT), (T_KH, khT)]

        block = ctx.enter_context(nc.Block())

        @block.sync
        def _(sp):
            sp.dma_start(h[:, :, :], x.rearrange("(t p) d -> p t d", p=P)).then_inc(x_landed, 16)
            sp.dma_start(con[:, :], consts).then_inc(par_landed, 16)
            sp.dma_start(col[:, :, :], cols).then_inc(par_landed, 16)
            for m in range(4 * W_TILES):
                if m >= RING:
                    used_piece(sp, m - RING)
                sp.dma_start(ring[:, m % RING, :], w[m]).then_inc(piece_landed[m % RING], 16)
                if m == 9:
                    sp.dma_start(spread, bass.AP(relt.tensor, 0, [[0, P], [1, HEADS * 384]])).then_inc(spread_stored, 16)
                if m == 17:
                    sp.wait_ge(spread_stored, 16)
                    sp.dma_start(bias[:, :, 0:256], bass.AP(spread.tensor, 127, [[HEADS * 384 - 1, P], [384, HEADS], [1, 256]])).then_inc(bias_ready, 16)
            sp.wait_ge(h_ready, 9)
            sp.dma_start(out.rearrange("(t p) d -> p t d", p=P), h[:, :, :]).then_inc(out_stored, 16)
            sp.wait_ge(out_stored, 16)

        @block.gpsimd
        def _(pool):
            made = [0]

            def low_until(until):
                for m in range(made[0], until):
                    if m // 4 not in PLAIN:
                        pool.wait_ge(high_made, SPLITS[m] + 1)
                        nc.gpsimd.tensor_tensor(low(m), raw(m), read(high(m)), ALU.subtract).then_inc(low_made, 1)
                made[0] = until

            def load_row(r):
                pool.dma_start(row[:, r % 5, :], bass.AP(rows.tensor, r * D, [[0, P], [1, D]])).then_inc(row_landed[r % 5], 16)

            for r in range(5):
                load_row(r)
            low_until(20)
            pool.wait_ge(bias_ready, 16)
            nc.gpsimd.memset(bias[0:64, :, 192:256], -1e30).then_inc(pool_step, 1)
            pool.wait_ge(pool_step, 1)
            nc.gpsimd.tensor_copy(bias[:, :, 256:384], bias[:, :, 128:256]).then_inc(mask_set, 1)
            low_until(4 * W_RKVG)
            pool.wait_ge(h_ready, 5)
            load_row(5)
            load_row(6)
            pool.dma_start(lora1_sb, lora1).then_inc(lor_landed, 16)
            pool.dma_start(lora2_sb[0:64], lora2).then_inc(lor_landed, 16)
            pool.wait_ge(lora2_read, 2)
            load_row(7)
            load_row(8)
            pool.wait_ge(decays, 3)
            for j in range(2):
                hl = slice(j * HALF, (j + 1) * HALF)
                pool.wait_ge(kk_unit, j + 1)
                nc.gpsimd.tensor_tensor(bet[:, :, hl], kap[:, :, hl], aN[:, :, hl], ALU.mult).then_inc(pool_step, 1)
                pool.wait_ge(pool_step, 2 + 2 * j)
                nc.gpsimd.tensor_tensor(bet[:, :, hl], bet[:, :, hl], Pi[:, :, hl], ALU.mult).then_inc(pool_step, 1)
                pool.wait_ge(pool_step, 3 + 2 * j)
                nc.gpsimd.tensor_tensor(kap[:, :, hl], kap[:, :, hl], Pp[:, :, hl], ALU.mult).then_inc(beta_kap, 1)
                pool.wait_ge(proj_dve, j + 1)
                nc.gpsimd.tensor_tensor(kN[:, :, hl], kN[:, :, hl], Pi[:, :, hl], ALU.mult).then_inc(khat, 1)
            pool.wait_ge(kk_unit, 2)
            load_row(9)
            pool.wait_ge(proj_act, 4)
            pool.wait_ge(bonus, 2)
            nc.gpsimd.tensor_tensor(bonus_v.rearrange("p t (h d) -> p t h d", d=HD), vN.rearrange("p t (h d) -> p t h d", d=HD),
                                    bon.unsqueeze(3).broadcast_to([P, NT, HEADS, HD]), ALU.mult).then_inc(bv_ready, 1)
            for pp in range(4):
                for b in range(2):
                    core_wait(pool, core_dve, DVE_AT, pp, b, "x3")
                    nc.gpsimd.tensor_tensor(U[b][:, :, 0, :], U[b][:, :, 1, :], ident.unsqueeze(1).broadcast_to([P, 4, P]),
                                            ALU.add).then_inc(core_pool[b], 1)
            for q in range(2):
                pool.wait_ge(xg_high, q + 1)
                u = slice(4 * q, 4 * q + 4)
                nc.gpsimd.tensor_tensor(XBL[:, u, :], xg[:, u, :], read(XBH[:, u, :]), ALU.subtract).then_inc(xg_low, 1)
                low_until(4 * W_RKVG + 26 + 6 * q)
            low_until(4 * W_PLE0)
            used(pool, W_RKVG + 7)
            pool.dma_start(pT_sb, pT[:, 0]).then_inc(lor_landed, 16)
            pool.wait_ge(y_ready, 1)
            for r in range(10, 14):
                load_row(r)
            pool.dma_start(lamb, bass.AP(lam.tensor, 0, [[0, P], [64, 4], [1, 64]])).then_inc(lam_landed, 16)
            cosb = C("cos").rearrange("p (t f) -> p t f", t=NT).unsqueeze(2).broadcast_to([P, NT, 16, 8])
            sinb = C("sin").rearrange("p (t f) -> p t f", t=NT).unsqueeze(2).broadcast_to([P, NT, 16, 8])
            n = 5
            for i, (a, count) in enumerate(((kD, 2), (qD, 6))):
                low_until(4 * (W_QG if i == 0 else W_OUT_B))
                pool.wait_ge(kv_act, count)
                pool.wait_ge(kv_dve, count)
                v = a.rearrange("p t (s d) -> p t s d", d=64)
                x1, x2 = v[:, :, :, 0:8], v[:, :, :, 8:16]
                for d, s0, s1 in ((0, x1, cosb), (1, x2, sinb), (2, x2, cosb), (3, x1, sinb)):
                    ins = nc.gpsimd.tensor_tensor(rt[d], s0, s1, ALU.mult)
                ins.then_inc(pool_step, 1)
                n += 1
                pool.wait_ge(pool_step, n)
                nc.gpsimd.tensor_tensor(x1, rt[0], rt[1], ALU.subtract)
                nc.gpsimd.tensor_tensor(x2, rt[2], rt[3], ALU.add).then_inc(roped, 1)
                pool.wait_ge(roped, i + 1)
            low_until(4 * W_PLE1)
            pool.wait_ge(od_ready, 1)
            pool.dma_start(pT_sb, pT[:, 1]).then_inc(lor_landed, 16)
            low_until(4 * W_TILES)

        @block.scalar
        def _(act):
            engines["act"] = act
            steps = [0]

            def settle(ins):
                steps[0] += 1
                ins.then_inc(act_step, 1)
                act.wait_ge(act_step, steps[0])

            def moments(i, src=h):
                for t in range(NT):
                    ins = nc.scalar.activation(junk_at(i)[:, t, :], src[:, t, :], ACT.Square, accum_out=ss[:, 2 * i + t:2 * i + t + 1])
                ins.then_inc(stat_sum, 1)
                act.wait_ge(stat_var, i + 1)
                nc.scalar.activation(root[:, 2 * i:2 * i + 2], var[:, 2 * i:2 * i + 2], ACT.Sqrt).then_inc(stat_root, 1)

            made = [0]
            LAST = 4 * W_TILES

            def split_until(until):
                for m in range(made[0], min(until, LAST)):
                    if m // 4 not in PLAIN:
                        act.wait_ge(piece_landed[m % RING], 16 * (m // RING + 1))
                        if m >= RING:
                            used_piece(act, m - RING)
                        nc.scalar.copy(high(m), raw(m)).then_inc(high_made, 1)
                made[0] = max(made[0], until)

            def split_for(n):
                split_until(4 * n + 4 + AHEAD)

            act.wait_ge(x_landed, 16)
            act.wait_ge(par_landed, 32)
            evacuate_high(act, T_H0, (XH, c8("norm_mix0")))
            split_until(4)
            moments(0)
            for c, (dst, half) in enumerate(QKV):
                split_for(W_QKV + c)
                used(act, W_QKV + c)
                act.wait_ge(rstd_ready, 1)
                nc.scalar.activation(dst[:, 0, half * HALF:(half + 1) * HALF], psum[:, 2 * (c % 2), :], ACT.Copy,
                                     scale=rstd[:, 0:1]).then_inc(qkv_act, 1)
            for inst, dst in ((T_Q, qT), (T_K, kT)):
                for b in (0, 2):
                    evacuate(act, inst, b, dst)
            attention_act(act, split_until)
            evacuate_high(act, T_O, (XH, None))
            split_for(W_O + 1)
            act.wait_ge(h_ready, 1)
            evacuate_high(act, T_H1, (XH, c8("norm_mlp0")))
            moments(1)
            act.wait_ge(decay_part, 1)
            nc.scalar.activation(spt[1], spt[0], ACT.Exp, scale=-1.0).then_inc(decay_part, 1)
            act.wait_ge(decay_part, 3)
            nc.scalar.activation(spt[3], spt[2], ACT.Ln).then_inc(decay_part, 1)
            mlp_act(act, 0, split_until)

            act.wait_ge(h_ready, 2)
            moments(2)
            evacuate_high(act, T_N2, (XH, c8("norm_mix1")))
            split_until(4 * W_INY + 4)
            for i in range(4):
                used_piece(act, 4 * W_GATES + i)
                for j in range(2):
                    f = 2 * i + j
                    nc.scalar.activation(rg[:, f, :], psum[:, 4 + i % 2, j * SEQ:(j + 1) * SEQ], ACT.Sigmoid,
                                         bias=c8("b_ga")[:, f:f + 1])
                    ins = nc.scalar.activation(ig[:, f, :], psum[:, 6 + i % 2, j * SEQ:(j + 1) * SEQ], ACT.Sigmoid,
                                               bias=c8("b_gx")[:, f:f + 1])
                ins.then_inc(gates_read, 1)
                split_until(4 * W_INY + 5 + i)
            act.wait_ge(gates_read, 4)
            act.wait_ge(decay_ready, 1)
            for q in range(2):
                u = slice(4 * q, 4 * q + 4)
                for f in range(4 * q, 4 * q + 4):
                    nc.scalar.activation(aa[:, f, :], rg[:, f, :], ACT.Exp, scale=nsp8[:, f:f + 1])
                for f in range(4 * q, 4 * q + 4):
                    ins = nc.scalar.activation(th[:, f, :], rg[:, f, :], ACT.Tanh, scale=sp8[:, f:f + 1])
                settle(ins)
                nc.scalar.activation(bb_[:, u, :], aa[:, u, :], ACT.Square).then_inc(g_ready, 1)
            for q in range(2):
                act.wait_ge(m2_ready, q + 1)
                nc.scalar.activation(th[:, 4 * q:4 * q + 4, :], th[:, 4 * q:4 * q + 4, :], ACT.Sqrt).then_inc(m_ready, 1)
            for i in range(4):
                split_until(4 * W_RO + 2 * i)
                used_piece(act, 4 * W_INY + 2 * i + 1)
                for j in range(2):
                    f = 2 * i + j
                    ins = nc.scalar.activation(yg[:, f, :], psum[:, i, j * SEQ:(j + 1) * SEQ], ACT.Gelu_apprx_tanh,
                                               bias=c8("b_in_y")[:, f:f + 1])
                ins.then_inc(y_read, 1)
            for q in range(2):
                act.wait_ge(o_ready, 5 + q)
                u = slice(4 * q, 4 * q + 4)
                nc.scalar.copy(xT2[0][:, u, :], og[:, u, :]).then_inc(og_high, 1)
                split_until(4 * W_RO + 8)
            split_for(W_RO + 1)
            act.wait_ge(h_ready, 3)
            evacuate_high(act, T_H3, (XH, c8("norm_mlp1")))
            moments(3)
            mlp_act(act, 1, split_until)
            act.wait_ge(h_ready, 4)
            moments(4)

            act.wait_ge(h_ready, 5)
            moments(5)
            for b in ODD_EVEN(T_N5)[0]:
                evacuate(act, T_N5, b, xTs[:, :, 1:SEQ + 1], c8("norm_pre0"))
            act.wait_ge(lora_filled, 1)
            nc.scalar.activation(lt[0:64, 0, :], psum[0:64, 4, 0:SEQ], ACT.Tanh).then_inc(lora_out, 1)
            act.wait_ge(lora_filled, 2)
            nc.scalar.copy(lt[0:64, 1, :], psum[0:64, 5, 0:SEQ]).then_inc(lora_out, 1)
            act.wait_ge(lora2_read, 1)
            nc.scalar.activation(sg, sg, ACT.Sigmoid).then_inc(sig_ready, 1)
            act.wait_ge(lora2_read, 2)
            nc.scalar.activation(aN, aN, ACT.Sigmoid).then_inc(sig_ready, 1)
            act.wait_ge(cum_prev, 1)
            cum = psum[:, 0:4, :].rearrange("p (t q) n -> p t (q n)", t=NT)
            CD = float(np.exp(-0.5))
            nc.scalar.activation(Pd, cum, ACT.Exp, scale=-CD).then_inc(decays, 1)
            nc.scalar.activation(Pi, cum, ACT.Exp, scale=CD).then_inc(decays, 1)
            nc.scalar.activation(Pp, Pp, ACT.Exp, scale=-CD).then_inc(decays, 1)

            def pair_out(c):
                return psum[:, 2 * (c % 2):2 * (c % 2) + 2, :]

            for j in range(2):
                used(act, W_RKVG + j)
                nc.scalar.copy(kN[:, :, j * HALF:(j + 1) * HALF], pair_out(j)).then_inc(proj_act, 1)
            act.wait_ge(last_filled, 1)
            nc.scalar.copy(pc.rearrange("p f g -> p (f g)"), psum[:, 4, 0:32]).then_inc(last_read, 1)
            for j in range(2):
                hl = slice(j * HALF, (j + 1) * HALF)
                act.wait_ge(kk_raw, j + 1)
                nc.scalar.activation(tmp1[:, :, hl], kap[:, :, hl], ACT.Square).then_inc(kk_sq, 1)
                act.wait_ge(kk_var, j + 1)
                nc.scalar.activation(nrm[j][1], nrm[j][0], ACT.Sqrt).then_inc(kk_root, 1)
            for j in range(2):
                used(act, W_RKVG + 4 + j)
                nc.scalar.copy(vN[:, :, j * HALF:(j + 1) * HALF], pair_out(j)).then_inc(proj_act, 1)
            for inst, dst in TF:
                for b in ODD_EVEN(inst)[0]:
                    evacuate(act, inst, b, dst)
            for pp in range(4):
                for s_ in (2, 3, 4, 6, 8, 10, 11):
                    for b in range(2):
                        f, B = 2 * pp + b, 4 * b
                        core_wait(act, core_filled, PE_AT, pp, b, s_)
                        four = lambda k: psum[:, B + k, :].rearrange("p (q n) -> p q n", q=4)
                        if s_ == 2:
                            act.wait_ge(core_pool[b], pp + 1)
                            nc.scalar.copy(U[b][:, :, 1, :], four(1))
                            ins = nc.scalar.copy(BV[b], psum[:, B + 3, 0:256].rearrange("p (q n) -> p q n", q=4))
                        elif s_ == 3:
                            nc.scalar.copy(U[b][:, :, 1, :], four(1))
                            ins = nc.scalar.copy(XX[b], four(2))
                        elif s_ == 4:
                            ins = nc.scalar.copy(XX[b], four(2))
                        elif s_ in (6, 8):
                            ins = nc.scalar.copy(XX[b], four(1))
                        elif s_ == 10:
                            ins = nc.scalar.activation(WU[b], four(1), ACT.Copy, scale=-1.0)
                        else:
                            nc.scalar.copy(MN[:, f, 0:3, :].rearrange("p g i -> p (g i)"), psum[:, B + 2, 0:192])
                            nc.scalar.copy(MN[:, f, 3:5, :].rearrange("p g i -> p (g i)"), psum[:, B + 3, 0:128])
                            dst = yN[:, :, 2 * f * HD:(2 * f + 2) * HD].rearrange("p t (h d) -> p h t d", d=HD)
                            ins = nc.scalar.copy(dst, psum[:, B, 0:256].rearrange("p (h t d) -> p h t d", h=2, t=NT))
                        ins.then_inc(core_act[b], 1)
            core_wait(act, core_filled, PE_AT, 3, 0, 11)
            core_wait(act, core_filled, PE_AT, 3, 1, 11)
            for q in range(2):
                u = slice(4 * q, 4 * q + 4)
                nc.scalar.copy(XBH[:, u, :], xg[:, u, :]).then_inc(xg_high, 1)
                split_until(4 * W_RKVG + 26 + 6 * q)
            act.wait_ge(y_cent, 1)
            nc.scalar.activation(bet, yN, ACT.Square).then_inc(y_sq, 1)
            act.wait_ge(y_var, 1)
            nc.scalar.activation(rt_y, vr_y, ACT.Sqrt).then_inc(y_root, 1)
            for j in range(2):
                split_for(W_RKVG + 6 + j)
                used(act, W_RKVG + 6 + j)
                nc.scalar.activation(gN[:, :, j * HALF:(j + 1) * HALF], pair_out(j), ACT.Silu).then_inc(proj_act, 1)

            def out_norm(i, first, e_n, T, ready):
                for c in range(2):
                    split_for(first + c)
                    used(act, first + c)
                    nc.scalar.copy(yo[:, :, c * HALF:(c + 1) * HALF], pair_out(c)).then_inc(yo_act, 1)
                act.wait_ge(yo_act, 2 * e_n + 2)
                moments(i, yo)

            def embed(i, tile, e_n, T):
                split_for(tile)
                used(act, tile)
                for c in range(2):
                    ins = nc.scalar.copy(eN[:, :, c * HALF:(c + 1) * HALF], pair_out(c))
                ins.then_inc(e_act, 1)
                evacuate_high(act, T, (XH, None))
                for c in range(2):
                    split_for(tile + 1 + c)
                    used(act, tile + 1 + c)
                    nc.scalar.activation(ge[:, :, c * HALF:(c + 1) * HALF], pair_out(c), ACT.Sigmoid).then_inc(gate_act, 1)
                act.wait_ge(ge_ready, 2 * e_n + 2)
                moments(i, ge)

            evacuate_high(act, T_YA, (XH, None))
            out_norm(6, W_OUT_A, 0, None, None)
            embed(7, W_PLE0, 0, T_H6)

            act.wait_ge(h_ready, 7)
            evacuate_high(act, T_H7, (XBH, c8("kv_norm")), (XH, c8("norm_pre1")))
            moments(8)
            act.wait_ge(lam_sum, 1)
            nc.scalar.activation(lame, lams, ACT.Exp).then_inc(lam_exp, 1)
            act.wait_ge(rstd_ready, 9)
            for c, dst in enumerate((kD, vD, qD, gD)):
                for j in range(2):
                    split_for(W_KV + 2 * c + j)
                    used(act, W_KV + 2 * c + j)
                    hl = slice(j * HALF, (j + 1) * HALF)
                    if c < 3:
                        ins = nc.scalar.activation(dst[:, 0, hl], pair_out(j)[:, 0], ACT.Copy, scale=rstd[:, 16:17])
                    else:
                        for t in range(NT):
                            ins = nc.scalar.activation(dst[:, t, hl], pair_out(j)[:, t], ACT.Silu,
                                                       scale=rstd[:, 16 + t:17 + t])
                    ins.then_inc(kv_act, 1)
            for inst, dst in ((T_KB, kDT), (T_QB, qDT)):
                for b in ODD_EVEN(inst)[0]:
                    evacuate(act, inst, b, dst)
            for hh in range(HEADS + 2):
                split_until(min(4 * W_OUT_B + 6 + hh, 4 * W_OUT_B + 8))
                if hh < HEADS:
                    act.wait_ge(mx_ready, HEADS + hh + 1)
                    buf = sd[:, hh % 4, :]
                    nc.scalar.activation(buf[:, 0:256], buf[:, 0:256], ACT.Exp, bias=nmx[:, hh, 1:2],
                                         accum_out=sums[:, hh, 1:2])
                    nc.scalar.activation(buf[:, 256:384], buf[:, 256:384], ACT.Exp, bias=nmx[:, hh, 0:1],
                                         accum_out=sums[:, hh, 0:1]).then_inc(exp_done, 1)
                if hh >= 3 and hh % 2 == 1:
                    g = (hh - 3) // 2
                    act.wait_ge(pt_filled, HEADS + g + 1)
                    if g >= 2:
                        act.wait_ge(pv_done, HEADS + g - 1)
                    nc.scalar.copy(pt2[:, g % 2, :], psum[:, 6 + g % 2, 0:384]).then_inc(pt_copied, 1)
            for g in range(2):
                act.wait_ge(pv_done, HEADS + 4 * g + 4)
                dst = oD[:, :, g * HALF:(g + 1) * HALF].rearrange("p t (h d) -> p h t d", d=P)
                src = psum[:, 2 * g:2 * g + 2, :].rearrange("p b (h t d) -> p (b h) t d", h=2, t=NT)
                ins = nc.scalar.copy(dst, src)
            settle(ins)
            nc.scalar.activation(oD2, oD, ACT.Square).then_inc(o_sq, 1)
            act.wait_ge(o_var, 1)
            nc.scalar.activation(rt_y[:, :, 0:8], vr_y[:, :, 0:8], ACT.Sqrt).then_inc(o_root, 1)
            evacuate_high(act, T_OB, (XH, None))
            out_norm(9, W_OUT_B, 1, None, None)
            embed(10, W_PLE1, 1, T_H8)

        @block.vector
        def _(dve):
            engines["dve"] = dve
            steps = [0]

            def settle(ins):
                steps[0] += 1
                ins.then_inc(dve_step, 1)
                dve.wait_ge(dve_step, steps[0])

            def rms(i, n=D, eps=EPS):
                dve.wait_ge(stat_sum, i + 1)
                nc.vector.tensor_scalar(var[:, 2 * i:2 * i + 2], ss[:, 2 * i:2 * i + 2], 1.0 / n, eps, ALU.mult,
                                        ALU.add).then_inc(stat_var, 1)
                dve.wait_ge(stat_root, i + 1)
                nc.vector.reciprocal(rstd[:, 2 * i:2 * i + 2], root[:, 2 * i:2 * i + 2]).then_inc(rstd_ready, 1)
                dve.wait_ge(rstd_ready, i + 1)

            def residual(first, chunks=2):
                for c in range(chunks):
                    used(dve, first + c)
                    for t in range(NT):
                        part = h[:, t, c * HALF:(c + 1) * HALF]
                        ins = nc.vector.tensor_tensor(part, psum[:, 2 * (c % 2) + t, :], part, ALU.add)
                ins.then_inc(h_ready, 1)

            dve.wait_ge(par_landed, 32)
            evacuate_low(dve, T_H0, (XH, XL, c8("norm_mix0")))
            rms(0)
            for c, (dst, half) in enumerate(QKV):
                used(dve, W_QKV + c)
                nc.vector.tensor_scalar(dst[:, 1, half * HALF:(half + 1) * HALF], psum[:, 2 * (c % 2) + 1, :],
                                        rstd[:, 1:2], None, ALU.mult).then_inc(qkv_dve, 1)
            for inst, dst in ((T_Q, qT), (T_K, kT)):
                for b in (1, 3):
                    evacuate(dve, inst, b, dst)
            dve.wait_ge(mask_set, 1)
            for hh in range(HEADS + 3):
                if hh < HEADS:
                    dve.wait_ge(sc_done, hh + 1)
                    if hh >= 3:
                        dve.wait_ge(pt_filled, hh - 2)
                    buf = sbuf_s[:, hh % 3, :]
                    nc.vector.scalar_tensor_tensor(out=buf, in0=psum[:, 4 + hh % 2, 0:384], scalar=HD ** -0.5,
                                                   in1=bias[:, hh, :], op0=ALU.mult, op1=ALU.add).then_inc(sc_read, 1)
                    dve.wait_ge(sc_read, hh + 1)
                    nc.vector.tensor_reduce(nmx[:, hh, 1:2], buf[:, 0:256], AX.X, ALU.max, negate=True)
                    nc.vector.tensor_reduce(nmx[:, hh, 0:1], buf[:, 256:384], AX.X, ALU.max, negate=True).then_inc(mx_ready, 1)
                if hh >= 6 and hh % 4 == 2:
                    head_outputs(dve, settle, (hh - 6) // 4)
            evacuate_low(dve, T_O, (XH, XL, None))
            residual(W_O)
            evacuate_low(dve, T_H1, (XH, XL, c8("norm_mlp0")))
            rms(1)
            p_ = c8("a_param")
            settle(nc.vector.tensor_scalar(spt[1], p_, -1.0, None, ALU.mult))
            nc.vector.tensor_tensor(spt[0], p_, spt[1], ALU.max).then_inc(decay_part, 1)
            dve.wait_ge(decay_part, 2)
            nc.vector.tensor_scalar(spt[2], spt[1], 1.0, None, ALU.add).then_inc(decay_part, 1)
            dve.wait_ge(decay_part, 4)
            settle(nc.vector.tensor_scalar(spt[2], spt[2], -1.0, None, ALU.add))
            settle(nc.vector.tensor_scalar(spt[4], spt[2], 0.0, None, ALU.is_equal))
            settle(nc.vector.tensor_tensor(spt[2], spt[2], spt[4], ALU.add))
            settle(nc.vector.reciprocal(spt[2], spt[2]))
            settle(nc.vector.tensor_tensor(spt[3], spt[3], spt[2], ALU.mult))
            settle(nc.vector.tensor_tensor(spt[3], spt[3], spt[4], ALU.add))
            settle(nc.vector.tensor_tensor(spt[3], spt[3], spt[1], ALU.mult))
            settle(nc.vector.tensor_scalar(spt[4], p_, -1.0, 0.0, ALU.mult, ALU.max))
            settle(nc.vector.tensor_tensor(spt[3], spt[3], spt[4], ALU.add))
            nc.vector.tensor_scalar(sp8, spt[3], 8.0, None, ALU.mult)
            nc.vector.tensor_scalar(nsp8, spt[3], -8.0, None, ALU.mult).then_inc(decay_ready, 1)
            mlp_dve(dve, settle, 0, 1)

            def normed(dst, i):
                for t in range(NT):
                    ins = nc.vector.tensor_scalar(dst[:, t, :], h[:, t, :], rstd[:, 2 * i + t:2 * i + t + 1], None, ALU.mult)
                ins.then_inc(xn_ready, 1)

            def row_of(name):
                r = ROWS.index(name)
                dve.wait_ge(row_landed[r % 5], 16 * (r // 5 + 1))
                return row[:, r % 5, :]

            rms(2)
            normed(xn, 2)
            nc.vector.memset(xb[:, :, 0:3], 0.0).then_inc(pad_zero, 1)
            bo = row_of("b_o")
            dve.wait_ge(xn_ready, 1)
            for t in range(NT):
                settle(nc.vector.tensor_tensor(h[:, t, :], h[:, t, :], bo, ALU.add))
            evacuate_low(dve, T_N2, (XH, XL, c8("norm_mix1")))
            dve.wait_ge(pad_zero, 1)
            for i in range(4):
                used_piece(dve, 4 * W_INX + 2 * i + 1)
                for j in range(2):
                    f = 2 * i + j
                    ins = nc.vector.tensor_scalar(xb[:, f, 3:], psum[:, i, j * SEQ:(j + 1) * SEQ],
                                                  c8("b_in_x")[:, f:f + 1], None, ALU.add)
                ins.then_inc(x_read, 1)
                dve.wait_ge(x_read, i + 1)
                for tap in range(4):
                    wc = c8(f"conv_w{tap}")
                    for j in range(2):
                        f = 2 * i + j
                        src, o = xb[:, f, tap:tap + SEQ], xc[:, f, :]
                        if tap == 0:
                            ins = nc.vector.tensor_scalar(o, src, wc[:, f:f + 1], c8("conv_b")[:, f:f + 1], ALU.mult, ALU.add)
                        else:
                            ins = nc.vector.scalar_tensor_tensor(out=o, in0=src, scalar=wc[:, f:f + 1], in1=o,
                                                                 op0=ALU.mult, op1=ALU.add)
                    if tap < 3:
                        settle(ins)
                ins.then_inc(xc_ready, 1)

            def og_low_part(q):
                u = slice(4 * q, 4 * q + 4)
                dve.wait_ge(og_high, q + 1)
                nc.vector.tensor_tensor(xT2[1][:, u, :], og[:, u, :], read(xT2[0][:, u, :]), ALU.subtract).then_inc(og_low, 1)

            dve.wait_ge(xc_ready, 4)
            dve.wait_ge(gates_read, 4)
            for q in range(2):
                u = slice(4 * q, 4 * q + 4)
                nc.vector.tensor_tensor(ig[:, u, :], ig[:, u, :], xc[:, u, :], ALU.mult)
                dve.wait_ge(g_ready, q + 1)
                nc.vector.scalar_tensor_tensor(out=th[:, u, :], in0=bb_[:, u, :], scalar=1.0, in1=th[:, u, :],
                                               op0=ALU.add, op1=ALU.mult).then_inc(m2_ready, 1)
            for q in range(2):
                u = slice(4 * q, 4 * q + 4)
                dve.wait_ge(m_ready, q + 1)
                if q == 1:
                    og_low_part(0)
                settle(nc.vector.tensor_tensor(bb_[:, u, :], th[:, u, :], ig[:, u, :], ALU.mult))
                for f in range(4 * q, 4 * q + 4):
                    ins = nc.vector.tensor_tensor_scan(hs[:, f, :], aa[:, f, :], bb_[:, f, :], 0.0, ALU.mult, ALU.add)
                settle(ins)
                dve.wait_ge(y_read, 2 * q + 2)
                nc.vector.tensor_tensor(og[:, u, :], hs[:, u, :], yg[:, u, :], ALU.mult).then_inc(o_ready, 1)
            og_low_part(1)
            residual(W_RO)
            evacuate_low(dve, T_H3, (XH, XL, c8("norm_mlp1")))
            rms(3)
            mlp_dve(dve, settle, 1, 3)
            rms(4)
            nf = row_of("norm_final")
            for t in range(NT):
                ins = nc.vector.scalar_tensor_tensor(out=h[:, t, :], in0=h[:, t, :], scalar=rstd[:, 8 + t:9 + t], in1=nf,
                                                     op0=ALU.mult, op1=ALU.mult)
            ins.then_inc(h_ready, 1)
            dve.wait_ge(h_ready, 5)

            rms(5)
            normed(xn5, 5)
            nc.vector.memset(xTs[:, :, 0:1], 0.0)
            for b in ODD_EVEN(T_N5)[1]:
                evacuate(dve, T_N5, b, xTs[:, :, 1:SEQ + 1], c8("norm_pre0"))
            evacuated(dve, T_N5)
            settle(nc.vector.tensor_tensor(dT, xTs[:, :, 0:SEQ], xTs[:, :, 1:SEQ + 1], ALU.subtract))

            def mix(i):
                if i in (2, 3):
                    dve.wait_ge(lora_filled, i - 1)
                if i == 4:
                    used(dve, W_RKVG + 1)
                if i == 5:
                    dve.wait_ge(bonus, 2)
                dst = xg if i == 5 else xm[i % 2]
                for k in range(KT):
                    ins = nc.vector.scalar_tensor_tensor(out=dst[:, k, :], in0=dT[:, k, :],
                                                         scalar=c8(f"mu{MIX[i]}")[:, k:k + 1],
                                                         in1=xTs[:, k, 1:SEQ + 1], op0=ALU.mult, op1=ALU.add)
                ins.then_inc(mix_ready, 1)

            mix(0)
            mix(1)
            four_banks = psum[:, 0:4, :].rearrange("p (t q) n -> p t (q n)", t=NT)
            for i, (dst, name) in enumerate(((sg, "w0"), (aN, "a0"))):
                r_ = row_of(name)
                dve.wait_ge(lora2_filled, i + 1)
                nc.vector.tensor_tensor(dst, four_banks, r_.unsqueeze(1).broadcast_to([P, NT, D]), ALU.add).then_inc(lora2_read, 1)
                mix(2 + i)
            dve.wait_ge(cum_filled, 1)
            nc.vector.tensor_tensor(Pp, four_banks, sg, ALU.subtract).then_inc(cum_prev, 1)
            for j in range(2):
                hl = slice(j * HALF, (j + 1) * HALF)
                over = lambda r_: r_[:, hl].unsqueeze(1).broadcast_to([P, NT, HALF])
                heads = lambda a: a[:, :, hl].rearrange("p t (h d) -> p t h d", d=HD)
                per_head = lambda a: a.unsqueeze(3).broadcast_to([P, NT, 8, HD])
                dve.wait_ge(proj_act, j + 1)
                nc.vector.tensor_tensor(kap[:, :, hl], kN[:, :, hl], over(row_of("k_k")), ALU.mult).then_inc(kk_raw, 1)
                dve.wait_ge(sig_ready, 2)
                for t in range(NT):
                    ins = nc.vector.scalar_tensor_tensor(out=tmp2[:, t, hl], in0=aN[:, t, hl], scalar=1.0,
                                                         in1=row_of("k_a")[:, hl], op0=ALU.subtract, op1=ALU.mult)
                settle(ins)
                nc.vector.scalar_tensor_tensor(out=kN[:, :, hl], in0=tmp2[:, :, hl], scalar=1.0, in1=kN[:, :, hl],
                                               op0=ALU.add, op1=ALU.mult).then_inc(k_ready, 1)
                dve.wait_ge(kk_sq, j + 1)
                settle(nc.vector.tensor_reduce(nrm[j][0], heads(tmp1), AX.X, ALU.add))
                nc.vector.tensor_scalar(nrm[j][0], nrm[j][0], 1e-24, None, ALU.max).then_inc(kk_var, 1)
                dve.wait_ge(kk_root, j + 1)
                settle(nc.vector.reciprocal(nrm[j][1], nrm[j][1]))
                dve.wait_ge(kk_raw, j + 1)
                nc.vector.tensor_tensor(heads(kap), heads(kap), per_head(nrm[j][1]), ALU.mult).then_inc(kk_unit, 1)
                if j == 0:
                    mix(4)
            for j in range(2):
                hl = slice(j * HALF, (j + 1) * HALF)
                heads = lambda a: a[:, :, hl].rearrange("p t (h d) -> p t h d", d=HD)
                used(dve, W_RKVG + 2 + j)
                pr = psum[:, 2 * j:2 * j + 2, :]
                dve.wait_ge(decays, 3)
                dve.wait_ge(k_ready, j + 1)
                nc.vector.tensor_tensor(rN[:, :, hl], pr, Pd[:, :, hl], ALU.mult)
                nc.vector.tensor_tensor(tmp1[:, :, hl], pr, kN[:, :, hl], ALU.mult).then_inc(proj_dve, 1)
                dve.wait_ge(proj_dve, j + 1)
                settle(nc.vector.tensor_tensor(tmp1[:, :, hl], tmp1[:, :, hl],
                                               row_of("r_k")[:, hl].unsqueeze(1).broadcast_to([P, NT, HALF]), ALU.mult))
                nc.vector.tensor_reduce(bon[:, :, 8 * j:8 * j + 8], heads(tmp1), AX.X, ALU.add).then_inc(bonus, 1)
            mix(5)
            for inst, dst in TF:
                for b in ODD_EVEN(inst)[1]:
                    evacuate(dve, inst, b, dst)

            for pp in range(4):
                for s_ in ("x0", "x1", "x2", "x3", 1, 2, 3, 4, 5, 6, 7, 8, 9, 11):
                    for b in range(2):
                        f, B = 2 * pp + b, 4 * b
                        core_wait(dve, core_filled, PE_AT, pp, b, s_)
                        four = lambda k: psum[:, B + k, :].rearrange("p (q n) -> p q n", q=4)
                        Z = U[b][:, :, 0, :]
                        if isinstance(s_, str):
                            q = int(s_[1])
                            ins = nc.vector.tensor_tensor(U[b][:, q, 1:5, :].rearrange("p a n -> p (a n)"), psum[:, B + q, :],
                                                          C("mask_x"), ALU.mult)
                        elif s_ == 1:
                            src = psum[:, B:B + 2, 0:256].rearrange("p h (t n) -> p h t n", t=2)
                            for m, dst in enumerate((XX[b], OFF[b][:, 0], OFF[b][:, 1])):
                                mk = C("mask_a")[:, m * P:(m + 1) * P].unsqueeze(1).unsqueeze(1).broadcast_to([P, 2, 2, P])
                                ins = nc.vector.tensor_tensor(dst.rearrange("p (h t) n -> p h t n", h=2), src, mk, ALU.mult)
                        elif s_ == 2:
                            ins = nc.vector.tensor_copy(XX[b], four(2))
                        elif s_ == 3:
                            dve.wait_ge(core_pool[b], pp + 1)
                            ins = nc.vector.tensor_tensor(Z, four(0), Z, ALU.add)
                        elif s_ == 4:
                            ins = nc.vector.tensor_tensor(Z, four(3), Z, ALU.add)
                        elif s_ == 5:
                            ins = nc.vector.tensor_tensor(Z, four(0), Z, ALU.add)
                        elif s_ in (6, 8):
                            ins = nc.vector.tensor_copy(U[b][:, :, 1, :], four(2))
                        elif s_ in (7, 9):
                            ins = nc.vector.tensor_tensor(Z, Z, four(0), ALU.subtract)
                        else:
                            ins = nc.vector.tensor_tensor(KR[:, f, 1, :], psum[:, B + 1, 0:256], KR[:, f, 1, :], ALU.add)
                        ins.then_inc(core_dve[b], 1)
            for b in range(2):
                core_wait(dve, core_act, ACT_AT, 3, b, 11)
                core_wait(dve, core_dve, DVE_AT, 3, b, 11)
            dve.wait_ge(last_read, 1)
            pcg = lambda g: pc[:, :, g:g + 1].broadcast_to([P, KT, 64])
            nc.vector.tensor_tensor(Sg[1], MN[:, :, N_OF[0], :], pcg(0), ALU.mult).then_inc(state_ready, 1)
            for g in (1, 2):
                dve.wait_ge(state_filled, g)
                for p0 in (0, HD):
                    hp = slice(p0, p0 + HD)
                    src = psum[hp, 4 + 2 * (g - 1) + p0 // HD, :].rearrange("p (f n) -> p f n", f=KT)
                    ins = nc.vector.tensor_tensor(stmp[hp], src, MN[hp, :, N_OF[g], :], ALU.add)
                settle(ins)
                nc.vector.tensor_tensor(Sg[g + 1], stmp, pcg(g), ALU.mult).then_inc(state_ready, 1)
            dve.wait_ge(ys_filled, 1)
            for par in range(2):
                for t, r_ in ((0, slice(64, P)), (1, slice(0, P))):
                    part = yN[r_, t, :].rearrange("p (f c d) -> p f c d", c=2, d=HD)[:, :, par]
                    ins = nc.vector.tensor_tensor(part, part, psum[r_, 4 + 2 * t + par, :].rearrange("p (f d) -> p f d", f=KT), ALU.add)
            settle(ins)
            yh = yN.rearrange("p t (h d) -> p t h d", d=HD)
            ph = lambda a: a.unsqueeze(3).broadcast_to([P, NT, HEADS, HD])
            settle(nc.vector.tensor_reduce(mu_y, yh, AX.X, ALU.add))
            settle(nc.vector.tensor_scalar(mu_y, mu_y, 1.0 / HD, None, ALU.mult))
            nc.vector.tensor_tensor(yh, yh, ph(mu_y), ALU.subtract).then_inc(y_cent, 1)
            dve.wait_ge(y_sq, 1)
            settle(nc.vector.tensor_reduce(vr_y, bet.rearrange("p t (h d) -> p t h d", d=HD), AX.X, ALU.add))
            nc.vector.tensor_scalar(vr_y, vr_y, 1.0 / HD, 64e-5, ALU.mult, ALU.add).then_inc(y_var, 1)
            dve.wait_ge(y_root, 1)
            settle(nc.vector.reciprocal(rs_y, rt_y))
            settle(nc.vector.tensor_tensor(yh, yh, ph(rs_y), ALU.mult))
            both = lambda r_: r_.unsqueeze(1).broadcast_to([P, NT, D])
            settle(nc.vector.tensor_tensor(yN, yN, both(row_of("lnx_g")), ALU.mult))
            settle(nc.vector.tensor_tensor(yN, yN, both(row_of("lnx_b")), ALU.add))
            dve.wait_ge(bv_ready, 1)
            settle(nc.vector.tensor_tensor(yN, yN, bonus_v, ALU.add))
            dve.wait_ge(proj_act, 6)
            nc.vector.tensor_tensor(yN, yN, gN, ALU.mult).then_inc(y_ready, 1)

            def add_normed(i, src, name):
                rms(i)
                g_ = row_of(name)
                for t in range(NT):
                    ins = nc.vector.scalar_tensor_tensor(out=posted[:, t, :], in0=src[:, t, :],
                                                         scalar=rstd[:, 2 * i + t:2 * i + t + 1], in1=g_,
                                                         op0=ALU.mult, op1=ALU.mult)
                settle(ins)
                nc.vector.tensor_tensor(h[:, :, :], h[:, :, :], posted, ALU.add).then_inc(h_ready, 1)

            def embed_dve(i, e_n, T, name):
                evacuate_low(dve, T, (XH, XL, None))
                dve.wait_ge(e_act, e_n + 1)
                for c in range(2):
                    dve.wait_ge(gate_act, 2 * e_n + c + 1)
                    hl = slice(c * HALF, (c + 1) * HALF)
                    nc.vector.tensor_tensor(ge[:, :, hl], ge[:, :, hl], eN[:, :, hl], ALU.mult).then_inc(ge_ready, 1)
                add_normed(i, ge, name)

            evacuate_low(dve, T_YA, (XH, XL, None))
            add_normed(6, yo, "norm_post0")
            dve.wait_ge(h_ready, 6)
            embed_dve(7, 0, T_H6, "ple_norm0")
            dve.wait_ge(h_ready, 7)

            evacuate_low(dve, T_H7, (XBH, XBL, c8("kv_norm")), (XH, XL, c8("norm_pre1")))
            dve.wait_ge(lam_landed, 16)
            lv = lamb.rearrange("p (a b) d -> p a b d", b=2)
            settle(nc.vector.tensor_tensor(lamp, lv[:, :, 0, :], lv[:, :, 1, :], ALU.mult))
            nc.vector.tensor_reduce(lams, lamp, AX.X, ALU.add).then_inc(lam_sum, 1)
            rms(8)
            dve.wait_ge(lam_exp, 1)
            settle(nc.vector.tensor_tensor(nlam, lame[:, 1:2], lame[:, 0:1], ALU.subtract))
            settle(nc.vector.tensor_scalar(nlam, nlam, -LAM0, None, ALU.add))
            for c, dst in enumerate((kD, vD, qD)):
                for j in range(2):
                    used(dve, W_KV + 2 * c + j)
                    nc.vector.tensor_scalar(dst[:, 1, j * HALF:(j + 1) * HALF], psum[:, 2 * j + 1, :], rstd[:, 17:18], None,
                                            ALU.mult).then_inc(kv_dve, 1)
            for inst, dst in ((T_KB, kDT), (T_QB, qDT)):
                for b in ODD_EVEN(inst)[1]:
                    evacuate(dve, inst, b, dst)
            for hh in range(HEADS + 1):
                if hh < HEADS:
                    dve.wait_ge(sc_done, HEADS + hh + 1)
                    if hh >= 4:
                        dve.wait_ge(pt_filled, HEADS + hh // 2 - 1)
                    buf = sd[:, hh % 4, :]
                    nc.vector.scalar_tensor_tensor(out=buf, in0=psum[:, 4 + hh % 2, 0:384], scalar=HD ** -0.5,
                                                   in1=C("causal"), op0=ALU.mult, op1=ALU.add).then_inc(sc_read, 1)
                    dve.wait_ge(sc_read, HEADS + hh + 1)
                    nc.vector.tensor_reduce(nmx[:, hh, 1:2], buf[:, 0:256], AX.X, ALU.max, negate=True)
                    nc.vector.tensor_reduce(nmx[:, hh, 0:1], buf[:, 256:384], AX.X, ALU.max, negate=True).then_inc(mx_ready, 1)
                if hh >= 2 and hh % 2 == 0:
                    g = hh // 2 - 1
                    dve.wait_ge(exp_done, HEADS + 2 * g + 2)
                    settle(nc.vector.reciprocal(rd[g % 2], sums[:, 2 * g:2 * g + 2, :]))
                    settle(nc.vector.tensor_scalar(rd[g % 2][:, 1, :], rd[g % 2][:, 1, :], nlam, None, ALU.mult))
                    b0, b1 = sd[:, (2 * g) % 4, :], sd[:, (2 * g + 1) % 4, :]
                    for t, cut in ((1, slice(0, 256)), (0, slice(256, 384))):
                        ins = nc.vector.tensor_scalar(b0[:, cut], b0[:, cut], rd[g % 2][:, 0, t:t + 1], None, ALU.mult)
                    settle(ins)
                    for t, cut in ((1, slice(0, 256)), (0, slice(256, 384))):
                        ins = nc.vector.scalar_tensor_tensor(out=b0[:, cut], in0=b1[:, cut], scalar=rd[g % 2][:, 1, t:t + 1],
                                                             in1=b0[:, cut], op0=ALU.mult, op1=ALU.add)
                    ins.then_inc(comb_ready, 1)
            dve.wait_ge(o_sq, 1)
            settle(nc.vector.tensor_reduce(vr_y[:, :, 0:8], oD2.rearrange("p t (h d) -> p t h d", d=P), AX.X, ALU.add))
            nc.vector.tensor_scalar(vr_y[:, :, 0:8], vr_y[:, :, 0:8], 1.0 / P, 1e-5, ALU.mult, ALU.add).then_inc(o_var, 1)
            dve.wait_ge(o_root, 1)
            settle(nc.vector.reciprocal(rs_y[:, :, 0:8], rt_y[:, :, 0:8]))
            oh = oD.rearrange("p t (h d) -> p t h d", d=P)
            settle(nc.vector.tensor_tensor(oh, oh, rs_y[:, :, 0:8].unsqueeze(3).broadcast_to([P, NT, 8, P]), ALU.mult))
            sl = row_of("subln")
            for t in range(NT):
                ins = nc.vector.scalar_tensor_tensor(out=oD[:, t, :], in0=oD[:, t, :], scalar=1.0 - LAM0, in1=sl,
                                                     op0=ALU.mult, op1=ALU.mult)
            settle(ins)
            dve.wait_ge(kv_act, 8)
            nc.vector.tensor_tensor(oD, oD, gD, ALU.mult).then_inc(od_ready, 1)
            evacuate_low(dve, T_OB, (XH, XL, None))
            add_normed(9, yo, "norm_post1")
            dve.wait_ge(h_ready, 8)
            embed_dve(10, 1, T_H8, "ple_norm1")

        @block.tensor
        def _(pe):
            pe.wait_ge(par_landed, 32)
            pe.wait_ge(x_landed, 16)
            pe_transposes(pe, T_H0, h)

            def qkv_free(pe, c):
                if c >= 2:
                    pe.wait_ge(qkv_act, c - 1)
                    pe.wait_ge(qkv_dve, c - 1)
            pe_linear(pe, W_QKV, 6, xT2, qkv_free, transposed(pe, T_H0))
            pe.wait_ge(qkv_act, 6)
            pe.wait_ge(qkv_dve, 6)
            pe_transposes(pe, T_Q, qn)
            pe_transposes(pe, T_K, kn)
            evacuated(pe, T_K)
            for hh in range(HEADS + 3):
                if hh < HEADS:
                    if hh >= 2:
                        pe.wait_ge(sc_read, hh - 1)
                    p0, f = HD * (hh % 2), hh // 2
                    q, k = qT[p0:p0 + HD, f, :], kT[p0:p0 + HD, f, :]
                    nc.tensor.matmul(psum[:, 4 + hh % 2, 0:256], q[:, P:2 * P], k, start=True, stop=True)
                    nc.tensor.matmul(psum[:, 4 + hh % 2, 256:384], q[:, 0:P], k[:, 0:P], start=True, stop=True).then_inc(sc_done, 1)
                if 2 <= hh < HEADS + 2:
                    g = hh - 2
                    pe.wait_ge(exp_done, g + 1)
                    if g >= 2:
                        pe.wait_ge(pt_copied, g - 1)
                    for j in range(3):
                        ins = nc.tensor.transpose(psum[:, 6 + g % 2, j * P:(j + 1) * P], sbuf_s[:, g % 3, j * P:(j + 1) * P], ident)
                    ins.then_inc(pt_filled, 1)
                if hh >= 3:
                    g = hh - 3
                    pe.wait_ge(pt_copied, g + 1)
                    pt = sbuf_pt[:, g % 2, :]
                    o = psum[:, g // 4, :].rearrange("p (h t d) -> p h t d", t=NT, d=HD)[:, g % 4]
                    v = vn[:, :, g * HD:(g + 1) * HD]
                    nc.tensor.matmul(o[:, 0], pt[:, 256:384], v[:, 0], start=True, stop=True)
                    nc.tensor.matmul(o[:, 1], pt[:, 0:128], v[:, 0], start=True, stop=False)
                    nc.tensor.matmul(o[:, 1], pt[:, 128:256], v[:, 1], start=False, stop=True).then_inc(pv_done, 1)
            pe.wait_ge(o_ready, 4)
            pe_transposes(pe, T_O, on)
            pe_linear(pe, W_O, 2, xT2, None, transposed(pe, T_O))
            pe.wait_ge(h_ready, 1)
            pe_transposes(pe, T_H1, h)
            mlp_pe(pe, 0, T_H1)

            pe.wait_ge(xn_ready, 1)
            pe_transposes(pe, T_N2, xn)
            pe.wait_ge(h_ready, 2)
            for i in range(4):
                for j in range(2):
                    pe_feature_tile(pe, 4 * W_INX + 2 * i + j, psum[:, i, j * SEQ:(j + 1) * SEQ],
                                    transposed(pe, T_N2) if i == 0 and j == 0 else None)
            for i in range(4):
                pe.wait_ge(xc_ready, i + 1)
                if i >= 2:
                    pe.wait_ge(gates_read, i - 1)
                piece_ready(pe, 4 * W_GATES + i)
                gw = raw(4 * W_GATES + i, 2, 4, P)
                for j in range(2):
                    f = 2 * i + j
                    nc.tensor.matmul(psum[:, 4 + i % 2, j * SEQ:(j + 1) * SEQ], gw[:, 0, j, :], xc[:, f, :], start=True, stop=True)
                    ins = nc.tensor.matmul(psum[:, 6 + i % 2, j * SEQ:(j + 1) * SEQ], gw[:, 0, 2 + j, :], xc[:, f, :], start=True, stop=True)
                ins.then_inc(piece_used, 1)
            for i in range(4):
                pe.wait_ge(x_read, i + 1)
                for j in range(2):
                    pe_feature_tile(pe, 4 * W_INY + 2 * i + j, psum[:, i, j * SEQ:(j + 1) * SEQ])
            pe.wait_ge(y_read, 4)
            pe_linear(pe, W_RO, 2, xT2, None, lambda i: pe.wait_ge(og_low, i // 2 + 1))
            pe.wait_ge(h_ready, 3)
            pe_transposes(pe, T_H3, h)
            mlp_pe(pe, 1, T_H3)

            pe.wait_ge(xn_ready, 2)
            pe_transposes(pe, T_N5, xn5)
            pe.wait_ge(lor_landed, 32)
            for i in range(2):
                pe.wait_ge(mix_ready, i + 1)
                for k in range(KT):
                    ins = nc.tensor.matmul(psum[0:64, 4 + i, 0:SEQ], lora1_sb[:, i, k, :], xm[i][:, k, :],
                                           start=(k == 0), stop=(k == KT - 1))
                ins.then_inc(lora_filled, 1)
            for i in range(2):
                pe.wait_ge(lora_out, i + 1)
                if i == 1:
                    pe.wait_ge(lora2_read, 1)
                for t in range(NT):
                    for half in range(2):
                        ins = nc.tensor.matmul(psum[:, 2 * t + half, :], lt[0:64, i, t * P:(t + 1) * P],
                                               lora2_sb[0:64, i, half * HALF:(half + 1) * HALF], start=True, stop=True)
                ins.then_inc(lora2_filled, 1)
            pe.wait_ge(sig_ready, 1)
            pe.wait_ge(lora2_read, 2)
            for t in range(NT):
                for half in range(2):
                    ins = nc.tensor.matmul(psum[:, 2 * t + half, :], C("tri_incl"), sg[:, t, half * HALF:(half + 1) * HALF],
                                           start=True, stop=True)
            ins.then_inc(cum_filled, 1)

            def rkvg_free(pe, c):
                if c == 0:
                    pe.wait_ge(decays, 2)
                    pe.wait_ge(cum_prev, 1)
                elif c in (2, 3):
                    pe.wait_ge(proj_act, c - 1)
                elif c in (4, 5):
                    pe.wait_ge(proj_dve, c - 3)
                if c % 2 == 0:
                    pe.wait_ge(mix_ready, 3 + c // 2)

            def project(i):
                for c in (2 * i, 2 * i + 1):
                    pe_chunk(pe, W_RKVG + c, c, xm[i % 2], rkvg_free)

            project(0)
            pe.wait_ge(decays, 1)
            for f in range(KT):
                for t in range(NT):
                    ins = nc.tensor.matmul(psum[:, 4, 4 * f + 2 * t:4 * f + 2 * t + 2], Pd[:, t, f * P:(f + 1) * P], C("last"),
                                           start=True, stop=True)
            ins.then_inc(last_filled, 1)
            project(1)
            project(2)
            pe.wait_ge(beta_kap, 2)
            pe.wait_ge(khat, 2)
            pe.wait_ge(bonus, 2)
            for inst, src in ((T_KAP, kap), (T_RH, rN), (T_BET, bet), (T_KH, kN)):
                pe_transposes(pe, inst, src)
            evacuated(pe, T_KH)

            pe.wait_ge(proj_act, 4)
            pe.wait_ge(last_read, 1)
            STEPS = ["x0", "x1", "x2", "x3"] + list(range(1, 12))
            for pp in range(4):
                for s_ in STEPS:
                    for b in range(2):
                        f, B = 2 * pp + b, 4 * b
                        dve_did = lambda st, p_=pp: core_wait(pe, core_dve, DVE_AT, p_, b, st)
                        act_did = lambda st, p_=pp: core_wait(pe, core_act, ACT_AT, p_, b, st)
                        u, x_, o_, z_ = U[b], XX[b], OFF[b], U[b][:, :, 0, :]
                        bank = lambda k, q: psum[:, B + k, q * P:(q + 1) * P]
                        for q in range(4):
                            hh, t = q // 2, q % 2
                            p0 = HD * hh
                            head = slice((2 * f + hh) * HD, (2 * f + hh + 1) * HD)
                            tt = slice(t * P, (t + 1) * P)
                            if isinstance(s_, str):
                                if q != int(s_[1]):
                                    continue
                                if q == 0 and pp > 0:
                                    dve_did(11, pp - 1)
                                    act_did(11, pp - 1)
                                kr = KR[p0:p0 + HD, f, :, tt]
                                nc.tensor.matmul(psum[:, B + q, 0:256], bT[p0:p0 + HD, f, tt], kr, start=True, stop=True)
                                ins = nc.tensor.matmul(psum[:, B + q, 256:512], khT[p0:p0 + HD, f, tt], kr, start=True, stop=True)
                            elif s_ == 1:
                                if q == 0:
                                    dve_did("x1")
                                ins = nc.tensor.matmul(psum[:, B + hh, tt], KR[p0:p0 + HD, f, 0, tt], bT[p0:p0 + HD, f, tt], start=True, stop=True)
                            elif s_ == 2:
                                if q == 0:
                                    dve_did(1)
                                nc.tensor.matmul(bank(1, q), x_[:, q, :], u[:, q, 1, :], start=True, stop=True)
                                nc.tensor.matmul(bank(2, q), u[:, q, 1, :], x_[:, q, :], start=True, stop=True)
                                ins = nc.tensor.matmul(psum[:, B + 3, q * 64:(q + 1) * 64], u[:, q, 3, :], vN[:, t, head], start=True, stop=True)
                            elif s_ == 3:
                                if q == 0:
                                    dve_did(2)
                                    act_did(2)
                                    pe.wait_ge(core_pool[b], pp + 1)
                                nc.tensor.matmul(bank(0, q), x_[:, q, :], z_[:, q, :], start=True, stop=True)
                                nc.tensor.matmul(bank(1, q), x_[:, q, :], u[:, q, 1, :], start=True, stop=True)
                                ins = nc.tensor.matmul(bank(2, q), u[:, q, 1, :], x_[:, q, :], start=True, stop=True)
                            elif s_ == 4:
                                if q == 0:
                                    dve_did(3)
                                    act_did(3)
                                nc.tensor.matmul(bank(3, q), x_[:, q, :], z_[:, q, :], start=True, stop=True)
                                ins = nc.tensor.matmul(bank(2, q), u[:, q, 1, :], x_[:, q, :], start=True, stop=True)
                            elif s_ == 5:
                                if q == 0:
                                    dve_did(4)
                                    act_did(4)
                                ins = nc.tensor.matmul(bank(0, q), x_[:, q, :], z_[:, q, :], start=True, stop=True)
                            elif s_ in (6, 8):
                                if q == 0:
                                    dve_did(s_ - 1)
                                nc.tensor.transpose(bank(1, q), z_[:, q, :], ident)
                                ins = nc.tensor.matmul(bank(2, q), o_[:, (s_ - 6) // 2, q, :], z_[:, q, :], start=True, stop=True)
                            elif s_ in (7, 9):
                                if q == 0:
                                    dve_did(s_ - 1)
                                    act_did(s_ - 1)
                                ins = nc.tensor.matmul(bank(0, q), x_[:, q, :], u[:, q, 1, :], start=True, stop=True)
                            elif s_ == 10:
                                if q == 0:
                                    dve_did(9)
                                nc.tensor.matmul(bank(1, q)[:, 0:64], z_[:, q, :], kap[:, t, head], start=True, stop=True)
                                ins = nc.tensor.matmul(bank(1, q)[:, 64:128], z_[:, q, :], BV[b][:, q, :], start=True, stop=True)
                            else:
                                if q == 0:
                                    act_did(10)
                                wu = WU[b][:, q, :]
                                for c in range(2):
                                    g = 2 * t + c
                                    cc = slice(64 * c, 64 * c + 64)
                                    at = lambda n: psum[p0:p0 + HD, B + 2 + c, 64 * (n - 3 * c):64 * (n - 3 * c) + 64]
                                    if g in (1, 2):
                                        o = at(M_OF[g])
                                        nc.tensor.matmul(o, C("eye2")[cc, :], C("eye2")[cc, :], start=True, stop=False)
                                        nc.tensor.matmul(o, wu[cc, 0:64], bet[cc, t, head], start=False, stop=True)
                                    if g < 3:
                                        o = at(N_OF[g])
                                        nc.tensor.matmul(o, kN[cc, t, head], vN[cc, t, head], start=True, stop=False)
                                        nc.tensor.matmul(o, bet[cc, t, head], wu[cc, 64:128], start=False, stop=True)
                                nc.tensor.matmul(psum[p0:p0 + HD, B + 1, tt], wu[:, 0:64], u[:, q, 2, :],
                                                 start=True, stop=True)
                                o = psum[:, B, q * 64:(q + 1) * 64]
                                nc.tensor.matmul(o, u[:, q, 4, :], vN[:, t, head], start=True, stop=False)
                                ins = nc.tensor.matmul(o, u[:, q, 2, :], wu[:, 64:128], start=False, stop=True)
                        ins.then_inc(core_filled[b], 1)
            for b in range(2):
                core_wait(pe, core_dve, DVE_AT, 3, b, 11)
                core_wait(pe, core_act, ACT_AT, 3, b, 11)
            for g in (1, 2):
                pe.wait_ge(state_ready, g)
                for f in range(KT):
                    for p0 in (0, HD):
                        ins = nc.tensor.matmul(psum[p0:p0 + HD, 4 + 2 * (g - 1) + p0 // HD, f * 64:(f + 1) * 64], MN[p0:p0 + HD, f, M_OF[g], :],
                                               Sg[g][p0:p0 + HD, f, :], start=True, stop=True)
                ins.then_inc(state_filled, 1)
            pe.wait_ge(state_ready, 3)
            for g in (1, 2, 3):
                t, c = g // 2, g % 2
                for hh in range(HEADS):
                    f, p0 = hh // 2, HD * (hh % 2)
                    ins = nc.tensor.matmul(psum[64 * c:64 * c + 64, 4 + 2 * t + hh % 2, f * 64:(f + 1) * 64],
                                           KR[p0:p0 + HD, f, 1, t * P + 64 * c:t * P + 64 * c + 64], Sg[g][p0:p0 + HD, f, :],
                                           start=True, stop=True)
            ins.then_inc(ys_filled, 1)
            for j in range(2):
                pe_chunk(pe, W_RKVG + 6 + j, j, xTb2, None, (lambda i: pe.wait_ge(xg_low, i // 2 + 1)) if j == 0 else None)
            pe.wait_ge(y_ready, 1)

            def embed_pe(tile, e_n, T):
                pe.wait_ge(lor_landed, 48 + 16 * e_n)
                pe.wait_ge(yo_act, 2 * e_n + 2)
                for c in range(2):
                    for k in range(2):
                        m = 4 * tile + 2 * c + k
                        piece_ready(pe, m)
                        for t in range(NT):
                            ins = nc.tensor.matmul(psum[:, 2 * c + t, :], pT_sb[:, k, t * P:(t + 1) * P],
                                                   raw(m)[:, c * HALF:(c + 1) * HALF], start=(k == 0), stop=(k == 1))
                        ins.then_inc(piece_used, 1)
                pe.wait_ge(h_ready, 6 + 2 * e_n)
                pe_transposes(pe, T, h)
                pe.wait_ge(e_act, e_n + 1)
                pe_linear(pe, tile + 1, 2, xT2, None, transposed(pe, T))

            pe_transposes(pe, T_YA, yN)
            pe_linear(pe, W_OUT_A, 2, xT2, None, transposed(pe, T_YA))
            embed_pe(W_PLE0, 0, T_H6)

            pe.wait_ge(h_ready, 7)
            pe_transposes(pe, T_H7, h)

            def kvqg_free(pe, c):
                if c >= 2:
                    pe.wait_ge(kv_act, c - 1)
                    pe.wait_ge(kv_dve, min(c - 1, 6))
            for c in range(8):
                pe_chunk(pe, W_KV + c, c, xTb2 if c < 4 else xT2, kvqg_free, transposed(pe, T_H7) if c == 0 else None)
            pe.wait_ge(roped, 1)
            pe_transposes(pe, T_KB, kD)
            pe.wait_ge(roped, 2)
            pe_transposes(pe, T_QB, qD)
            evacuated(pe, T_QB)
            pe.wait_ge(kv_act, 8)
            for hh in range(HEADS + 4):
                if hh < HEADS:
                    if hh >= 2:
                        pe.wait_ge(sc_read, HEADS + hh - 1)
                    p0, f = HD * (hh % 2), hh // 2
                    q, k = qDT[p0:p0 + HD, f, :], kDT[p0:p0 + HD, f, :]
                    nc.tensor.matmul(psum[:, 4 + hh % 2, 0:256], q[:, P:2 * P], k, start=True, stop=True)
                    nc.tensor.matmul(psum[:, 4 + hh % 2, 256:384], q[:, 0:P], k[:, 0:P], start=True, stop=True).then_inc(sc_done, 1)
                if hh >= 5 and hh % 2 == 1:
                    g = (hh - 5) // 2
                    pe.wait_ge(pt_copied, HEADS + g + 1)
                    pt = pt2[:, g % 2, :]
                    o = psum[:, g // 2, :].rearrange("p (h t d) -> p h t d", t=NT, d=P)[:, g % 2]
                    v = vD[:, :, g * P:(g + 1) * P]
                    nc.tensor.matmul(o[:, 0], pt[:, 256:384], v[:, 0], start=True, stop=True)
                    nc.tensor.matmul(o[:, 1], pt[:, 0:128], v[:, 0], start=True, stop=False)
                    nc.tensor.matmul(o[:, 1], pt[:, 128:256], v[:, 1], start=False, stop=True).then_inc(pv_done, 1)
                if 3 <= hh < HEADS + 3 and hh % 2 == 1:
                    g = (hh - 3) // 2
                    pe.wait_ge(comb_ready, g + 1)
                    if g >= 2:
                        pe.wait_ge(pt_copied, HEADS + g - 1)
                    for j in range(3):
                        ins = nc.tensor.transpose(psum[:, 6 + g % 2, j * P:(j + 1) * P], sd[:, (2 * g) % 4, j * P:(j + 1) * P], ident)
                    ins.then_inc(pt_filled, 1)
            pe.wait_ge(od_ready, 1)
            pe_transposes(pe, T_OB, oD)
            pe_linear(pe, W_OUT_B, 2, xT2, None, transposed(pe, T_OB))
            embed_pe(W_PLE1, 1, T_H8)

def layout(inp):
    f = lambda n: np.ascontiguousarray(np.asarray(inp[n]))
    tiles = []

    def cols_tile(wm, c):
        tiles.append(wm[:, c * HALF:(c + 1) * HALF].reshape(KT, P, HALF).transpose(1, 0, 2).reshape(P, 4096))

    def rows_tile(wm, c):
        tiles.append(wm[c * HALF:(c + 1) * HALF].reshape(4, P, D).transpose(1, 0, 2).reshape(P, 4096))

    def feature_tiles(wm, c):
        tiles.append(wm[:, c * HALF:(c + 1) * HALF].reshape(KT, P, 4, P).transpose(1, 2, 0, 3).reshape(P, 4096))

    def mlp(m):
        w1, w2 = f("mlp_w1")[m], f("mlp_w2")[m]
        feature_tiles(w1, 0)
        for c in range(1, 8):
            feature_tiles(w1, c)
            rows_tile(w2, c - 1)
        rows_tile(w2, 7)

    def ple(i):
        half = f("ple_w_2")[i].reshape(2, P, D).transpose(1, 0, 2).reshape(P, 2048)
        tiles.append(np.concatenate([half, half], 1))
        for c in range(2):
            cols_tile(f("ple_gate_2")[i], c)

    qkv = f("attn_w_qkv")[0]
    for c in (0, 2, 4, 1, 3, 5):
        cols_tile(qkv, c)
    for c in range(2):
        cols_tile(f("attn_w_o")[0], c)
    mlp(0)
    for c in range(2):
        feature_tiles(f("rec_w_in")[0], c)
    gates = np.stack([f(n)[0].reshape(4, 2, P, P) for n in ("rec_w_ga", "rec_w_gx")], 1)
    tiles.append(np.stack([gates, gates], 1).transpose(4, 0, 1, 2, 3, 5).reshape(P, 4096))
    for c in (2, 3):
        feature_tiles(f("rec_w_in")[0], c)
    for c in range(2):
        cols_tile(f("rec_w_o")[0], c)
    mlp(1)
    for j in (1, 0, 2, 3):
        for c in range(2):
            cols_tile(f("a_w_in_2")[0, j], c)
    for c in range(2):
        cols_tile(f("a_w_out_2")[0], c)
    ple(0)
    for c in range(4):
        cols_tile(f("kv_w_2"), c)
    for c in range(4):
        cols_tile(f("b_w_in_2")[0], c)
    for c in range(2):
        cols_tile(f("b_w_out_2")[0], c)
    ple(1)
    assert len(tiles) == W_TILES
    w = np.stack(tiles).reshape(W_TILES, P, 4, PIECE).transpose(0, 2, 1, 3).reshape(4 * W_TILES, P, PIECE)

    col = lambda v: v.reshape(KT, P).T
    b_in, cw, mu = f("rec_b_in")[0], f("rec_conv_w")[0], f("a_mu_2")[0]
    vals = {"norm_mix0": f("norm_mix")[0], "norm_mix1": f("norm_mix")[1], "norm_mlp0": f("norm_mlp")[0],
            "norm_mlp1": f("norm_mlp")[1], "b_in_x": b_in[:D], "b_in_y": b_in[D:], "conv_b": f("rec_conv_b")[0],
            "b_ga": f("rec_b_ga")[0].reshape(-1), "b_gx": f("rec_b_gx")[0].reshape(-1), "a_param": f("rec_a_param")[0],
            "norm_pre0": f("norm_pre_2")[0], "norm_pre1": f("norm_pre_2")[1], "kv_norm": f("kv_norm_2")}
    vals |= {f"conv_w{i}": cw[i] for i in range(4)} | {f"mu{i}": mu[i] for i in range(6)}
    cols = np.stack([col(vals[n]) for n in COLS], 1)
    rv = {"b_o": f("rec_b_o")[0], "norm_final": f("norm_final"), "w0": f("a_w0_2")[0], "a0": f("a_a0_2")[0],
          "k_k": f("a_k_k_2")[0], "k_a": f("a_k_a_2")[0], "r_k": f("a_r_k_2")[0].reshape(-1),
          "lnx_g": f("a_lnx_g_2")[0], "lnx_b": f("a_lnx_b_2")[0], "norm_post0": f("norm_post_2")[0],
          "norm_post1": f("norm_post_2")[1], "ple_norm0": f("ple_norm_2")[0], "ple_norm1": f("ple_norm_2")[1],
          "subln": np.concatenate([f("b_subln_2")[0]] * 8)}
    rows = np.stack([rv[n] for n in ROWS])
    rel = f("attn_rel_bias")[0][:, ::-1]
    relt = np.concatenate([rel[:, :1]] * 127 + [rel], 1)
    lora1 = np.stack([f(n)[0].reshape(KT, P, 64).transpose(1, 0, 2) for n in ("a_w1_2", "a_a1_2")], 1)
    lora2 = np.stack([f(n)[0] for n in ("a_w2_2", "a_a2_2")], 1)
    pT = f("p_2")[:, 0].transpose(0, 2, 1).reshape(2, 2, P, SEQ).transpose(2, 0, 1, 3)
    lam = f("b_lambda_2")[0].reshape(1, 256)
    x = f("x")[0]
    return {"x": x, "w": w, "cols": cols, "rows": rows, "consts": shape_constants(), "relt": relt, "lora1": lora1,
            "lora2": lora2, "pT": pT, "lam": lam}


def kernel(**inputs):
    import concourse.bacc as bacc
    from concourse.bass_utils import run_bass_kernel_spmd

    nc = bacc.Bacc("TRN2", target_bir_lowering=False, num_devices=1)
    arrays = {k: np.ascontiguousarray(v) for k, v in layout(inputs).items()}
    aps = {k: nc.dram_tensor(k, v.shape, F32, kind="ExternalInput").ap() for k, v in arrays.items()}
    out = nc.dram_tensor("out", (SEQ, D), F32, kind="ExternalOutput").ap()
    build(nc, **aps, out=out)
    r = run_bass_kernel_spmd(nc, [arrays], core_ids=[0])
    return r.results[0]["out"].reshape(1, SEQ, D)
```

```python
from contextlib import ExitStack

import numpy as np

import concourse.bass as bass
from concourse import mybir

ALU = mybir.AluOpType
ACT = mybir.ActivationFunctionType
F32 = mybir.dt.float32
F32R = mybir.dt.float32r
AX = mybir.AxisListType

P = 128
SEQ, D = 256, 1024
NT, KT = SEQ // P, D // P
HALF = 512
HEADS, HD = 16, 64
EPS = 1e-6
PIECE = 1024
RING = 8

W_QKV, W_O, W_MLP0, W_INX, W_GATES, W_INY, W_RO, W_MLP1 = 0, 6, 8, 24, 26, 27, 29, 31
W_RKVG, W_OUT_A, W_PLE0, W_KV, W_QG, W_OUT_B, W_PLE1, W_TILES = 47, 55, 57, 60, 64, 68, 70, 73

PLAIN = {W_GATES, W_PLE0, W_PLE1} | set(range(W_RKVG, W_RKVG + 6))
SPLITS = [0]
for _m in range(4 * W_TILES):
    SPLITS.append(SPLITS[-1] + (_m // 4 not in PLAIN))

COLS = ["norm_mix0", "norm_mix1", "norm_mlp0", "norm_mlp1", "b_in_x", "b_in_y", "conv_w0", "conv_w1", "conv_w2",
        "conv_w3", "conv_b", "b_ga", "b_gx", "a_param", "norm_pre0", "norm_pre1", "kv_norm",
        "mu0", "mu1", "mu2", "mu3", "mu4", "mu5"]
ROWS = ["b_o", "norm_final", "w0", "a0", "k_k", "k_a", "r_k", "lnx_g", "lnx_b", "norm_post0", "ple_norm0",
        "subln", "norm_post1", "ple_norm1"]
CONSTS = {}
_at = 0
for _name, _n in (("ident", 128), ("tri_incl", 128), ("mask_x", 512), ("mask_a", 384), ("causal", 384),
                  ("cos", 16), ("sin", 16), ("eye2", 64), ("last", 2)):
    CONSTS[_name] = (_at, _n)
    _at += _n
N_CONSTS = _at


def shape_constants():
    i = np.arange(P)
    c = np.zeros((P, N_CONSTS), np.float32)

    def put(name, value):
        a, n = CONSTS[name]
        c[:, a:a + n] = np.asarray(value, np.float32).reshape(P, n)

    r, s = i[:, None], i[None, :]
    same = lambda n: (r // n) == (s // n)
    put("ident", r == s)
    put("tri_incl", (r <= s) & same(64))
    put("mask_x", np.stack([-1.0 * ((r < s) & same(16)), 1.0 * ((r <= s) & same(64)),
                            1.0 * ((r < s) & same(64)), 1.0 * ((r <= s) & same(64))], 1))
    put("mask_a", np.stack([-1.0 * ((s < r) & same(16)), 1.0 * ((s < r) & same(32) & ~same(16)),
                            1.0 * ((s < r) & same(64) & ~same(32))], 1))
    k = np.arange(SEQ)[None, :]
    put("causal", np.concatenate([np.where(k <= P + r, 0, -1e30), np.where(s <= r, 0, -1e30)], 1))
    inv = np.float32(500000.0) ** (-np.arange(0, 16, 2, dtype=np.float32) / np.float32(16))
    ang = (np.arange(SEQ, dtype=np.float32)[:, None] * inv.astype(np.float32)[None, :]).astype(np.float32)
    tok = ang.reshape(NT, P, 8).transpose(1, 0, 2)
    put("cos", np.cos(tok.astype(np.float64)))
    put("sin", np.sin(tok.astype(np.float64)))
    put("eye2", (i[:, None] % 64) == np.arange(64)[None, :])
    put("last", np.stack([i == 63, i == 127], 1))
    return c


def build(nc, x, w, cols, rows, consts, relt, lora1, lora2, pT, lam, out):
    with ExitStack() as ctx:
        def sb(name, shape):
            return ctx.enter_context(nc.sbuf_tensor(name, shape, F32))

        def sem(name):
            return ctx.enter_context(nc.semaphore(name))

        ring = sb("ring", [P, RING, PIECE])
        ring_r = nc.alloc_sbuf_tensor_at("ring_r", [P, RING, PIECE], F32R, offset=nc.sbuf_base - 4 * RING * PIECE,
                                         align_bytes=32)
        h = sb("h", [P, NT, D])
        ARENA = 32800
        arena = sb("arena", [P, ARENA])
        arena_base = nc.sbuf_base - 4 * ARENA
        col = sb("col", [P, len(COLS), KT])
        row = sb("row", [P, 5, D])
        con = sb("con", [P, N_CONSTS])
        small = sb("small", [P, 1024])
        psum = ctx.enter_context(nc.psum_tensor("psum", [P, 8, HALF], F32))

        def C(name):
            a, n = CONSTS[name]
            return con[:, a:a + n]

        ident = C("ident")

        def c8(name):
            return col[:, COLS.index(name), :]

        def shaped(v, dims):
            if len(dims) < 2:
                return v
            names = "abcd"[:len(dims)]
            return v.rearrange("p (" + " ".join(names) + ") -> p " + " ".join(names),
                               **{k: d for k, d in zip(names[1:], dims[1:])})

        def view(off, *dims):
            n = int(np.prod(dims))
            assert off + n <= ARENA, (off, dims)
            return shaped(arena[:, off:off + n], dims)

        def place_r(name, off, n):
            assert off + n <= ARENA
            return nc.alloc_sbuf_tensor_at(name, [P, n], F32R, offset=arena_base + 4 * off, align_bytes=32)[:, :]

        def raw(m, *dims):
            return shaped(ring[:, m % RING, :], dims)

        def high(m, *dims):
            return shaped(high_r[:, PIECE * (m % RING):PIECE * (m % RING + 1)], dims)

        def read(v):
            return v.bitcast(F32)

        def low(m, *dims):
            return shaped(ring_r[:, m % RING, :], dims)

        small_at = [0]

        def little(n):
            small_at[0] += n
            assert small_at[0] <= 1024
            return small[:, small_at[0] - n:small_at[0]]

        S = 2048
        high_r = place_r("high_r", 12 * S, RING * PIECE)
        piece_landed = [sem(f"piece_landed{i}") for i in range(RING)]
        high_made, low_made, piece_used = sem("high_made"), sem("low_made"), sem("piece_used")
        x_landed, spread_stored = sem("x_landed"), sem("spread_stored")
        spread = nc.dram_tensor("bias_spread", (P, HEADS * 384), F32, kind="Internal").ap()
        par_landed, con_landed = sem("par_landed"), sem("con_landed")
        row_landed = [sem(f"row_landed{i}") for i in range(5)]
        act_step, dve_step, pool_step = sem("act_step"), sem("dve_step"), sem("pool_step")
        stat_sum, stat_var, stat_root, rstd_ready = sem("stat_sum"), sem("stat_var"), sem("stat_root"), sem("rstd_ready")
        h_ready = sem("h_ready")
        tp_filled = sem("tp_filled")
        tp_act, tp_dve = sem("tp_act"), sem("tp_dve")
        out_stored = sem("out_stored")

        N_STATS = 12
        ss, var, root, rstd = little(2 * N_STATS), little(2 * N_STATS), little(2 * N_STATS), little(2 * N_STATS)

        (T_H0, T_Q, T_K, T_O, T_H1, T_N2, T_H3, T_N5, T_BET, T_KAP, T_RH, T_KH, T_YA, T_H6, T_H7, T_KB, T_QB, T_OB,
         T_H8) = range(19)

        SPLIT_T = {T_H0, T_O, T_H1, T_N2, T_H3, T_YA, T_H6, T_H7, T_OB, T_H8}
        BANK_OF, ACT_BANKS, DVE_BANKS, PREVIOUS, _last = [], [0], [0], [], {}
        for _i in range(T_H8 + 1):
            for _b in range(4):
                bank_ = 4 + _b if _i in SPLIT_T else 6 + _b % 2
                BANK_OF.append(bank_)
                PREVIOUS.append(_last.get(bank_))
                _last[bank_] = len(BANK_OF) - 1
                ACT_BANKS.append(ACT_BANKS[-1] + (_i in SPLIT_T or _b % 2 == 0))
                DVE_BANKS.append(DVE_BANKS[-1] + (_i in SPLIT_T or _b % 2 == 1))

        def bank_out(eng, g):
            if ACT_BANKS[g + 1]:
                eng.wait_ge(tp_act, ACT_BANKS[g + 1])
            if DVE_BANKS[g + 1]:
                eng.wait_ge(tp_dve, DVE_BANKS[g + 1])

        def pe_transposes(pe, inst, src, ready=None):
            for b in range(4):
                if ready is not None:
                    ready(b)
                g = 4 * inst + b
                if PREVIOUS[g] is not None:
                    bank_out(pe, PREVIOUS[g])
                for j in range(2):
                    for t in range(NT):
                        ins = nc.tensor.transpose(psum[:, BANK_OF[g], (2 * j + t) * P:(2 * j + t + 1) * P],
                                                  src[:, t, (2 * b + j) * P:(2 * b + j + 1) * P], ident)
                ins.then_inc(tp_filled, 1)

        def filling(g):
            return psum[:, BANK_OF[g], :].rearrange("p (j t) -> p j t", j=2)

        def evacuate(eng, inst, b, dst, gain=None):
            g = 4 * inst + b
            eng.wait_ge(tp_filled, g + 1)
            on_act = b % 2 == 0
            assert on_act == (eng is engines["act"])
            if gain is None:
                dd = dst[:, 2 * b:2 * b + 2, :]
                ins = nc.scalar.copy(dd, filling(g)) if on_act else nc.vector.tensor_copy(dd, filling(g))
            else:
                for j in range(2):
                    k = 2 * b + j
                    if on_act:
                        ins = nc.scalar.activation(dst[:, k, :], filling(g)[:, j, :], ACT.Copy, scale=gain[:, k:k + 1])
                    else:
                        ins = nc.vector.tensor_scalar(dst[:, k, :], filling(g)[:, j, :], gain[:, k:k + 1], None, ALU.mult)
            ins.then_inc(tp_act if on_act else tp_dve, 1)

        def evacuate_high(act, inst, *pairs, between=None):
            for b in range(4):
                g = 4 * inst + b
                act.wait_ge(tp_filled, g + 1)
                for dst, gain in pairs:
                    if gain is None:
                        ins = nc.scalar.copy(dst[:, 2 * b:2 * b + 2, :], filling(g))
                    else:
                        for j in range(2):
                            k = 2 * b + j
                            ins = nc.scalar.activation(dst[:, k, :], filling(g)[:, j, :], ACT.Copy, scale=gain[:, k:k + 1])
                ins.then_inc(tp_act, 1)
                if between is not None:
                    between(b)

        def evacuate_low(dve, inst, *triples):
            for b in range(4):
                g = 4 * inst + b
                dve.wait_ge(tp_act, ACT_BANKS[g + 1])
                for hi, dst, gain in triples:
                    if gain is None:
                        u = slice(2 * b, 2 * b + 2)
                        ins = nc.vector.tensor_tensor(dst[:, u, :], filling(g), read(hi[:, u, :]), ALU.subtract)
                    else:
                        for j in range(2):
                            k = 2 * b + j
                            ins = nc.vector.scalar_tensor_tensor(out=dst[:, k, :], in0=filling(g)[:, j, :],
                                                                 scalar=gain[:, k:k + 1], in1=read(hi[:, k, :]),
                                                                 op0=ALU.mult, op1=ALU.subtract)
                ins.then_inc(tp_dve, 1)

        def evacuated(eng, inst):
            bank_out(eng, 4 * inst + 3)

        def h_halves(pe, n):
            return lambda b: pe.wait_ge(h_half, {1: 1, 3: 2, 6: 3, 7: 4, 8: 5}[n]) if b < 2 else pe.wait_ge(h_ready, n)

        engines = {}

        qkv_act, qkv_dve = sem("qkv_act"), sem("qkv_dve")
        sc_done, sc_read, mx_ready, exp_done, pt_filled, pt_copied, pv_done, o_ready = (
            sem(n) for n in ("sc_done", "sc_read", "mx_ready", "exp_done", "pt_filled", "pt_copied", "pv_done", "o_ready"))
        bias_ready = sem("bias_ready")
        z_relu, zz_ready, z_high, z_low = sem("z_relu"), sem("zz_ready"), sem("z_high"), sem("z_low")
        mask_set = sem("mask_set")

        x_read, y_read, xc_ready, gates_read, og_high, og_low = (
            sem(n) for n in ("x_read", "y_read", "xc_ready", "gates_read", "og_high", "og_low"))
        xn_ready, pad_zero, decay_ready, decay_part, m2_ready, m_ready, g_ready = (
            sem(n) for n in ("xn_ready", "pad_zero", "decay_ready", "decay_part", "m2_ready", "m_ready", "g_ready"))
        lor_landed, lam_landed = sem("lor_landed"), sem("lam_landed")
        mix_ready, lora_filled, lora_out, lora2_filled, lora2_read, sig_ready, cum_filled, cum_prev, decays, last_filled, last_read = (
            sem(n) for n in ("mix_ready", "lora_filled", "lora_out", "lora2_filled", "lora2_read", "sig_ready",
                             "cum_filled", "cum_prev", "decays", "last_filled", "last_read"))
        proj_act, proj_dve, kk_raw, kk_sq, kk_var, kk_root, kk_unit, k_ready, beta_kap, khat, bonus = (
            sem(n) for n in ("proj_act", "proj_dve", "kk_raw", "kk_sq", "kk_var", "kk_root", "kk_unit", "k_ready",
                             "beta_kap", "khat", "bonus"))
        xg_high, xg_low, hg_ready, h_tile0 = sem("xg_high"), sem("xg_low"), sem("hg_ready"), sem("h_tile0")
        part_sq, part_gain, h_half, gate_gain = sem("part_sq"), sem("part_gain"), sem("h_half"), sem("gate_gain")
        core_filled, core_dve, core_act, core_pool = ([sem(f"{n}{b}") for b in range(2)] for n in
                                                      ("core_filled", "core_dve", "core_act", "core_pool"))
        state_filled, state_ready, ys_filled, y_sq, y_var, y_root, y_ready, bv_ready, y_cent = (
            sem(n) for n in ("state_filled", "state_ready", "ys_filled", "y_sq", "y_var", "y_root", "y_ready",
                             "bv_ready", "y_cent"))
        e_act, gate_act, ge_ready = sem("e_act"), sem("gate_act"), sem("ge_ready")
        kv_act, kv_dve, roped, lam_sum, lam_exp, comb_ready, o_act, o_sq, o_var, o_root, od_ready = (
            sem(n) for n in ("kv_act", "kv_dve", "roped", "lam_sum", "lam_exp", "comb_ready", "o_act", "o_sq", "o_var",
                             "o_root", "od_ready"))

        qn, kn, vn = (view(i * S, NT, D) for i in (0, 1, 2))
        qT, kT = view(3 * S, KT, SEQ), view(4 * S, KT, SEQ)
        on = view(5 * S, NT, D)
        bias = view(6 * S, HEADS, 384)
        sbuf_s = view(9 * S, 3, 384)
        sbuf_pt = view(9 * S + 1152, 2, 384)
        XT = 30720
        XH, XL, XBH, XBL = (shaped(place_r(name, at * S, S), (KT, SEQ)) for name, at in
                            (("x_high", 10), ("x_low", 11), ("xb_high", 6), ("xb_low", 7)))
        xT2, xTb2 = (XH, XL), (XBH, XBL)

        def junk_at(i):
            return view((5 if i < 6 else 8) * S, NT, D)
        nmx = little(2 * 2 * HEADS).rearrange("p (h t) -> p h t", t=2)
        sums = little(2 * 2 * HEADS).rearrange("p (h t) -> p h t", t=2)
        rsum = little(2 * 2 * HEADS).rearrange("p (h t) -> p h t", t=2)
        QKV = [(qn, 0), (kn, 0), (vn, 0), (qn, 1), (kn, 1), (vn, 1)]
        zr, zz = view(0, 4, SEQ), view(1024, 4, SEQ)
        zh, zl = (shaped(place_r(name, at * S, S), (2, 4, SEQ)) for name, at in (("zz_high", 1), ("zz_low", 2)))

        def used_piece(eng, m):
            eng.wait_ge(piece_used, m + 1)

        def used(eng, n):
            used_piece(eng, 4 * n + 3)

        def piece_ready(pe, m):
            if m // 4 in PLAIN:
                pe.wait_ge(piece_landed[m % RING], 16 * (m // RING + 1))
            else:
                pe.wait_ge(low_made, SPLITS[m] + 1)

        def parts(lhs, rhs):
            return ((lhs[0], rhs[0]), (lhs[0], rhs[1]), (lhs[1], rhs[0]))

        def transposed(pe, inst):
            return lambda i: bank_out(pe, 4 * inst + i)

        def pe_chunk(pe, n, c, lhs, banks_free, ready=None):
            for i in range(4):
                m = 4 * n + i
                piece_ready(pe, m)
                if ready is not None:
                    ready(i)
                if i == 0 and banks_free is not None:
                    banks_free(pe, c)
                for t in range(NT):
                    tt = slice(t * P, (t + 1) * P)
                    for j in range(2):
                        k = 2 * i + j
                        if n in PLAIN:
                            pairs = ((lhs[:, k, tt], raw(m, 2, HALF)[:, j, :]),)
                        else:
                            pairs = parts([x_[:, k, tt] for x_ in lhs], (high(m, 2, HALF)[:, j, :], low(m, 2, HALF)[:, j, :]))
                        for q, (a, b) in enumerate(pairs):
                            ins = nc.tensor.matmul(psum[:, 2 * (c % 2) + t, :], a, b, start=(k == 0 and q == 0),
                                                   stop=(k == KT - 1 and q == len(pairs) - 1))
                ins.then_inc(piece_used, 1)

        def pe_linear(pe, first, chunks, lhs, banks_free=None, ready=None):
            for c in range(chunks):
                pe_chunk(pe, first + c, c, lhs, banks_free, ready if c == 0 else None)

        def pe_feature_tile(pe, m, out, ready=None):
            piece_ready(pe, m)
            for k in range(KT):
                if ready is not None and k % 2 == 0:
                    ready(k // 2)
                for q, (a, b) in enumerate(parts((high(m, KT, P)[:, k, :], low(m, KT, P)[:, k, :]), [x_[:, k, :] for x_ in xT2])):
                    ins = nc.tensor.matmul(out, a, b, start=(k == 0 and q == 0), stop=(k == KT - 1 and q == 2))
            ins.then_inc(piece_used, 1)

        xn = view(0, NT, D)
        xb = view(2 * S, KT, SEQ + 3)
        yg, xc, rg, ig, aa, th, bb_, hs = (view(i * S, KT, SEQ) for i in (4, 5, 6, 7, 8, 9, 0, 1))
        og = xc
        sp8, nsp8 = little(KT), little(KT)
        spt = [little(KT) for _ in range(5)]

        vN, kap, bet, kN = (view(i * S, NT, D) for i in (0, 1, 2, 3))
        Pd, Pi, Pp, aN, rN = (view(i * S, NT, D) for i in (4, 5, 6, 7, 8))
        gN, tmp1, tmp2, sg = view(9 * S, NT, D), view(9 * S, NT, D), view(10 * S, NT, D), view(11 * S, NT, D)
        yN = rN
        KR = view(4 * S, KT, 2, SEQ)
        bT, khT = view(6 * S, KT, SEQ), view(7 * S, KT, SEQ)
        xTs = view(XT, KT, SEQ + 1)
        dT = view(14 * S, KT, SEQ)
        xm = [view(13 * S, KT, SEQ), view(12 * S, KT, SEQ)]
        xn5 = view(4 * S, NT, D)
        lora2_sb = view(8 * S, 2, D)
        lora1_sb = view(9 * S, 2, KT, 64)
        lt = view(10 * S, 2, SEQ)
        WORK = 23040
        MN = view(10 * S, KT, 5, 64)
        M_OF, N_OF = {1: 3, 2: 0}, {0: 1, 1: 4, 2: 2}
        U = [view(WORK + 4864 * b, 4, 5, P) for b in range(2)]
        OFF = [view(WORK + 4864 * b + 2560, 2, 4, P) for b in range(2)]
        XX = [view(WORK + 4864 * b + 3584, 4, P) for b in range(2)]
        BV = [view(WORK + 4864 * b + 4096, 4, 64) for b in range(2)]
        WU = [view(WORK + 4864 * b + 4352, 4, P) for b in range(2)]
        Sg = [None] + [view(WORK + 512 * g, KT, 64) for g in range(3)]
        stmp = view(2 * S, KT, 64)
        xg = view(9 * S, KT, SEQ)
        bonus_v = row[:, 0:2, :]
        bon = little(32).rearrange("p (t h) -> p t h", t=NT)
        pc = little(32).rearrange("p (f g) -> p f g", f=KT)
        nrm = [[little(16).rearrange("p (t h) -> p t h", t=NT) for _ in range(2)] for _ in range(2)]
        mu_y, vr_y, rt_y, rs_y = (little(32).rearrange("p (t h) -> p t h", t=NT) for _ in range(4))
        eN, ge = view(4 * S, NT, D), view(5 * S, NT, D)
        pss = [little(4).rearrange("p (c t) -> p c t", c=2) for _ in range(4)]
        posted = view(6 * S, NT, D)
        pT_sb = view(7 * S, 2, SEQ)
        MIXES = ["k", "w", "a", "v", "r", "g"]
        MU = {"r": 0, "k": 1, "v": 2, "g": 3, "w": 4, "a": 5}
        mixture = {"k": xm[0], "w": view(4 * S, KT, SEQ), "a": view(5 * S, KT, SEQ), "v": xm[1], "r": xm[0], "g": xg}
        hg = view(2 * S, NT, D)

        DVE_AT = {s_: i for i, s_ in enumerate(["x0", "x1", "x2", "x3", 1, 2, 3, 4, 5, 6, 7, 8, 9, 11])}
        ACT_AT = {s_: i for i, s_ in enumerate([2, 3, 4, 6, 8, 10, 11])}
        PE_AT = {s_: i for i, s_ in enumerate(["x0", "x1", "x2", "x3"] + list(range(1, 12)))}

        def core_wait(eng, sems, table, pp, b, step):
            eng.wait_ge(sems[b], pp * len(table) + table[step] + 1)

        kD, vD, qD, gD = (view(i * S, NT, D) for i in (0, 1, 2, 3))
        kDT, qDT, oD, oD2 = view(4 * S, KT, SEQ), view(5 * S, KT, SEQ), view(6 * S, NT, D), view(7 * S, NT, D)
        rt = [view(8 * S + 256 * i, NT, 16, 8) for i in range(4)]
        sd = view(9 * S, 4, 384)
        pt2 = view(8 * S + 1024, 2, 384)
        lamb = view(9 * S + 1536, 4, 64)
        lamp = view(9 * S + 1792, 2, 64)
        lams, lame, nlam = little(2), little(2), little(1)
        LAM0 = 0.8 - 0.6 * float(np.exp(-0.3))
        rd = [little(4).rearrange("p (c t) -> p c t", c=2) for _ in range(2)]

        def mlp_order():
            yield 1, 0
            for c in range(1, 8):
                yield 1, c
                yield 2, c - 1
            yield 2, 7

        def w1_piece(m, c, f):
            return 4 * ((W_MLP0, W_MLP1)[m] + list(mlp_order()).index((1, c))) + f

        def w2_piece(m, c, f):
            return 4 * ((W_MLP0, W_MLP1)[m] + list(mlp_order()).index((2, c))) + f

        def attention_act(act, split_until):
            for hh in range(HEADS + 1):
                split_until(min(4 * W_O + 1 + hh, 4 * W_O + 8))
                if hh < HEADS:
                    act.wait_ge(mx_ready, hh + 1)
                    buf = sbuf_s[:, hh % 3, :]
                    nc.scalar.activation(buf[:, 0:256], buf[:, 0:256], ACT.Exp, bias=nmx[:, hh, 1:2],
                                         accum_out=sums[:, hh, 1:2])
                    nc.scalar.activation(buf[:, 256:384], buf[:, 256:384], ACT.Exp, bias=nmx[:, hh, 0:1],
                                         accum_out=sums[:, hh, 0:1]).then_inc(exp_done, 1)
                if hh >= 1:
                    g = hh - 1
                    act.wait_ge(pt_filled, g + 1)
                    if g >= 2:
                        act.wait_ge(pv_done, g - 1)
                    nc.scalar.copy(sbuf_pt[:, g % 2, :], psum[:, 6 + g % 2, 0:384]).then_inc(pt_copied, 1)

        def mlp_act(act, m, split_until):
            for c in range(8):
                for b in range(2):
                    split_until(w1_piece(m, c, 2 * b + 1) + 1 + AHEAD)
                    used_piece(act, w1_piece(m, c, 2 * b + 1))
                    if c >= 1:
                        act.wait_ge(z_low, 16 * m + 2 * (c - 1) + b + 1)
                    u = slice(2 * b, 2 * b + 2)
                    nc.scalar.activation(zr[:, u, :], psum[:, 4 + 2 * (c % 2) + b, :], ACT.Relu).then_inc(z_relu, 1)
                    act.wait_ge(z_relu, 16 * m + 2 * c + b + 1)
                    if c >= 2:
                        used_piece(act, w2_piece(m, c - 2, 3))
                    nc.scalar.activation(zh[:, c % 2, u, :], zr[:, u, :], ACT.Square).then_inc(z_high, 1)
            split_until(min(w2_piece(m, 7, 3) + 1 + AHEAD, 4 * W_RKVG))

        def head_outputs(dve, settle, g):
            dve.wait_ge(exp_done, 4 * g + 4)
            settle(nc.vector.reciprocal(rsum[:, 4 * g:4 * g + 4, :], sums[:, 4 * g:4 * g + 4, :]))
            dve.wait_ge(pv_done, 4 * g + 4)
            dst = on[:, :, 4 * g * HD:(4 * g + 4) * HD].rearrange("p t (h d) -> p h t d", d=HD)
            src = psum[:, g, :].rearrange("p (h t d) -> p h t d", t=NT, d=HD)
            nc.vector.tensor_tensor(dst, src, rsum[:, 4 * g:4 * g + 4, :].unsqueeze(3).broadcast_to([P, 4, NT, HD]),
                                    ALU.mult).then_inc(o_ready, 1)

        def mlp_dve(dve, settle, m, i):
            for c in range(8):
                for b in range(2):
                    i_ = 16 * m + 2 * c + b + 1
                    u = slice(2 * b, 2 * b + 2)
                    dve.wait_ge(z_relu, i_)
                    nc.vector.tensor_tensor(zz[:, u, :], zr[:, u, :], zr[:, u, :], ALU.mult).then_inc(zz_ready, 1)
                    dve.wait_ge(zz_ready, i_)
                    dve.wait_ge(z_high, i_)
                    if c >= 2:
                        used_piece(dve, w2_piece(m, c - 2, 3))
                    nc.vector.tensor_tensor(zl[:, c % 2, u, :], zz[:, u, :], read(zh[:, c % 2, u, :]),
                                            ALU.subtract).then_inc(z_low, 1)
            r2 = rstd[:, 2 * i:2 * i + 2]
            settle(nc.vector.tensor_tensor(root[:, 2 * i:2 * i + 2], r2, r2, ALU.mult))
            used_piece(dve, w2_piece(m, 7, 3))
            for t in range(NT):
                for c in range(2):
                    part = h[:, t, c * HALF:(c + 1) * HALF]
                    ins = nc.vector.scalar_tensor_tensor(out=part, in0=psum[:, 2 * t + c, :],
                                                         scalar=root[:, 2 * i + t:2 * i + t + 1], in1=part,
                                                         op0=ALU.mult, op1=ALU.add)
                ins.then_inc(h_tile0 if t == 0 else h_ready, 1)

        def mlp_pe(pe, m, inst):
            for kind, c in mlp_order():
                for f in range(4):
                    if kind == 1:
                        if c >= 2 and f % 2 == 0:
                            pe.wait_ge(z_relu, 16 * m + 2 * (c - 2) + f // 2 + 1)
                        pe_feature_tile(pe, w1_piece(m, c, f), psum[:, 4 + 2 * (c % 2) + f // 2, (f % 2) * SEQ:(f % 2 + 1) * SEQ],
                                        transposed(pe, inst) if c == 0 and f == 0 else None)
                    else:
                        n = w2_piece(m, c, f)
                        piece_ready(pe, n)
                        pe.wait_ge(z_low, 16 * m + 2 * c + f // 2 + 1)
                        for t in range(NT):
                            for half in range(2):
                                hf = slice(half * HALF, (half + 1) * HALF)
                                pairs = parts([z[:, c % 2, f, t * P:(t + 1) * P] for z in (zh, zl)], (high(n)[:, hf], low(n)[:, hf]))
                                for q, (a, b) in enumerate(pairs):
                                    ins = nc.tensor.matmul(psum[:, 2 * t + half, :], a, b, start=(c == 0 and f == 0 and q == 0),
                                                           stop=(c == 7 and f == 3 and q == 2))
                        ins.then_inc(piece_used, 1)

        def ODD_EVEN(inst):
            return [0, 2], [1, 3]

        AHEAD = 6

        TF = [(T_BET, bT), (T_KAP, KR[:, :, 0, :]), (T_RH, KR[:, :, 1, :]), (T_KH, khT)]

        block = ctx.enter_context(nc.Block())

        @block.sync
        def _(sp):
            sp.dma_start(h[:, :, :], x.rearrange("(t p) d -> p t d", p=P)).then_inc(x_landed, 16)
            sp.dma_start(ident, consts[:, 0:P]).then_inc(par_landed, 16)
            sp.dma_start(col[:, :, :], cols).then_inc(par_landed, 16)
            for m in range(4 * W_TILES):
                if m >= RING:
                    used_piece(sp, m - RING)
                sp.dma_start(ring[:, m % RING, :], w[m]).then_inc(piece_landed[m % RING], 16)
                if m == 8:
                    sp.dma_start(con[:, P:], consts[:, P:]).then_inc(con_landed, 16)
                if m == 9:
                    sp.dma_start(spread, bass.AP(relt.tensor, 0, [[0, P], [1, HEADS * 384]])).then_inc(spread_stored, 16)
                if m == 17:
                    sp.wait_ge(spread_stored, 16)
                    sp.dma_start(bias[:, :, 0:256], bass.AP(spread.tensor, 127, [[HEADS * 384 - 1, P], [384, HEADS], [1, 256]])).then_inc(bias_ready, 16)
            else:
                sp.wait_ge(h_ready, 9)
                sp.dma_start(out.rearrange("(t p) d -> p t d", p=P), h[:, :, :]).then_inc(out_stored, 16)
                sp.wait_ge(out_stored, 16)

        @block.gpsimd
        def _(pool):
            made = [0]

            def low_until(until):
                for m in range(made[0], until):
                    if m // 4 not in PLAIN:
                        pool.wait_ge(high_made, SPLITS[m] + 1)
                        nc.gpsimd.tensor_tensor(low(m), raw(m), read(high(m)), ALU.subtract).then_inc(low_made, 1)
                made[0] = until

            def load_row(r):
                pool.dma_start(row[:, r % 5, :], bass.AP(rows.tensor, r * D, [[0, P], [1, D]])).then_inc(row_landed[r % 5], 16)

            for r in range(5):
                load_row(r)
            low_until(20)
            pool.wait_ge(con_landed, 16)
            pool.wait_ge(bias_ready, 16)
            nc.gpsimd.memset(bias[0:64, :, 192:256], -1e30).then_inc(pool_step, 1)
            pool.wait_ge(pool_step, 1)
            nc.gpsimd.tensor_copy(bias[:, :, 256:384], bias[:, :, 128:256]).then_inc(mask_set, 1)
            low_until(4 * W_RKVG)
            pool.wait_ge(h_ready, 3)
            pool.dma_start(lora1_sb, lora1).then_inc(lor_landed, 16)
            pool.dma_start(lora2_sb[0:64], lora2).then_inc(lor_landed, 16)
            load_row(5)
            pool.wait_ge(hg_ready, 2)
            load_row(6)
            pool.wait_ge(lora2_read, 2)
            load_row(7)
            load_row(8)
            pool.wait_ge(decays, 3)
            for j in range(2):
                hl = slice(j * HALF, (j + 1) * HALF)
                pool.wait_ge(kk_unit, j + 1)
                nc.gpsimd.tensor_tensor(bet[:, :, hl], kap[:, :, hl], aN[:, :, hl], ALU.mult).then_inc(pool_step, 1)
                pool.wait_ge(pool_step, 2 + 2 * j)
                nc.gpsimd.tensor_tensor(bet[:, :, hl], bet[:, :, hl], Pi[:, :, hl], ALU.mult).then_inc(pool_step, 1)
                pool.wait_ge(pool_step, 3 + 2 * j)
                nc.gpsimd.tensor_tensor(kap[:, :, hl], kap[:, :, hl], Pp[:, :, hl], ALU.mult).then_inc(beta_kap, 1)
                pool.wait_ge(proj_dve, j + 1)
                nc.gpsimd.tensor_tensor(kN[:, :, hl], kN[:, :, hl], Pi[:, :, hl], ALU.mult).then_inc(khat, 1)
            pool.wait_ge(kk_unit, 2)
            load_row(9)
            pool.wait_ge(proj_act, 4)
            pool.wait_ge(bonus, 2)
            nc.gpsimd.tensor_tensor(bonus_v.rearrange("p t (h d) -> p t h d", d=HD), vN.rearrange("p t (h d) -> p t h d", d=HD),
                                    bon.unsqueeze(3).broadcast_to([P, NT, HEADS, HD]), ALU.mult).then_inc(bv_ready, 1)
            for pp in range(4):
                for b in range(2):
                    core_wait(pool, core_dve, DVE_AT, pp, b, "x3")
                    nc.gpsimd.tensor_tensor(U[b][:, :, 0, :], U[b][:, :, 1, :], ident.unsqueeze(1).broadcast_to([P, 4, P]),
                                            ALU.add).then_inc(core_pool[b], 1)
            for q in range(2):
                pool.wait_ge(xg_high, q + 1)
                u = slice(4 * q, 4 * q + 4)
                nc.gpsimd.tensor_tensor(XBL[:, u, :], xg[:, u, :], read(XBH[:, u, :]), ALU.subtract).then_inc(xg_low, 1)
                low_until(4 * W_RKVG + 26 + 6 * q)
            low_until(4 * W_PLE0)
            used(pool, W_RKVG + 7)
            pool.dma_start(pT_sb, pT[:, 0]).then_inc(lor_landed, 16)
            pool.wait_ge(y_ready, 1)
            for r in range(10, 14):
                load_row(r)
            pool.dma_start(lamb, bass.AP(lam.tensor, 0, [[0, P], [64, 4], [1, 64]])).then_inc(lam_landed, 16)
            pool.wait_ge(con_landed, 16)
            cosb = C("cos").rearrange("p (t f) -> p t f", t=NT).unsqueeze(2).broadcast_to([P, NT, 16, 8])
            sinb = C("sin").rearrange("p (t f) -> p t f", t=NT).unsqueeze(2).broadcast_to([P, NT, 16, 8])
            n = 5
            for i, (a, count) in enumerate(((kD, 2), (qD, 6))):
                low_until(4 * (W_QG if i == 0 else W_OUT_B))
                pool.wait_ge(kv_act, count)
                pool.wait_ge(kv_dve, count)
                v = a.rearrange("p t (s d) -> p t s d", d=64)
                x1, x2 = v[:, :, :, 0:8], v[:, :, :, 8:16]
                for d, s0, s1 in ((0, x1, cosb), (1, x2, sinb), (2, x2, cosb), (3, x1, sinb)):
                    ins = nc.gpsimd.tensor_tensor(rt[d], s0, s1, ALU.mult)
                ins.then_inc(pool_step, 1)
                n += 1
                pool.wait_ge(pool_step, n)
                nc.gpsimd.tensor_tensor(x1, rt[0], rt[1], ALU.subtract)
                nc.gpsimd.tensor_tensor(x2, rt[2], rt[3], ALU.add).then_inc(roped, 1)
                pool.wait_ge(roped, i + 1)
            low_until(4 * W_PLE1)
            pool.wait_ge(kv_act, 8)
            sl = ROWS.index("subln")
            pool.wait_ge(row_landed[sl % 5], 16 * (sl // 5 + 1))
            nc.gpsimd.tensor_tensor(gD, gD, row[:, sl % 5, :].unsqueeze(1).broadcast_to([P, NT, D]), ALU.mult).then_inc(gate_gain, 1)
            pool.wait_ge(od_ready, 2)
            pool.dma_start(pT_sb, pT[:, 1]).then_inc(lor_landed, 16)
            low_until(4 * W_TILES)

        @block.scalar
        def _(act):
            engines["act"] = act
            steps = [0]

            def settle(ins):
                steps[0] += 1
                ins.then_inc(act_step, 1)
                act.wait_ge(act_step, steps[0])

            def moments(i, src=h, tiles_ready=None):
                for t in range(NT):
                    if tiles_ready is not None:
                        act.wait_ge(*tiles_ready[t])
                    ins = nc.scalar.activation(junk_at(i)[:, t, :], src[:, t, :], ACT.Square, accum_out=ss[:, 2 * i + t:2 * i + t + 1])
                ins.then_inc(stat_sum, 1)
                act.wait_ge(stat_var, i + 1)
                nc.scalar.activation(root[:, 2 * i:2 * i + 2], var[:, 2 * i:2 * i + 2], ACT.Sqrt).then_inc(stat_root, 1)

            made = [0]
            LAST = 4 * W_TILES

            def split_until(until):
                for m in range(made[0], min(until, LAST)):
                    if m // 4 not in PLAIN:
                        act.wait_ge(piece_landed[m % RING], 16 * (m // RING + 1))
                        if m >= RING:
                            used_piece(act, m - RING)
                        nc.scalar.copy(high(m), raw(m)).then_inc(high_made, 1)
                made[0] = max(made[0], until)

            def split_for(n):
                split_until(4 * n + 4 + AHEAD)

            act.wait_ge(x_landed, 16)
            act.wait_ge(par_landed, 32)
            evacuate_high(act, T_H0, (XH, c8("norm_mix0")), between=lambda b: split_until(b + 1))
            moments(0)
            for c, (dst, half) in enumerate(QKV):
                split_for(W_QKV + c)
                used(act, W_QKV + c)
                act.wait_ge(rstd_ready, 1)
                nc.scalar.activation(dst[:, 0, half * HALF:(half + 1) * HALF], psum[:, 2 * (c % 2), :], ACT.Copy,
                                     scale=rstd[:, 0:1]).then_inc(qkv_act, 1)
            for inst, dst in ((T_Q, qT), (T_K, kT)):
                for b in (0, 2):
                    evacuate(act, inst, b, dst)
            attention_act(act, split_until)
            evacuate_high(act, T_O, (XH, None))
            split_for(W_O + 1)
            act.wait_ge(h_ready, 1)
            evacuate_high(act, T_H1, (XH, c8("norm_mlp0")))
            moments(1)
            act.wait_ge(decay_part, 1)
            nc.scalar.activation(spt[1], spt[0], ACT.Exp, scale=-1.0).then_inc(decay_part, 1)
            act.wait_ge(decay_part, 3)
            nc.scalar.activation(spt[3], spt[2], ACT.Ln).then_inc(decay_part, 1)
            mlp_act(act, 0, split_until)

            moments(2, tiles_ready=((h_tile0, 1), (h_ready, 2)))
            evacuate_high(act, T_N2, (XH, c8("norm_mix1")))
            split_until(4 * W_INY + 4)
            for i in range(4):
                used_piece(act, 4 * W_GATES + i)
                for j in range(2):
                    f = 2 * i + j
                    nc.scalar.activation(rg[:, f, :], psum[:, 4 + i % 2, j * SEQ:(j + 1) * SEQ], ACT.Sigmoid,
                                         bias=c8("b_ga")[:, f:f + 1])
                    ins = nc.scalar.activation(ig[:, f, :], psum[:, 6 + i % 2, j * SEQ:(j + 1) * SEQ], ACT.Sigmoid,
                                               bias=c8("b_gx")[:, f:f + 1])
                ins.then_inc(gates_read, 1)
                split_until(4 * W_INY + 5 + i)
            act.wait_ge(gates_read, 4)
            act.wait_ge(decay_ready, 1)
            for q in range(2):
                u = slice(4 * q, 4 * q + 4)
                for f in range(4 * q, 4 * q + 4):
                    nc.scalar.activation(aa[:, f, :], rg[:, f, :], ACT.Exp, scale=nsp8[:, f:f + 1])
                for f in range(4 * q, 4 * q + 4):
                    ins = nc.scalar.activation(th[:, f, :], rg[:, f, :], ACT.Tanh, scale=sp8[:, f:f + 1])
                settle(ins)
                nc.scalar.activation(bb_[:, u, :], aa[:, u, :], ACT.Square).then_inc(g_ready, 1)
            for q in range(2):
                act.wait_ge(m2_ready, q + 1)
                nc.scalar.activation(th[:, 4 * q:4 * q + 4, :], th[:, 4 * q:4 * q + 4, :], ACT.Sqrt).then_inc(m_ready, 1)
            for i in range(4):
                split_until(4 * W_RO + 2 * i)
                used_piece(act, 4 * W_INY + 2 * i + 1)
                for j in range(2):
                    f = 2 * i + j
                    ins = nc.scalar.activation(yg[:, f, :], psum[:, i, j * SEQ:(j + 1) * SEQ], ACT.Gelu_apprx_tanh,
                                               bias=c8("b_in_y")[:, f:f + 1])
                ins.then_inc(y_read, 1)
                if i >= 2:
                    q = i - 2
                    act.wait_ge(o_ready, 5 + q)
                    u = slice(4 * q, 4 * q + 4)
                    nc.scalar.copy(XBH[:, u, :], og[:, u, :]).then_inc(og_high, 1)
            split_until(4 * W_RO + 8)
            split_for(W_RO + 1)
            act.wait_ge(h_ready, 3)
            evacuate_high(act, T_H3, (XH, c8("norm_mlp1")))
            moments(3)
            mlp_act(act, 1, split_until)
            for i, src in ((4, h), (5, hg)):
                for t in range(NT):
                    if i == 4:
                        act.wait_ge(*((h_tile0, 2), (h_ready, 4))[t])
                    else:
                        act.wait_ge(hg_ready, t + 1)
                    ins = nc.scalar.activation(view((i + 1) * S, NT, D)[:, t, :], src[:, t, :], ACT.Square,
                                               accum_out=ss[:, 2 * i + t:2 * i + t + 1])
                ins.then_inc(stat_sum, 1)
            for i in (4, 5):
                act.wait_ge(stat_var, i + 1)
                nc.scalar.activation(root[:, 2 * i:2 * i + 2], var[:, 2 * i:2 * i + 2], ACT.Sqrt).then_inc(stat_root, 1)

            for b in ODD_EVEN(T_N5)[0]:
                evacuate(act, T_N5, b, xTs[:, :, 1:SEQ + 1], c8("norm_pre0"))

            def pair_out(c):
                return psum[:, 2 * (c % 2):2 * (c % 2) + 2, :]

            def projected(c, dst):
                used(act, W_RKVG + c)
                nc.scalar.copy(dst[:, :, (c % 2) * HALF:(c % 2 + 1) * HALF], pair_out(c)).then_inc(proj_act, 1)

            def key_norm(j):
                hl = slice(j * HALF, (j + 1) * HALF)
                act.wait_ge(kk_raw, j + 1)
                nc.scalar.activation(tmp1[:, :, hl], kap[:, :, hl], ACT.Square).then_inc(kk_sq, 1)
                act.wait_ge(kk_var, j + 1)
                nc.scalar.activation(nrm[j][1], nrm[j][0], ACT.Sqrt).then_inc(kk_root, 1)

            projected(0, kN)
            act.wait_ge(lora_filled, 1)
            nc.scalar.activation(lt[0:64, 0, :], psum[0:64, 4, 0:SEQ], ACT.Tanh).then_inc(lora_out, 1)
            act.wait_ge(lora_filled, 2)
            nc.scalar.copy(lt[0:64, 1, :], psum[0:64, 5, 0:SEQ]).then_inc(lora_out, 1)
            projected(1, kN)
            act.wait_ge(lora2_read, 1)
            nc.scalar.activation(sg, sg, ACT.Sigmoid).then_inc(sig_ready, 1)
            projected(2, vN)
            act.wait_ge(lora2_read, 2)
            nc.scalar.activation(aN, aN, ACT.Sigmoid).then_inc(sig_ready, 1)
            key_norm(0)
            projected(3, vN)
            act.wait_ge(cum_prev, 1)
            cum = psum[:, 4:8, :].rearrange("p (t q) n -> p t (q n)", t=NT)
            CD = float(np.exp(-0.5))
            nc.scalar.activation(Pd, cum, ACT.Exp, scale=-CD).then_inc(decays, 1)
            nc.scalar.activation(Pi, cum, ACT.Exp, scale=CD).then_inc(decays, 1)
            nc.scalar.activation(Pp, Pp, ACT.Exp, scale=-CD).then_inc(decays, 1)
            act.wait_ge(last_filled, 1)
            nc.scalar.copy(pc.rearrange("p f g -> p (f g)"), psum[:, 4, 0:32]).then_inc(last_read, 1)
            key_norm(1)
            for inst, dst in TF:
                for b in ODD_EVEN(inst)[0]:
                    evacuate(act, inst, b, dst)
            for pp in range(4):
                for s_ in (2, 3, 4, 6, 8, 10, 11):
                    for b in range(2):
                        f, B = 2 * pp + b, 4 * b
                        core_wait(act, core_filled, PE_AT, pp, b, s_)
                        four = lambda k: psum[:, B + k, :].rearrange("p (q n) -> p q n", q=4)
                        if s_ == 2:
                            act.wait_ge(core_pool[b], pp + 1)
                            nc.scalar.copy(U[b][:, :, 1, :], four(1))
                            ins = nc.scalar.copy(BV[b], psum[:, B + 3, 0:256].rearrange("p (q n) -> p q n", q=4))
                        elif s_ == 3:
                            nc.scalar.copy(U[b][:, :, 1, :], four(1))
                            ins = nc.scalar.copy(XX[b], four(2))
                        elif s_ == 4:
                            ins = nc.scalar.copy(XX[b], four(2))
                        elif s_ in (6, 8):
                            ins = nc.scalar.copy(XX[b], four(1))
                        elif s_ == 10:
                            ins = nc.scalar.activation(WU[b], four(1), ACT.Copy, scale=-1.0)
                        else:
                            nc.scalar.copy(MN[:, f, 0:3, :].rearrange("p g i -> p (g i)"), psum[:, B + 2, 0:192])
                            nc.scalar.copy(MN[:, f, 3:5, :].rearrange("p g i -> p (g i)"), psum[:, B + 3, 0:128])
                            dst = yN[:, :, 2 * f * HD:(2 * f + 2) * HD].rearrange("p t (h d) -> p h t d", d=HD)
                            ins = nc.scalar.copy(dst, psum[:, B, 0:256].rearrange("p (h t d) -> p h t d", h=2, t=NT))
                        ins.then_inc(core_act[b], 1)
            core_wait(act, core_filled, PE_AT, 3, 0, 11)
            core_wait(act, core_filled, PE_AT, 3, 1, 11)
            for q in range(2):
                u = slice(4 * q, 4 * q + 4)
                nc.scalar.copy(XBH[:, u, :], xg[:, u, :]).then_inc(xg_high, 1)
                split_until(4 * W_RKVG + 26 + 6 * q)
            act.wait_ge(y_cent, 1)
            nc.scalar.activation(bet, yN, ACT.Square).then_inc(y_sq, 1)
            act.wait_ge(y_var, 1)
            nc.scalar.activation(rt_y, vr_y, ACT.Sqrt).then_inc(y_root, 1)
            for j in range(2):
                split_for(W_RKVG + 6 + j)
                used(act, W_RKVG + 6 + j)
                nc.scalar.activation(gN[:, :, j * HALF:(j + 1) * HALF], pair_out(j), ACT.Silu).then_inc(proj_act, 1)

            def post_root(i):
                act.wait_ge(stat_var, i + 1)
                nc.scalar.activation(root[:, 2 * i:2 * i + 2], var[:, 2 * i:2 * i + 2], ACT.Sqrt).then_inc(stat_root, 1)

            def square_half(src, c, t, e):
                nc.scalar.activation(view(8 * S, NT, D)[:, t, c * HALF:(c + 1) * HALF], src, ACT.Square,
                                     accum_out=pss[e][:, c, t:t + 1]).then_inc(part_sq, 1)

            def out_norm(i, first, e_n):
                for c in range(2):
                    split_for(first + c)
                    used(act, first + c)
                    square_half(pair_out(c)[:, 0], c, 0, 2 * e_n)
                    act.wait_ge(part_gain, 4 * e_n + 2 * c + 1)
                    square_half(pair_out(c)[:, 1], c, 1, 2 * e_n)
                post_root(i)

            def embed(i, tile, e_n, T):
                split_for(tile)
                used(act, tile)
                for c in range(2):
                    ins = nc.scalar.copy(eN[:, :, c * HALF:(c + 1) * HALF], pair_out(c))
                ins.then_inc(e_act, 1)
                evacuate_high(act, T, (XH, None))
                for c in range(2):
                    split_for(tile + 1 + c)
                    used(act, tile + 1 + c)
                    hl = slice(c * HALF, (c + 1) * HALF)
                    nc.scalar.activation(ge[:, :, hl], pair_out(c), ACT.Sigmoid).then_inc(gate_act, 1)
                    act.wait_ge(ge_ready, 2 * e_n + c + 1)
                    for t in range(NT):
                        square_half(ge[:, t, hl], c, t, 2 * e_n + 1)
                post_root(i)

            evacuate_high(act, T_YA, (XH, None))
            out_norm(6, W_OUT_A, 0)
            embed(7, W_PLE0, 0, T_H6)

            act.wait_ge(h_ready, 7)
            evacuate_high(act, T_H7, (XBH, c8("kv_norm")), (XH, c8("norm_pre1")))
            moments(8)
            act.wait_ge(lam_sum, 1)
            nc.scalar.activation(lame, lams, ACT.Exp).then_inc(lam_exp, 1)
            act.wait_ge(rstd_ready, 9)
            for c, dst in enumerate((kD, vD, qD, gD)):
                for j in range(2):
                    split_for(W_KV + 2 * c + j)
                    used(act, W_KV + 2 * c + j)
                    hl = slice(j * HALF, (j + 1) * HALF)
                    if c < 3:
                        ins = nc.scalar.activation(dst[:, 0, hl], pair_out(j)[:, 0], ACT.Copy, scale=rstd[:, 16:17])
                    else:
                        for t in range(NT):
                            ins = nc.scalar.activation(dst[:, t, hl], pair_out(j)[:, t], ACT.Silu,
                                                       scale=rstd[:, 16 + t:17 + t])
                    ins.then_inc(kv_act, 1)
            for inst, dst in ((T_KB, kDT), (T_QB, qDT)):
                for b in ODD_EVEN(inst)[0]:
                    evacuate(act, inst, b, dst)
            def heads_square(g):
                act.wait_ge(pv_done, HEADS + 4 * g + 4)
                dst = oD2[:, :, g * HALF:(g + 1) * HALF].rearrange("p t (h d) -> p h t d", d=P)
                src = psum[:, 2 * g:2 * g + 2, :].rearrange("p b (h t d) -> p (b h) t d", h=2, t=NT)
                nc.scalar.activation(dst, src, ACT.Square).then_inc(o_sq, 1)

            def heads_root(g):
                act.wait_ge(o_var, g + 1)
                u = slice(4 * g, 4 * g + 4)
                nc.scalar.activation(rt_y[:, :, u], vr_y[:, :, u], ACT.Sqrt).then_inc(o_root, 1)

            for hh in range(HEADS + 2):
                split_until(min(4 * W_OUT_B + 6 + hh, 4 * W_OUT_B + 8))
                if hh == 14:
                    heads_square(0)
                if hh < HEADS:
                    act.wait_ge(mx_ready, HEADS + hh + 1)
                    buf = sd[:, hh % 4, :]
                    nc.scalar.activation(buf[:, 0:256], buf[:, 0:256], ACT.Exp, bias=nmx[:, hh, 1:2],
                                         accum_out=sums[:, hh, 1:2])
                    nc.scalar.activation(buf[:, 256:384], buf[:, 256:384], ACT.Exp, bias=nmx[:, hh, 0:1],
                                         accum_out=sums[:, hh, 0:1]).then_inc(exp_done, 1)
                if hh >= 3 and hh % 2 == 1:
                    g = (hh - 3) // 2
                    act.wait_ge(pt_filled, HEADS + g + 1)
                    if g >= 2:
                        act.wait_ge(pv_done, HEADS + g - 1)
                    nc.scalar.copy(pt2[:, g % 2, :], psum[:, 6 + g % 2, 0:384]).then_inc(pt_copied, 1)
            heads_root(0)
            heads_square(1)
            heads_root(1)
            evacuate_high(act, T_OB, (XH, None))
            out_norm(9, W_OUT_B, 1)
            embed(10, W_PLE1, 1, T_H8)

        @block.vector
        def _(dve):
            engines["dve"] = dve
            steps = [0]

            def settle(ins):
                steps[0] += 1
                ins.then_inc(dve_step, 1)
                dve.wait_ge(dve_step, steps[0])

            def rms(i, n=D, eps=EPS):
                dve.wait_ge(stat_sum, i + 1 if i < 6 else i - 1)
                nc.vector.tensor_scalar(var[:, 2 * i:2 * i + 2], ss[:, 2 * i:2 * i + 2], 1.0 / n, eps, ALU.mult,
                                        ALU.add).then_inc(stat_var, 1)
                dve.wait_ge(stat_root, i + 1)
                nc.vector.reciprocal(rstd[:, 2 * i:2 * i + 2], root[:, 2 * i:2 * i + 2]).then_inc(rstd_ready, 1)
                dve.wait_ge(rstd_ready, i + 1)

            def residual(first, chunks=2):
                for c in range(chunks):
                    used(dve, first + c)
                    for t in range(NT):
                        part = h[:, t, c * HALF:(c + 1) * HALF]
                        ins = nc.vector.tensor_tensor(part, psum[:, 2 * (c % 2) + t, :], part, ALU.add)
                    ins.then_inc(h_half if c == 0 else h_ready, 1)

            dve.wait_ge(par_landed, 32)
            evacuate_low(dve, T_H0, (XH, XL, c8("norm_mix0")))
            rms(0)
            for c, (dst, half) in enumerate(QKV):
                used(dve, W_QKV + c)
                nc.vector.tensor_scalar(dst[:, 1, half * HALF:(half + 1) * HALF], psum[:, 2 * (c % 2) + 1, :],
                                        rstd[:, 1:2], None, ALU.mult).then_inc(qkv_dve, 1)
            for inst, dst in ((T_Q, qT), (T_K, kT)):
                for b in (1, 3):
                    evacuate(dve, inst, b, dst)
            dve.wait_ge(con_landed, 16)
            dve.wait_ge(mask_set, 1)
            for hh in range(HEADS + 3):
                if hh < HEADS:
                    dve.wait_ge(sc_done, hh + 1)
                    if hh >= 3:
                        dve.wait_ge(pt_filled, hh - 2)
                    buf = sbuf_s[:, hh % 3, :]
                    nc.vector.scalar_tensor_tensor(out=buf, in0=psum[:, 4 + hh % 2, 0:384], scalar=HD ** -0.5,
                                                   in1=bias[:, hh, :], op0=ALU.mult, op1=ALU.add).then_inc(sc_read, 1)
                    dve.wait_ge(sc_read, hh + 1)
                    nc.vector.tensor_reduce(nmx[:, hh, 1:2], buf[:, 0:256], AX.X, ALU.max, negate=True)
                    nc.vector.tensor_reduce(nmx[:, hh, 0:1], buf[:, 256:384], AX.X, ALU.max, negate=True).then_inc(mx_ready, 1)
                if hh >= 6 and hh % 4 == 2:
                    head_outputs(dve, settle, (hh - 6) // 4)
            evacuate_low(dve, T_O, (XH, XL, None))
            residual(W_O)
            evacuate_low(dve, T_H1, (XH, XL, c8("norm_mlp0")))
            rms(1)
            p_ = c8("a_param")
            settle(nc.vector.tensor_scalar(spt[1], p_, -1.0, None, ALU.mult))
            nc.vector.tensor_tensor(spt[0], p_, spt[1], ALU.max).then_inc(decay_part, 1)
            dve.wait_ge(decay_part, 2)
            nc.vector.tensor_scalar(spt[2], spt[1], 1.0, None, ALU.add).then_inc(decay_part, 1)
            dve.wait_ge(decay_part, 4)
            settle(nc.vector.tensor_scalar(spt[2], spt[2], -1.0, None, ALU.add))
            settle(nc.vector.tensor_scalar(spt[4], spt[2], 0.0, None, ALU.is_equal))
            settle(nc.vector.tensor_tensor(spt[2], spt[2], spt[4], ALU.add))
            settle(nc.vector.reciprocal(spt[2], spt[2]))
            settle(nc.vector.tensor_tensor(spt[3], spt[3], spt[2], ALU.mult))
            settle(nc.vector.tensor_tensor(spt[3], spt[3], spt[4], ALU.add))
            settle(nc.vector.tensor_tensor(spt[3], spt[3], spt[1], ALU.mult))
            settle(nc.vector.tensor_scalar(spt[4], p_, -1.0, 0.0, ALU.mult, ALU.max))
            settle(nc.vector.tensor_tensor(spt[3], spt[3], spt[4], ALU.add))
            nc.vector.tensor_scalar(sp8, spt[3], 8.0, None, ALU.mult)
            nc.vector.tensor_scalar(nsp8, spt[3], -8.0, None, ALU.mult).then_inc(decay_ready, 1)
            mlp_dve(dve, settle, 0, 1)

            def normed(dst, i):
                for t in range(NT):
                    ins = nc.vector.tensor_scalar(dst[:, t, :], h[:, t, :], rstd[:, 2 * i + t:2 * i + t + 1], None, ALU.mult)
                ins.then_inc(xn_ready, 1)

            def row_of(name):
                r = ROWS.index(name)
                dve.wait_ge(row_landed[r % 5], 16 * (r // 5 + 1))
                return row[:, r % 5, :]

            rms(2)
            normed(xn, 2)
            nc.vector.memset(xb[:, :, 0:3], 0.0).then_inc(pad_zero, 1)
            bo = row_of("b_o")
            dve.wait_ge(xn_ready, 1)
            for t in range(NT):
                settle(nc.vector.tensor_tensor(h[:, t, :], h[:, t, :], bo, ALU.add))
            evacuate_low(dve, T_N2, (XH, XL, c8("norm_mix1")))
            dve.wait_ge(pad_zero, 1)
            for i in range(4):
                used_piece(dve, 4 * W_INX + 2 * i + 1)
                for j in range(2):
                    f = 2 * i + j
                    ins = nc.vector.tensor_scalar(xb[:, f, 3:], psum[:, i, j * SEQ:(j + 1) * SEQ],
                                                  c8("b_in_x")[:, f:f + 1], None, ALU.add)
                ins.then_inc(x_read, 1)
                dve.wait_ge(x_read, i + 1)
                for tap in range(4):
                    wc = c8(f"conv_w{tap}")
                    for j in range(2):
                        f = 2 * i + j
                        src, o = xb[:, f, tap:tap + SEQ], xc[:, f, :]
                        if tap == 0:
                            ins = nc.vector.tensor_scalar(o, src, wc[:, f:f + 1], c8("conv_b")[:, f:f + 1], ALU.mult, ALU.add)
                        else:
                            ins = nc.vector.scalar_tensor_tensor(out=o, in0=src, scalar=wc[:, f:f + 1], in1=o,
                                                                 op0=ALU.mult, op1=ALU.add)
                    if tap < 3:
                        settle(ins)
                ins.then_inc(xc_ready, 1)

            def og_low_part(q):
                u = slice(4 * q, 4 * q + 4)
                dve.wait_ge(og_high, q + 1)
                nc.vector.tensor_tensor(XBL[:, u, :], og[:, u, :], read(XBH[:, u, :]), ALU.subtract).then_inc(og_low, 1)

            dve.wait_ge(xc_ready, 4)
            dve.wait_ge(gates_read, 4)
            for q in range(2):
                u = slice(4 * q, 4 * q + 4)
                nc.vector.tensor_tensor(ig[:, u, :], ig[:, u, :], xc[:, u, :], ALU.mult)
                dve.wait_ge(g_ready, q + 1)
                nc.vector.scalar_tensor_tensor(out=th[:, u, :], in0=bb_[:, u, :], scalar=1.0, in1=th[:, u, :],
                                               op0=ALU.add, op1=ALU.mult).then_inc(m2_ready, 1)
            for q in range(2):
                u = slice(4 * q, 4 * q + 4)
                dve.wait_ge(m_ready, q + 1)
                settle(nc.vector.tensor_tensor(bb_[:, u, :], th[:, u, :], ig[:, u, :], ALU.mult))
                for f in range(4 * q, 4 * q + 4):
                    ins = nc.vector.tensor_tensor_scan(hs[:, f, :], aa[:, f, :], bb_[:, f, :], 0.0, ALU.mult, ALU.add)
                settle(ins)
            for q in range(2):
                u = slice(4 * q, 4 * q + 4)
                dve.wait_ge(y_read, 2 * q + 2)
                nc.vector.tensor_tensor(og[:, u, :], hs[:, u, :], yg[:, u, :], ALU.mult).then_inc(o_ready, 1)
                og_low_part(q)
            residual(W_RO)
            evacuate_low(dve, T_H3, (XH, XL, c8("norm_mlp1")))
            rms(3)
            mlp_dve(dve, settle, 1, 3)
            nf = row_of("norm_final")
            dve.wait_ge(h_ready, 4)
            for t in range(NT):
                nc.vector.tensor_tensor(hg[:, t, :], h[:, t, :], nf, ALU.mult).then_inc(hg_ready, 1)
            rms(4)
            r4, r5, r45 = rstd[:, 8:10], rstd[:, 10:12], var[:, 8:10]
            dve.wait_ge(stat_sum, 6)
            settle(nc.vector.tensor_tensor(r45, r4, r4, ALU.mult))
            settle(nc.vector.tensor_tensor(r45, r45, ss[:, 10:12], ALU.mult))
            nc.vector.tensor_scalar(var[:, 10:12], r45, 1.0 / D, EPS, ALU.mult, ALU.add).then_inc(stat_var, 1)
            dve.wait_ge(stat_root, 6)
            nc.vector.reciprocal(r5, root[:, 10:12]).then_inc(rstd_ready, 1)
            dve.wait_ge(rstd_ready, 6)
            settle(nc.vector.tensor_tensor(r45, r4, r5, ALU.mult))

            for t in range(NT):
                ins = nc.vector.tensor_scalar(xn5[:, t, :], hg[:, t, :], r45[:, t:t + 1], None, ALU.mult)
            ins.then_inc(xn_ready, 1)
            settle(nc.vector.memset(xTs[:, :, 0:1], 0.0))

            def mix(i):
                name = MIXES[i]
                if name == "r":
                    used(dve, W_RKVG + 1)
                if name == "g":
                    dve.wait_ge(bonus, 2)
                for k in range(KT):
                    if i == 0 and k % 2 == 0:
                        b = k // 2
                        if b in ODD_EVEN(T_N5)[1]:
                            evacuate(dve, T_N5, b, xTs[:, :, 1:SEQ + 1], c8("norm_pre0"))
                        bank_out(dve, 4 * T_N5 + b)
                        settle(nc.vector.tensor_tensor(dT[:, k:k + 2, :], xTs[:, k:k + 2, 0:SEQ], xTs[:, k:k + 2, 1:SEQ + 1],
                                                       ALU.subtract))
                    ins = nc.vector.scalar_tensor_tensor(out=mixture[name][:, k, :], in0=dT[:, k, :],
                                                         scalar=c8(f"mu{MU[name]}")[:, k:k + 1],
                                                         in1=xTs[:, k, 1:SEQ + 1], op0=ALU.mult, op1=ALU.add)
                    if k % 2 == 1:
                        ins.then_inc(mix_ready, 1)

            mix(0)
            mix(1)
            mix(2)
            for t in range(NT):
                ins = nc.vector.tensor_scalar(h[:, t, :], hg[:, t, :], r4[:, t:t + 1], None, ALU.mult)
            ins.then_inc(h_ready, 1)
            mix(3)
            four_banks = psum[:, 4:8, :].rearrange("p (t q) n -> p t (q n)", t=NT)
            for i, (dst, name) in enumerate(((sg, "w0"), (aN, "a0"))):
                r_ = row_of(name)
                dve.wait_ge(lora2_filled, i + 1)
                nc.vector.tensor_tensor(dst, four_banks, r_.unsqueeze(1).broadcast_to([P, NT, D]), ALU.add).then_inc(lora2_read, 1)
                if i == 0:
                    mix(4)

            def previous_sums():
                dve.wait_ge(cum_filled, 1)
                nc.vector.tensor_tensor(Pp, four_banks, sg, ALU.subtract).then_inc(cum_prev, 1)

            for j in range(2):
                hl = slice(j * HALF, (j + 1) * HALF)
                over = lambda r_: r_[:, hl].unsqueeze(1).broadcast_to([P, NT, HALF])
                heads = lambda a: a[:, :, hl].rearrange("p t (h d) -> p t h d", d=HD)
                per_head = lambda a: a.unsqueeze(3).broadcast_to([P, NT, 8, HD])
                dve.wait_ge(proj_act, j + 1)
                nc.vector.tensor_tensor(kap[:, :, hl], kN[:, :, hl], over(row_of("k_k")), ALU.mult).then_inc(kk_raw, 1)
                dve.wait_ge(sig_ready, 2)
                for t in range(NT):
                    ins = nc.vector.scalar_tensor_tensor(out=tmp2[:, t, hl], in0=aN[:, t, hl], scalar=1.0,
                                                         in1=row_of("k_a")[:, hl], op0=ALU.subtract, op1=ALU.mult)
                settle(ins)
                nc.vector.scalar_tensor_tensor(out=kN[:, :, hl], in0=tmp2[:, :, hl], scalar=1.0, in1=kN[:, :, hl],
                                               op0=ALU.add, op1=ALU.mult).then_inc(k_ready, 1)
                dve.wait_ge(kk_sq, j + 1)
                settle(nc.vector.tensor_reduce(nrm[j][0], heads(tmp1), AX.X, ALU.add))
                nc.vector.tensor_scalar(nrm[j][0], nrm[j][0], 1e-24, None, ALU.max).then_inc(kk_var, 1)
                dve.wait_ge(kk_root, j + 1)
                settle(nc.vector.reciprocal(nrm[j][1], nrm[j][1]))
                dve.wait_ge(kk_raw, j + 1)
                nc.vector.tensor_tensor(heads(kap), heads(kap), per_head(nrm[j][1]), ALU.mult).then_inc(kk_unit, 1)
                if j == 0:
                    previous_sums()
            for j in range(2):
                hl = slice(j * HALF, (j + 1) * HALF)
                heads = lambda a: a[:, :, hl].rearrange("p t (h d) -> p t h d", d=HD)
                used(dve, W_RKVG + 4 + j)
                pr = psum[:, 2 * j:2 * j + 2, :]
                dve.wait_ge(decays, 3)
                dve.wait_ge(k_ready, j + 1)
                nc.vector.tensor_tensor(rN[:, :, hl], pr, Pd[:, :, hl], ALU.mult)
                nc.vector.tensor_tensor(tmp1[:, :, hl], pr, kN[:, :, hl], ALU.mult).then_inc(proj_dve, 1)
                dve.wait_ge(proj_dve, j + 1)
                settle(nc.vector.tensor_tensor(tmp1[:, :, hl], tmp1[:, :, hl],
                                               row_of("r_k")[:, hl].unsqueeze(1).broadcast_to([P, NT, HALF]), ALU.mult))
                nc.vector.tensor_reduce(bon[:, :, 8 * j:8 * j + 8], heads(tmp1), AX.X, ALU.add).then_inc(bonus, 1)
            mix(5)
            for inst, dst in TF:
                for b in ODD_EVEN(inst)[1]:
                    evacuate(dve, inst, b, dst)

            for pp in range(4):
                for s_ in ("x0", "x1", "x2", "x3", 1, 2, 3, 4, 5, 6, 7, 8, 9, 11):
                    for b in range(2):
                        f, B = 2 * pp + b, 4 * b
                        core_wait(dve, core_filled, PE_AT, pp, b, s_)
                        four = lambda k: psum[:, B + k, :].rearrange("p (q n) -> p q n", q=4)
                        Z = U[b][:, :, 0, :]
                        if isinstance(s_, str):
                            q = int(s_[1])
                            ins = nc.vector.tensor_tensor(U[b][:, q, 1:5, :].rearrange("p a n -> p (a n)"), psum[:, B + q, :],
                                                          C("mask_x"), ALU.mult)
                        elif s_ == 1:
                            src = psum[:, B:B + 2, 0:256].rearrange("p h (t n) -> p h t n", t=2)
                            for m, dst in enumerate((XX[b], OFF[b][:, 0], OFF[b][:, 1])):
                                mk = C("mask_a")[:, m * P:(m + 1) * P].unsqueeze(1).unsqueeze(1).broadcast_to([P, 2, 2, P])
                                ins = nc.vector.tensor_tensor(dst.rearrange("p (h t) n -> p h t n", h=2), src, mk, ALU.mult)
                        elif s_ == 2:
                            ins = nc.vector.tensor_copy(XX[b], four(2))
                        elif s_ == 3:
                            dve.wait_ge(core_pool[b], pp + 1)
                            ins = nc.vector.tensor_tensor(Z, four(0), Z, ALU.add)
                        elif s_ == 4:
                            ins = nc.vector.tensor_tensor(Z, four(3), Z, ALU.add)
                        elif s_ == 5:
                            ins = nc.vector.tensor_tensor(Z, four(0), Z, ALU.add)
                        elif s_ in (6, 8):
                            ins = nc.vector.tensor_copy(U[b][:, :, 1, :], four(2))
                        elif s_ in (7, 9):
                            ins = nc.vector.tensor_tensor(Z, Z, four(0), ALU.subtract)
                        else:
                            ins = nc.vector.tensor_tensor(KR[:, f, 1, :], psum[:, B + 1, 0:256], KR[:, f, 1, :], ALU.add)
                        ins.then_inc(core_dve[b], 1)
            for b in range(2):
                core_wait(dve, core_act, ACT_AT, 3, b, 11)
                core_wait(dve, core_dve, DVE_AT, 3, b, 11)
            dve.wait_ge(last_read, 1)
            pcg = lambda g: pc[:, :, g:g + 1].broadcast_to([P, KT, 64])
            nc.vector.tensor_tensor(Sg[1], MN[:, :, N_OF[0], :], pcg(0), ALU.mult).then_inc(state_ready, 1)
            for g in (1, 2):
                dve.wait_ge(state_filled, g)
                for p0 in (0, HD):
                    hp = slice(p0, p0 + HD)
                    src = psum[hp, 4 + 2 * (g - 1) + p0 // HD, :].rearrange("p (f n) -> p f n", f=KT)
                    ins = nc.vector.tensor_tensor(stmp[hp], src, MN[hp, :, N_OF[g], :], ALU.add)
                settle(ins)
                nc.vector.tensor_tensor(Sg[g + 1], stmp, pcg(g), ALU.mult).then_inc(state_ready, 1)
            dve.wait_ge(ys_filled, 1)
            for par in range(2):
                for t, r_ in ((0, slice(64, P)), (1, slice(0, P))):
                    part = yN[r_, t, :].rearrange("p (f c d) -> p f c d", c=2, d=HD)[:, :, par]
                    ins = nc.vector.tensor_tensor(part, part, psum[r_, 4 + 2 * t + par, :].rearrange("p (f d) -> p f d", f=KT), ALU.add)
            settle(ins)
            yh = yN.rearrange("p t (h d) -> p t h d", d=HD)
            ph = lambda a: a.unsqueeze(3).broadcast_to([P, NT, HEADS, HD])
            settle(nc.vector.tensor_reduce(mu_y, yh, AX.X, ALU.add))
            settle(nc.vector.tensor_scalar(mu_y, mu_y, 1.0 / HD, None, ALU.mult))
            nc.vector.tensor_tensor(yh, yh, ph(mu_y), ALU.subtract).then_inc(y_cent, 1)
            dve.wait_ge(y_sq, 1)
            settle(nc.vector.tensor_reduce(vr_y, bet.rearrange("p t (h d) -> p t h d", d=HD), AX.X, ALU.add))
            nc.vector.tensor_scalar(vr_y, vr_y, 1.0 / HD, 64e-5, ALU.mult, ALU.add).then_inc(y_var, 1)
            dve.wait_ge(y_root, 1)
            settle(nc.vector.reciprocal(rs_y, rt_y))
            settle(nc.vector.tensor_tensor(yh, yh, ph(rs_y), ALU.mult))
            both = lambda r_: r_.unsqueeze(1).broadcast_to([P, NT, D])
            settle(nc.vector.tensor_tensor(yN, yN, both(row_of("lnx_g")), ALU.mult))
            settle(nc.vector.tensor_tensor(yN, yN, both(row_of("lnx_b")), ALU.add))
            dve.wait_ge(bv_ready, 1)
            settle(nc.vector.tensor_tensor(yN, yN, bonus_v, ALU.add))
            dve.wait_ge(proj_act, 6)
            nc.vector.tensor_tensor(yN, yN, gN, ALU.mult).then_inc(y_ready, 1)

            def add_normed(i, e):
                dve.wait_ge(part_sq, 4 * e + 4)
                rows2 = slice(2 * i, 2 * i + 2)
                settle(nc.vector.tensor_tensor(ss[:, rows2], pss[e][:, 0, :], pss[e][:, 1, :], ALU.add))
                nc.vector.tensor_scalar(var[:, rows2], ss[:, rows2], 1.0 / D, EPS, ALU.mult, ALU.add).then_inc(stat_var, 1)
                dve.wait_ge(stat_root, i + 1)
                nc.vector.reciprocal(rstd[:, rows2], root[:, rows2]).then_inc(rstd_ready, 1)
                dve.wait_ge(rstd_ready, i + 1)
                for c in range(2):
                    hl = slice(c * HALF, (c + 1) * HALF)
                    for t in range(NT):
                        ins = nc.vector.scalar_tensor_tensor(out=h[:, t, hl], in0=posted[:, t, hl],
                                                             scalar=rstd[:, 2 * i + t:2 * i + t + 1], in1=h[:, t, hl],
                                                             op0=ALU.mult, op1=ALU.add)
                    ins.then_inc(h_half if c == 0 else h_ready, 1)

            def out_gain(i, first, e_n, name):
                g_ = row_of(name)
                for c in range(2):
                    hl = slice(c * HALF, (c + 1) * HALF)
                    used(dve, first + c)
                    for t in (1, 0):
                        if t == 0:
                            dve.wait_ge(part_sq, 8 * e_n + 2 * c + 1)
                        nc.vector.tensor_tensor(posted[:, t, hl], psum[:, 2 * c + t, :], g_[:, hl], ALU.mult).then_inc(part_gain, 1)
                dve.wait_ge(part_gain, 4 * e_n + 4)
                add_normed(i, 2 * e_n)

            def embed_dve(i, e_n, T, name):
                evacuate_low(dve, T, (XH, XL, None))
                dve.wait_ge(e_act, e_n + 1)
                g_ = row_of(name)
                for c in range(2):
                    dve.wait_ge(gate_act, 2 * e_n + c + 1)
                    hl = slice(c * HALF, (c + 1) * HALF)
                    nc.vector.tensor_tensor(ge[:, :, hl], ge[:, :, hl], eN[:, :, hl], ALU.mult).then_inc(ge_ready, 1)
                    dve.wait_ge(ge_ready, 2 * e_n + c + 1)
                    settle(nc.vector.tensor_tensor(posted[:, :, hl], ge[:, :, hl],
                                                   g_[:, hl].unsqueeze(1).broadcast_to([P, NT, HALF]), ALU.mult))
                add_normed(i, 2 * e_n + 1)

            evacuate_low(dve, T_YA, (XH, XL, None))
            out_gain(6, W_OUT_A, 0, "norm_post0")
            dve.wait_ge(h_ready, 6)
            embed_dve(7, 0, T_H6, "ple_norm0")
            dve.wait_ge(h_ready, 7)

            evacuate_low(dve, T_H7, (XBH, XBL, c8("kv_norm")), (XH, XL, c8("norm_pre1")))
            dve.wait_ge(lam_landed, 16)
            lv = lamb.rearrange("p (a b) d -> p a b d", b=2)
            settle(nc.vector.tensor_tensor(lamp, lv[:, :, 0, :], lv[:, :, 1, :], ALU.mult))
            nc.vector.tensor_reduce(lams, lamp, AX.X, ALU.add).then_inc(lam_sum, 1)
            rms(8)
            dve.wait_ge(lam_exp, 1)
            settle(nc.vector.tensor_tensor(nlam, lame[:, 1:2], lame[:, 0:1], ALU.subtract))
            settle(nc.vector.tensor_scalar(nlam, nlam, -LAM0, None, ALU.add))
            for c, dst in enumerate((kD, vD, qD)):
                for j in range(2):
                    used(dve, W_KV + 2 * c + j)
                    nc.vector.tensor_scalar(dst[:, 1, j * HALF:(j + 1) * HALF], psum[:, 2 * j + 1, :], rstd[:, 17:18], None,
                                            ALU.mult).then_inc(kv_dve, 1)
            for inst, dst in ((T_KB, kDT), (T_QB, qDT)):
                for b in ODD_EVEN(inst)[1]:
                    evacuate(dve, inst, b, dst)
            def heads_var(g):
                dve.wait_ge(o_sq, g + 1)
                u = slice(4 * g, 4 * g + 4)
                settle(nc.vector.tensor_reduce(vr_y[:, :, u], oD2[:, :, g * HALF:(g + 1) * HALF].rearrange(
                    "p t (h d) -> p t h d", d=P), AX.X, ALU.add))
                nc.vector.tensor_scalar(vr_y[:, :, u], vr_y[:, :, u], 1.0 / P, 1e-5, ALU.mult, ALU.add).then_inc(o_var, 1)

            def heads_norm(g):
                dve.wait_ge(o_root, g + 1)
                u, hl = slice(4 * g, 4 * g + 4), slice(g * HALF, (g + 1) * HALF)
                settle(nc.vector.reciprocal(rs_y[:, :, u], rt_y[:, :, u]))
                dst = oD[:, :, hl].rearrange("p t (h d) -> p h t d", d=P)
                src = psum[:, 2 * g:2 * g + 2, :].rearrange("p b (h t d) -> p (b h) t d", h=2, t=NT)
                per_head = rs_y[:, :, u].rearrange("p t h -> p h t").unsqueeze(3).broadcast_to([P, 4, NT, P])
                settle(nc.vector.tensor_tensor(dst, src, per_head, ALU.mult))
                dve.wait_ge(gate_gain, 1)
                nc.vector.scalar_tensor_tensor(out=oD[:, :, hl], in0=oD[:, :, hl], scalar=1.0 - LAM0, in1=gD[:, :, hl],
                                               op0=ALU.mult, op1=ALU.mult).then_inc(od_ready, 1)

            for hh in range(HEADS + 1):
                if hh == 15:
                    heads_var(0)
                if hh < HEADS:
                    dve.wait_ge(sc_done, HEADS + hh + 1)
                    if hh >= 4:
                        dve.wait_ge(pt_filled, HEADS + hh // 2 - 1)
                    buf = sd[:, hh % 4, :]
                    nc.vector.scalar_tensor_tensor(out=buf, in0=psum[:, 4 + hh % 2, 0:384], scalar=HD ** -0.5,
                                                   in1=C("causal"), op0=ALU.mult, op1=ALU.add).then_inc(sc_read, 1)
                    dve.wait_ge(sc_read, HEADS + hh + 1)
                    nc.vector.tensor_reduce(nmx[:, hh, 1:2], buf[:, 0:256], AX.X, ALU.max, negate=True)
                    nc.vector.tensor_reduce(nmx[:, hh, 0:1], buf[:, 256:384], AX.X, ALU.max, negate=True).then_inc(mx_ready, 1)
                if hh >= 2 and hh % 2 == 0:
                    g = hh // 2 - 1
                    dve.wait_ge(exp_done, HEADS + 2 * g + 2)
                    settle(nc.vector.reciprocal(rd[g % 2], sums[:, 2 * g:2 * g + 2, :]))
                    settle(nc.vector.tensor_scalar(rd[g % 2][:, 1, :], rd[g % 2][:, 1, :], nlam, None, ALU.mult))
                    b0, b1 = sd[:, (2 * g) % 4, :], sd[:, (2 * g + 1) % 4, :]
                    for t, cut in ((1, slice(0, 256)), (0, slice(256, 384))):
                        ins = nc.vector.tensor_scalar(b0[:, cut], b0[:, cut], rd[g % 2][:, 0, t:t + 1], None, ALU.mult)
                    settle(ins)
                    for t, cut in ((1, slice(0, 256)), (0, slice(256, 384))):
                        ins = nc.vector.scalar_tensor_tensor(out=b0[:, cut], in0=b1[:, cut], scalar=rd[g % 2][:, 1, t:t + 1],
                                                             in1=b0[:, cut], op0=ALU.mult, op1=ALU.add)
                    ins.then_inc(comb_ready, 1)
            heads_norm(0)
            heads_var(1)
            heads_norm(1)
            evacuate_low(dve, T_OB, (XH, XL, None))
            out_gain(9, W_OUT_B, 1, "norm_post1")
            dve.wait_ge(h_ready, 8)
            embed_dve(10, 1, T_H8, "ple_norm1")

        @block.tensor
        def _(pe):
            pe.wait_ge(par_landed, 32)
            pe.wait_ge(x_landed, 16)
            pe_transposes(pe, T_H0, h)

            def qkv_free(pe, c):
                if c >= 2:
                    pe.wait_ge(qkv_act, c - 1)
                    pe.wait_ge(qkv_dve, c - 1)
            pe_linear(pe, W_QKV, 6, xT2, qkv_free, transposed(pe, T_H0))
            pe.wait_ge(con_landed, 16)
            pe.wait_ge(qkv_act, 6)
            pe.wait_ge(qkv_dve, 6)
            pe_transposes(pe, T_Q, qn)
            pe_transposes(pe, T_K, kn)
            evacuated(pe, T_K)
            for hh in range(HEADS + 3):
                if hh < HEADS:
                    if hh >= 2:
                        pe.wait_ge(sc_read, hh - 1)
                    p0, f = HD * (hh % 2), hh // 2
                    q, k = qT[p0:p0 + HD, f, :], kT[p0:p0 + HD, f, :]
                    nc.tensor.matmul(psum[:, 4 + hh % 2, 0:256], q[:, P:2 * P], k, start=True, stop=True)
                    nc.tensor.matmul(psum[:, 4 + hh % 2, 256:384], q[:, 0:P], k[:, 0:P], start=True, stop=True).then_inc(sc_done, 1)
                if 2 <= hh < HEADS + 2:
                    g = hh - 2
                    pe.wait_ge(exp_done, g + 1)
                    if g >= 2:
                        pe.wait_ge(pt_copied, g - 1)
                    for j in range(3):
                        ins = nc.tensor.transpose(psum[:, 6 + g % 2, j * P:(j + 1) * P], sbuf_s[:, g % 3, j * P:(j + 1) * P], ident)
                    ins.then_inc(pt_filled, 1)
                if hh >= 3:
                    g = hh - 3
                    pe.wait_ge(pt_copied, g + 1)
                    pt = sbuf_pt[:, g % 2, :]
                    o = psum[:, g // 4, :].rearrange("p (h t d) -> p h t d", t=NT, d=HD)[:, g % 4]
                    v = vn[:, :, g * HD:(g + 1) * HD]
                    nc.tensor.matmul(o[:, 0], pt[:, 256:384], v[:, 0], start=True, stop=True)
                    nc.tensor.matmul(o[:, 1], pt[:, 0:128], v[:, 0], start=True, stop=False)
                    nc.tensor.matmul(o[:, 1], pt[:, 128:256], v[:, 1], start=False, stop=True).then_inc(pv_done, 1)
            pe.wait_ge(o_ready, 4)
            pe_transposes(pe, T_O, on)
            pe_linear(pe, W_O, 2, xT2, None, transposed(pe, T_O))
            pe_transposes(pe, T_H1, h, h_halves(pe, 1))
            mlp_pe(pe, 0, T_H1)

            pe.wait_ge(xn_ready, 1)
            pe_transposes(pe, T_N2, xn)
            pe.wait_ge(h_ready, 2)
            for i in range(4):
                for j in range(2):
                    pe_feature_tile(pe, 4 * W_INX + 2 * i + j, psum[:, i, j * SEQ:(j + 1) * SEQ],
                                    transposed(pe, T_N2) if i == 0 and j == 0 else None)
            for i in range(4):
                pe.wait_ge(xc_ready, i + 1)
                if i >= 2:
                    pe.wait_ge(gates_read, i - 1)
                piece_ready(pe, 4 * W_GATES + i)
                gw = raw(4 * W_GATES + i, 2, 4, P)
                for j in range(2):
                    f = 2 * i + j
                    nc.tensor.matmul(psum[:, 4 + i % 2, j * SEQ:(j + 1) * SEQ], gw[:, 0, j, :], xc[:, f, :], start=True, stop=True)
                    ins = nc.tensor.matmul(psum[:, 6 + i % 2, j * SEQ:(j + 1) * SEQ], gw[:, 0, 2 + j, :], xc[:, f, :], start=True, stop=True)
                ins.then_inc(piece_used, 1)
            for i in range(4):
                pe.wait_ge(x_read, i + 1)
                for j in range(2):
                    pe_feature_tile(pe, 4 * W_INY + 2 * i + j, psum[:, i, j * SEQ:(j + 1) * SEQ])
            pe_linear(pe, W_RO, 2, xTb2, lambda pe, c: pe.wait_ge(y_read, 2 * c + 2), lambda i: pe.wait_ge(og_low, i // 2 + 1))
            pe_transposes(pe, T_H3, h, h_halves(pe, 3))
            mlp_pe(pe, 1, T_H3)

            pe.wait_ge(xn_ready, 2)
            pe_transposes(pe, T_N5, xn5)

            def mixed(name):
                return lambda i: pe.wait_ge(mix_ready, 4 * MIXES.index(name) + i + 1)

            def rkv_free(pe, c):
                if c >= 2:
                    pe.wait_ge(proj_act, c - 1)

            def project(name, c):
                pe_chunk(pe, W_RKVG + c, c, mixture[name], rkv_free, mixed(name) if c % 2 == 0 else None)

            def decay_banks(i):
                for t in range(NT):
                    for half in range(2):
                        ins = nc.tensor.matmul(psum[:, 4 + 2 * t + half, :], lt[0:64, i, t * P:(t + 1) * P],
                                               lora2_sb[0:64, i, half * HALF:(half + 1) * HALF], start=True, stop=True)
                ins.then_inc(lora2_filled, 1)

            project("k", 0)
            pe.wait_ge(lor_landed, 32)
            evacuated(pe, T_N5)
            for i, name in enumerate(("w", "a")):
                mixed(name)(3)
                for k in range(KT):
                    ins = nc.tensor.matmul(psum[0:64, 4 + i, 0:SEQ], lora1_sb[:, i, k, :], mixture[name][:, k, :],
                                           start=(k == 0), stop=(k == KT - 1))
                ins.then_inc(lora_filled, 1)
            project("k", 1)
            pe.wait_ge(lora_out, 2)
            decay_banks(0)
            project("v", 2)
            pe.wait_ge(lora2_read, 1)
            decay_banks(1)
            project("v", 3)
            pe.wait_ge(sig_ready, 1)
            pe.wait_ge(lora2_read, 2)
            for t in range(NT):
                for half in range(2):
                    ins = nc.tensor.matmul(psum[:, 4 + 2 * t + half, :], C("tri_incl"), sg[:, t, half * HALF:(half + 1) * HALF],
                                           start=True, stop=True)
            ins.then_inc(cum_filled, 1)
            project("r", 4)
            pe.wait_ge(decays, 2)
            for f in range(KT):
                for t in range(NT):
                    ins = nc.tensor.matmul(psum[:, 4, 4 * f + 2 * t:4 * f + 2 * t + 2], Pd[:, t, f * P:(f + 1) * P], C("last"),
                                           start=True, stop=True)
            ins.then_inc(last_filled, 1)
            project("r", 5)
            pe.wait_ge(beta_kap, 2)
            pe_transposes(pe, T_BET, bet)
            pe.wait_ge(proj_dve, 2)
            pe.wait_ge(khat, 2)
            pe_transposes(pe, T_KAP, kap)
            pe_transposes(pe, T_RH, rN)
            pe_transposes(pe, T_KH, kN)
            evacuated(pe, T_KH)

            pe.wait_ge(proj_act, 4)
            pe.wait_ge(last_read, 1)
            STEPS = ["x0", "x1", "x2", "x3"] + list(range(1, 12))
            for pp in range(4):
                for s_ in STEPS:
                    for b in range(2):
                        f, B = 2 * pp + b, 4 * b
                        dve_did = lambda st, p_=pp: core_wait(pe, core_dve, DVE_AT, p_, b, st)
                        act_did = lambda st, p_=pp: core_wait(pe, core_act, ACT_AT, p_, b, st)
                        u, x_, o_, z_ = U[b], XX[b], OFF[b], U[b][:, :, 0, :]
                        bank = lambda k, q: psum[:, B + k, q * P:(q + 1) * P]
                        for q in range(4):
                            hh, t = q // 2, q % 2
                            p0 = HD * hh
                            head = slice((2 * f + hh) * HD, (2 * f + hh + 1) * HD)
                            tt = slice(t * P, (t + 1) * P)
                            if isinstance(s_, str):
                                if q != int(s_[1]):
                                    continue
                                if q == 0 and pp > 0:
                                    dve_did(11, pp - 1)
                                    act_did(11, pp - 1)
                                kr = KR[p0:p0 + HD, f, :, tt]
                                nc.tensor.matmul(psum[:, B + q, 0:256], bT[p0:p0 + HD, f, tt], kr, start=True, stop=True)
                                ins = nc.tensor.matmul(psum[:, B + q, 256:512], khT[p0:p0 + HD, f, tt], kr, start=True, stop=True)
                            elif s_ == 1:
                                if q == 0:
                                    dve_did("x1")
                                ins = nc.tensor.matmul(psum[:, B + hh, tt], KR[p0:p0 + HD, f, 0, tt], bT[p0:p0 + HD, f, tt], start=True, stop=True)
                            elif s_ == 2:
                                if q == 0:
                                    dve_did(1)
                                nc.tensor.matmul(bank(1, q), x_[:, q, :], u[:, q, 1, :], start=True, stop=True)
                                nc.tensor.matmul(bank(2, q), u[:, q, 1, :], x_[:, q, :], start=True, stop=True)
                                ins = nc.tensor.matmul(psum[:, B + 3, q * 64:(q + 1) * 64], u[:, q, 3, :], vN[:, t, head], start=True, stop=True)
                            elif s_ == 3:
                                if q == 0:
                                    dve_did(2)
                                    act_did(2)
                                    pe.wait_ge(core_pool[b], pp + 1)
                                nc.tensor.matmul(bank(0, q), x_[:, q, :], z_[:, q, :], start=True, stop=True)
                                nc.tensor.matmul(bank(1, q), x_[:, q, :], u[:, q, 1, :], start=True, stop=True)
                                ins = nc.tensor.matmul(bank(2, q), u[:, q, 1, :], x_[:, q, :], start=True, stop=True)
                            elif s_ == 4:
                                if q == 0:
                                    dve_did(3)
                                    act_did(3)
                                nc.tensor.matmul(bank(3, q), x_[:, q, :], z_[:, q, :], start=True, stop=True)
                                ins = nc.tensor.matmul(bank(2, q), u[:, q, 1, :], x_[:, q, :], start=True, stop=True)
                            elif s_ == 5:
                                if q == 0:
                                    dve_did(4)
                                    act_did(4)
                                ins = nc.tensor.matmul(bank(0, q), x_[:, q, :], z_[:, q, :], start=True, stop=True)
                            elif s_ in (6, 8):
                                if q == 0:
                                    dve_did(s_ - 1)
                                nc.tensor.transpose(bank(1, q), z_[:, q, :], ident)
                                ins = nc.tensor.matmul(bank(2, q), o_[:, (s_ - 6) // 2, q, :], z_[:, q, :], start=True, stop=True)
                            elif s_ in (7, 9):
                                if q == 0:
                                    dve_did(s_ - 1)
                                    act_did(s_ - 1)
                                ins = nc.tensor.matmul(bank(0, q), x_[:, q, :], u[:, q, 1, :], start=True, stop=True)
                            elif s_ == 10:
                                if q == 0:
                                    dve_did(9)
                                nc.tensor.matmul(bank(1, q)[:, 0:64], z_[:, q, :], kap[:, t, head], start=True, stop=True)
                                ins = nc.tensor.matmul(bank(1, q)[:, 64:128], z_[:, q, :], BV[b][:, q, :], start=True, stop=True)
                            else:
                                if q == 0:
                                    act_did(10)
                                wu = WU[b][:, q, :]
                                for c in range(2):
                                    g = 2 * t + c
                                    cc = slice(64 * c, 64 * c + 64)
                                    at = lambda n: psum[p0:p0 + HD, B + 2 + c, 64 * (n - 3 * c):64 * (n - 3 * c) + 64]
                                    if g in (1, 2):
                                        o = at(M_OF[g])
                                        nc.tensor.matmul(o, C("eye2")[cc, :], C("eye2")[cc, :], start=True, stop=False)
                                        nc.tensor.matmul(o, wu[cc, 0:64], bet[cc, t, head], start=False, stop=True)
                                    if g < 3:
                                        o = at(N_OF[g])
                                        nc.tensor.matmul(o, kN[cc, t, head], vN[cc, t, head], start=True, stop=False)
                                        nc.tensor.matmul(o, bet[cc, t, head], wu[cc, 64:128], start=False, stop=True)
                                nc.tensor.matmul(psum[p0:p0 + HD, B + 1, tt], wu[:, 0:64], u[:, q, 2, :],
                                                 start=True, stop=True)
                                o = psum[:, B, q * 64:(q + 1) * 64]
                                nc.tensor.matmul(o, u[:, q, 4, :], vN[:, t, head], start=True, stop=False)
                                ins = nc.tensor.matmul(o, u[:, q, 2, :], wu[:, 64:128], start=False, stop=True)
                        ins.then_inc(core_filled[b], 1)
            for b in range(2):
                core_wait(pe, core_dve, DVE_AT, 3, b, 11)
                core_wait(pe, core_act, ACT_AT, 3, b, 11)
            for g in (1, 2):
                pe.wait_ge(state_ready, g)
                for f in range(KT):
                    for p0 in (0, HD):
                        ins = nc.tensor.matmul(psum[p0:p0 + HD, 4 + 2 * (g - 1) + p0 // HD, f * 64:(f + 1) * 64], MN[p0:p0 + HD, f, M_OF[g], :],
                                               Sg[g][p0:p0 + HD, f, :], start=True, stop=True)
                ins.then_inc(state_filled, 1)
            pe.wait_ge(state_ready, 3)
            for g in (1, 2, 3):
                t, c = g // 2, g % 2
                for hh in range(HEADS):
                    f, p0 = hh // 2, HD * (hh % 2)
                    ins = nc.tensor.matmul(psum[64 * c:64 * c + 64, 4 + 2 * t + hh % 2, f * 64:(f + 1) * 64],
                                           KR[p0:p0 + HD, f, 1, t * P + 64 * c:t * P + 64 * c + 64], Sg[g][p0:p0 + HD, f, :],
                                           start=True, stop=True)
            ins.then_inc(ys_filled, 1)
            for j in range(2):
                pe_chunk(pe, W_RKVG + 6 + j, j, xTb2, None, (lambda i: pe.wait_ge(xg_low, i // 2 + 1)) if j == 0 else None)
            pe.wait_ge(y_ready, 1)

            def embed_pe(tile, e_n, T):
                pe.wait_ge(lor_landed, 48 + 16 * e_n)
                pe.wait_ge(part_sq, 8 * e_n + 4)
                pe.wait_ge(part_gain, 4 * e_n + 4)
                for c in range(2):
                    for k in range(2):
                        m = 4 * tile + 2 * c + k
                        piece_ready(pe, m)
                        for t in range(NT):
                            ins = nc.tensor.matmul(psum[:, 2 * c + t, :], pT_sb[:, k, t * P:(t + 1) * P],
                                                   raw(m)[:, c * HALF:(c + 1) * HALF], start=(k == 0), stop=(k == 1))
                        ins.then_inc(piece_used, 1)
                pe_transposes(pe, T, h, h_halves(pe, 6 + 2 * e_n))
                pe.wait_ge(e_act, e_n + 1)
                pe_linear(pe, tile + 1, 2, xT2, None, transposed(pe, T))

            pe_transposes(pe, T_YA, yN)
            pe_linear(pe, W_OUT_A, 2, xT2, None, transposed(pe, T_YA))
            embed_pe(W_PLE0, 0, T_H6)

            pe_transposes(pe, T_H7, h, h_halves(pe, 7))

            def kvqg_free(pe, c):
                if c >= 2:
                    pe.wait_ge(kv_act, c - 1)
                    pe.wait_ge(kv_dve, min(c - 1, 6))
            for c in range(8):
                pe_chunk(pe, W_KV + c, c, xTb2 if c < 4 else xT2, kvqg_free, transposed(pe, T_H7) if c == 0 else None)
            pe.wait_ge(roped, 1)
            pe_transposes(pe, T_KB, kD)
            pe.wait_ge(roped, 2)
            pe_transposes(pe, T_QB, qD)
            evacuated(pe, T_QB)
            pe.wait_ge(kv_act, 8)
            for hh in range(HEADS + 4):
                if hh < HEADS:
                    if hh >= 2:
                        pe.wait_ge(sc_read, HEADS + hh - 1)
                    p0, f = HD * (hh % 2), hh // 2
                    q, k = qDT[p0:p0 + HD, f, :], kDT[p0:p0 + HD, f, :]
                    nc.tensor.matmul(psum[:, 4 + hh % 2, 0:256], q[:, P:2 * P], k, start=True, stop=True)
                    nc.tensor.matmul(psum[:, 4 + hh % 2, 256:384], q[:, 0:P], k[:, 0:P], start=True, stop=True).then_inc(sc_done, 1)
                if hh >= 5 and hh % 2 == 1:
                    g = (hh - 5) // 2
                    pe.wait_ge(pt_copied, HEADS + g + 1)
                    pt = pt2[:, g % 2, :]
                    o = psum[:, g // 2, :].rearrange("p (h t d) -> p h t d", t=NT, d=P)[:, g % 2]
                    v = vD[:, :, g * P:(g + 1) * P]
                    nc.tensor.matmul(o[:, 0], pt[:, 256:384], v[:, 0], start=True, stop=True)
                    nc.tensor.matmul(o[:, 1], pt[:, 0:128], v[:, 0], start=True, stop=False)
                    nc.tensor.matmul(o[:, 1], pt[:, 128:256], v[:, 1], start=False, stop=True).then_inc(pv_done, 1)
                if 3 <= hh < HEADS + 3 and hh % 2 == 1:
                    g = (hh - 3) // 2
                    pe.wait_ge(comb_ready, g + 1)
                    if g >= 2:
                        pe.wait_ge(pt_copied, HEADS + g - 1)
                    for j in range(3):
                        ins = nc.tensor.transpose(psum[:, 6 + g % 2, j * P:(j + 1) * P], sd[:, (2 * g) % 4, j * P:(j + 1) * P], ident)
                    ins.then_inc(pt_filled, 1)
            pe_transposes(pe, T_OB, oD, lambda b: pe.wait_ge(od_ready, b // 2 + 1))
            pe_linear(pe, W_OUT_B, 2, xT2, None, transposed(pe, T_OB))
            embed_pe(W_PLE1, 1, T_H8)

def layout(inp):
    f = lambda n: np.ascontiguousarray(np.asarray(inp[n]))
    tiles = []

    def cols_tile(wm, c):
        tiles.append(wm[:, c * HALF:(c + 1) * HALF].reshape(KT, P, HALF).transpose(1, 0, 2).reshape(P, 4096))

    def rows_tile(wm, c):
        tiles.append(wm[c * HALF:(c + 1) * HALF].reshape(4, P, D).transpose(1, 0, 2).reshape(P, 4096))

    def feature_tiles(wm, c):
        tiles.append(wm[:, c * HALF:(c + 1) * HALF].reshape(KT, P, 4, P).transpose(1, 2, 0, 3).reshape(P, 4096))

    def mlp(m):
        w1, w2 = f("mlp_w1")[m], f("mlp_w2")[m]
        feature_tiles(w1, 0)
        for c in range(1, 8):
            feature_tiles(w1, c)
            rows_tile(w2, c - 1)
        rows_tile(w2, 7)

    def ple(i):
        half = f("ple_w_2")[i].reshape(2, P, D).transpose(1, 0, 2).reshape(P, 2048)
        tiles.append(np.concatenate([half, half], 1))
        for c in range(2):
            cols_tile(f("ple_gate_2")[i], c)

    qkv = f("attn_w_qkv")[0]
    for c in (0, 2, 4, 1, 3, 5):
        cols_tile(qkv, c)
    for c in range(2):
        cols_tile(f("attn_w_o")[0], c)
    mlp(0)
    for c in range(2):
        feature_tiles(f("rec_w_in")[0], c)
    gates = np.stack([f(n)[0].reshape(4, 2, P, P) for n in ("rec_w_ga", "rec_w_gx")], 1)
    tiles.append(np.stack([gates, gates], 1).transpose(4, 0, 1, 2, 3, 5).reshape(P, 4096))
    for c in (2, 3):
        feature_tiles(f("rec_w_in")[0], c)
    for c in range(2):
        cols_tile(f("rec_w_o")[0], c)
    mlp(1)
    for j in (1, 2, 0, 3):
        for c in range(2):
            cols_tile(f("a_w_in_2")[0, j], c)
    for c in range(2):
        cols_tile(f("a_w_out_2")[0], c)
    ple(0)
    for c in range(4):
        cols_tile(f("kv_w_2"), c)
    for c in range(4):
        cols_tile(f("b_w_in_2")[0], c)
    for c in range(2):
        cols_tile(f("b_w_out_2")[0], c)
    ple(1)
    assert len(tiles) == W_TILES
    w = np.stack(tiles).reshape(W_TILES, P, 4, PIECE).transpose(0, 2, 1, 3).reshape(4 * W_TILES, P, PIECE)

    col = lambda v: v.reshape(KT, P).T
    b_in, cw, mu = f("rec_b_in")[0], f("rec_conv_w")[0], f("a_mu_2")[0]
    vals = {"norm_mix0": f("norm_mix")[0], "norm_mix1": f("norm_mix")[1], "norm_mlp0": f("norm_mlp")[0],
            "norm_mlp1": f("norm_mlp")[1], "b_in_x": b_in[:D], "b_in_y": b_in[D:], "conv_b": f("rec_conv_b")[0],
            "b_ga": f("rec_b_ga")[0].reshape(-1), "b_gx": f("rec_b_gx")[0].reshape(-1), "a_param": f("rec_a_param")[0],
            "norm_pre0": f("norm_pre_2")[0], "norm_pre1": f("norm_pre_2")[1], "kv_norm": f("kv_norm_2")}
    vals |= {f"conv_w{i}": cw[i] for i in range(4)} | {f"mu{i}": mu[i] for i in range(6)}
    cols = np.stack([col(vals[n]) for n in COLS], 1)
    rv = {"b_o": f("rec_b_o")[0], "norm_final": f("norm_final"), "w0": f("a_w0_2")[0], "a0": f("a_a0_2")[0],
          "k_k": f("a_k_k_2")[0], "k_a": f("a_k_a_2")[0], "r_k": f("a_r_k_2")[0].reshape(-1),
          "lnx_g": f("a_lnx_g_2")[0], "lnx_b": f("a_lnx_b_2")[0], "norm_post0": f("norm_post_2")[0],
          "norm_post1": f("norm_post_2")[1], "ple_norm0": f("ple_norm_2")[0], "ple_norm1": f("ple_norm_2")[1],
          "subln": np.concatenate([f("b_subln_2")[0]] * 8)}
    rows = np.stack([rv[n] for n in ROWS])
    rel = f("attn_rel_bias")[0][:, ::-1]
    relt = np.concatenate([rel[:, :1]] * 127 + [rel], 1)
    lora1 = np.stack([f(n)[0].reshape(KT, P, 64).transpose(1, 0, 2) for n in ("a_w1_2", "a_a1_2")], 1)
    lora2 = np.stack([f(n)[0] for n in ("a_w2_2", "a_a2_2")], 1)
    pT = f("p_2")[:, 0].transpose(0, 2, 1).reshape(2, 2, P, SEQ).transpose(2, 0, 1, 3)
    lam = f("b_lambda_2")[0].reshape(1, 256)
    x = f("x")[0]
    return {"x": x, "w": w, "cols": cols, "rows": rows, "consts": shape_constants(), "relt": relt, "lora1": lora1,
            "lora2": lora2, "pT": pT, "lam": lam}


def kernel(**inputs):
    import concourse.bacc as bacc
    from concourse.bass_utils import run_bass_kernel_spmd

    nc = bacc.Bacc("TRN2", target_bir_lowering=False, num_devices=1)
    arrays = {k: np.ascontiguousarray(v) for k, v in layout(inputs).items()}
    aps = {k: nc.dram_tensor(k, v.shape, F32, kind="ExternalInput").ap() for k, v in arrays.items()}
    out = nc.dram_tensor("out", (SEQ, D), F32, kind="ExternalOutput").ap()
    build(nc, **aps, out=out)
    r = run_bass_kernel_spmd(nc, [arrays], core_ids=[0])
    return r.results[0]["out"].reshape(1, SEQ, D)
```
